# Optimizing a Trainium2 kernel written in Bass

```python
import math
import jax, jax.numpy as jnp
from jax import lax
import numpy as np

D_MODEL = 2048
BATCH = 1
SEQ = 256
DEPTH = 1

CTX_LEN = 256
GRID_W = 64

ATTN_HEADS = 8
ATTN_HEAD_DIM = 64
ATTN_VALUE_DIM = 2 * ATTN_HEAD_DIM
ATTN_WIDTH = ATTN_HEADS * ATTN_VALUE_DIM
QK_WIDTH = 2 * ATTN_HEADS * ATTN_HEAD_DIM
ROPE_THETA = 10000.0
Q_BLOCK = 128

POOL_WINDOWS = (2, 4, 8, 16)
POOL_GROUPS = len(POOL_WINDOWS)
POOL_WIDTH = D_MODEL // 2
POOL_GROUP_DIM = POOL_WIDTH // POOL_GROUPS

N_BRANCHES = 2
D_FF = 4 * D_MODEL
EPS = 1e-6

Q_OFF = 0
K_OFF = Q_OFF + QK_WIDTH
V_OFF = K_OFF + QK_WIDTH
P_OFF = V_OFF + ATTN_WIDTH
G_OFF = P_OFF + POOL_WIDTH
IN_WIDTH = G_OFF + N_BRANCHES * D_MODEL


def rmsnorm(x, w):
    xf = x.astype(jnp.float32)
    y = xf * lax.rsqrt(jnp.mean(xf * xf, axis=-1, keepdims=True) + EPS)
    return (y * w.astype(jnp.float32)).astype(x.dtype)

def modulate(x, w, shift, scale):
    return rmsnorm(x, w) * (1 + scale) + shift

def split_qk(t):
    B, L, _ = t.shape
    return t.reshape(B, L, 2 * ATTN_HEADS, ATTN_HEAD_DIM).transpose(0, 2, 1, 3)

def split_v(t):
    B, L, _ = t.shape
    return t.reshape(B, L, ATTN_HEADS, ATTN_VALUE_DIM).transpose(0, 2, 1, 3)

def axial_rope(x, row, col):
    half = x.shape[-1] // 2
    inv_freq = ROPE_THETA ** (-jnp.arange(0, half, 2, dtype=jnp.float32) / half)

    def rot(xa, pos):
        ang = pos.astype(jnp.float32)[:, None] * inv_freq[None, :]
        cos, sin = jnp.cos(ang), jnp.sin(ang)
        x1, x2 = xa[..., : half // 2], xa[..., half // 2:]
        return jnp.concatenate([x1 * cos - x2 * sin, x1 * sin + x2 * cos], axis=-1)

    xf = x.astype(jnp.float32)
    out = jnp.concatenate([rot(xf[..., :half], row), rot(xf[..., half:], col)], axis=-1)
    return out.astype(x.dtype)

def diff_attention(q, k, v, lam):
    B, _, Lq, dh = q.shape
    Lk = k.shape[2]
    nblk = Lq // Q_BLOCK
    qb = q.reshape(B, 2 * ATTN_HEADS, nblk, Q_BLOCK, dh).transpose(2, 0, 1, 3, 4)
    scale = dh ** -0.5

    def block(qi):
        s = jnp.einsum('bhqd,bhkd->bhqk', qi, k, preferred_element_type=jnp.float32) * scale
        p = jax.nn.softmax(s, axis=-1).reshape(B, ATTN_HEADS, 2, Q_BLOCK, Lk)
        a = (p[:, :, 0] - lam * p[:, :, 1]).astype(v.dtype)
        return jnp.einsum('bhqk,bhkd->bqhd', a, v)

    o = lax.map(block, qb)
    return o.transpose(1, 0, 2, 3, 4).reshape(B, Lq, ATTN_HEADS, ATTN_VALUE_DIM)

def multiscale_pool(u, pool_w, pool_scale):
    B, L, _ = u.shape
    uf = u.astype(jnp.float32)
    cs = jnp.pad(jnp.cumsum(uf, axis=1), ((0, 0), (1, 0), (0, 0)))
    t = jnp.arange(L)
    outs = []
    for g, w in enumerate(POOL_WINDOWS):
        sl = slice(g * POOL_GROUP_DIM, (g + 1) * POOL_GROUP_DIM)
        lo = jnp.clip(t - w // 2, 0, L)
        hi = jnp.clip(t + w - w // 2, 0, L)
        csg = cs[..., sl]
        mean = (csg[:, hi] - csg[:, lo]) / (hi - lo).astype(jnp.float32)[None, :, None]
        outs.append(mean - uf[..., sl])
    d = jnp.stack(outs, axis=2).astype(u.dtype)
    y = jnp.einsum('blgc,gcd->blgd', d, pool_w).reshape(B, L, POOL_WIDTH)
    return y * pool_scale

def token_mixer(q, k_all, v_all, pool_in, gate_logits, lam, lam_init, subln_w,
                pool_w, pool_scale, w_a_up, w_b_up, w_o):
    B, L = pool_in.shape[:2]
    heads = diff_attention(q, k_all, v_all, lam)
    heads = rmsnorm(heads, subln_w) * (1.0 - lam_init)
    y_a = heads.reshape(B, L, ATTN_WIDTH) @ w_a_up
    y_b = multiscale_pool(pool_in, pool_w, pool_scale) @ w_b_up
    g = jax.nn.sigmoid(gate_logits.astype(jnp.float32)).astype(y_a.dtype)
    g_a, g_b = g[..., :D_MODEL], g[..., D_MODEL:]
    return (g_a * y_a + g_b * y_b) @ w_o

def sq_relu_mlp(h, w1, w2):
    return jnp.square(jax.nn.relu(h @ w1)) @ w2

def first_inputs(seed: int = 0) -> dict:
    key = jax.random.key(seed)
    ks = jax.random.split(key, 24)
    f32 = jnp.float32

    def nrm(k, shape, scale):
        return jax.random.normal(k, shape, f32) * scale

    return {
        "x": nrm(ks[0], (BATCH, SEQ, D_MODEL), 1.0),
        "c": nrm(ks[1], (BATCH, D_MODEL), 1.0),
        "ctx": nrm(ks[2], (BATCH, CTX_LEN, D_MODEL), 1.0),
        "c_ctx": nrm(ks[3], (D_MODEL,), 1.0),
        "w_mod": nrm(ks[4], (DEPTH, D_MODEL, 6 * D_MODEL), D_MODEL ** -0.5),
        "b_mod": nrm(ks[5], (DEPTH, 6 * D_MODEL), 0.02),
        "norm_attn_w": 1.0 + nrm(ks[6], (DEPTH, D_MODEL), 0.1),
        "w_in": nrm(ks[7], (DEPTH, D_MODEL, IN_WIDTH), D_MODEL ** -0.5),
        "q_norm_w": 1.0 + nrm(ks[8], (DEPTH, ATTN_HEAD_DIM), 0.1),
        "k_norm_w": 1.0 + nrm(ks[9], (DEPTH, ATTN_HEAD_DIM), 0.1),
        "lambda_q1": nrm(ks[10], (DEPTH, ATTN_HEAD_DIM), 0.1),
        "lambda_k1": nrm(ks[11], (DEPTH, ATTN_HEAD_DIM), 0.1),
        "lambda_q2": nrm(ks[12], (DEPTH, ATTN_HEAD_DIM), 0.1),
        "lambda_k2": nrm(ks[13], (DEPTH, ATTN_HEAD_DIM), 0.1),
        "subln_w": 1.0 + nrm(ks[14], (DEPTH, ATTN_VALUE_DIM), 0.1),
        "pool_w": nrm(ks[15], (DEPTH, POOL_GROUPS, POOL_GROUP_DIM, POOL_GROUP_DIM), POOL_GROUP_DIM ** -0.5),
        "pool_scale": 1.0 + nrm(ks[16], (DEPTH, POOL_WIDTH), 0.1),
        "w_a_up": nrm(ks[17], (DEPTH, ATTN_WIDTH, D_MODEL), ATTN_WIDTH ** -0.5),
        "w_b_up": nrm(ks[18], (DEPTH, POOL_WIDTH, D_MODEL), POOL_WIDTH ** -0.5),
        "w_o": nrm(ks[19], (DEPTH, D_MODEL, D_MODEL), D_MODEL ** -0.5),
        "norm_mlp_w": 1.0 + nrm(ks[20], (DEPTH, D_MODEL), 0.1),
        "w_ff1": nrm(ks[21], (DEPTH, D_MODEL, D_FF), D_MODEL ** -0.5),
        "w_ff2": nrm(ks[22], (DEPTH, D_FF, D_MODEL), D_FF ** -0.5),
    }

def first_block(x, c, ctx, c_ctx, w_mod, b_mod, norm_attn_w, w_in, q_norm_w, k_norm_w,
              lambda_q1, lambda_k1, lambda_q2, lambda_k2, subln_w, pool_w, pool_scale,
              w_a_up, w_b_up, w_o, norm_mlp_w, w_ff1, w_ff2):
    L = x.shape[1]
    rows = L // GRID_W
    row = jnp.repeat(jnp.arange(rows), GRID_W)
    col = jnp.tile(jnp.arange(GRID_W), rows)

    x_ctx = ctx
    for l in range(DEPTH):
        last = l == DEPTH - 1
        lam_init = 0.8 - 0.6 * math.exp(-0.3 * l)
        lam = (jnp.exp(jnp.sum(lambda_q1[l].astype(jnp.float32) * lambda_k1[l].astype(jnp.float32)))
               - jnp.exp(jnp.sum(lambda_q2[l].astype(jnp.float32) * lambda_k2[l].astype(jnp.float32)))
               + lam_init)

        mod = (jax.nn.silu(c) @ w_mod[l] + b_mod[l])[:, None, :]
        sa, ca, ga, sm, cm, gm = jnp.split(mod, 6, axis=-1)
        mod_c = jax.nn.silu(c_ctx) @ w_mod[l] + b_mod[l]
        sa_c, ca_c, ga_c, sm_c, cm_c, gm_c = jnp.split(mod_c, 6, axis=-1)

        h_c = modulate(x_ctx, norm_attn_w[l], sa_c, ca_c)
        if last:
            p_c_kv = h_c @ w_in[l][:, K_OFF:P_OFF]
        else:
            p_c = h_c @ w_in[l]
            p_c_kv = p_c[..., K_OFF:P_OFF]
        k_c = rmsnorm(split_qk(p_c_kv[..., :QK_WIDTH]), k_norm_w[l])
        v_c = split_v(p_c_kv[..., QK_WIDTH:])

        h = modulate(x, norm_attn_w[l], sa, ca)
        p = h @ w_in[l]
        q = axial_rope(rmsnorm(split_qk(p[..., Q_OFF:K_OFF]), q_norm_w[l]), row, col)
        k = axial_rope(rmsnorm(split_qk(p[..., K_OFF:V_OFF]), k_norm_w[l]), row, col)
        v = split_v(p[..., V_OFF:P_OFF])
        k_all = jnp.concatenate([k, k_c], axis=2)
        v_all = jnp.concatenate([v, v_c], axis=2)
        mix = token_mixer(q, k_all, v_all, p[..., P_OFF:G_OFF], p[..., G_OFF:], lam, lam_init,
                          subln_w[l], pool_w[l], pool_scale[l], w_a_up[l], w_b_up[l], w_o[l])
        x = x + ga * mix
        x = x + gm * sq_relu_mlp(modulate(x, norm_mlp_w[l], sm, cm), w_ff1[l], w_ff2[l])

        if not last:
            q_c = rmsnorm(split_qk(p_c[..., Q_OFF:K_OFF]), q_norm_w[l])
            mix_c = token_mixer(q_c, k_c, v_c, p_c[..., P_OFF:G_OFF], p_c[..., G_OFF:], lam, lam_init,
                                subln_w[l], pool_w[l], pool_scale[l], w_a_up[l], w_b_up[l], w_o[l])
            x_ctx = x_ctx + ga_c * mix_c
            x_ctx = x_ctx + gm_c * sq_relu_mlp(modulate(x_ctx, norm_mlp_w[l], sm_c, cm_c),
                                               w_ff1[l], w_ff2[l])
    return x


DEPTH_2 = 2

N_MIXERS = 3
HEAD_DIM = 64
ROPE_DIM = HEAD_DIM // 4
ROPE_THETA_2 = 500000.0
NORM_EPS = 1e-5

A_HEADS = D_MODEL // HEAD_DIM
A_KV_HEADS = A_HEADS // 8
A_GROUP = A_HEADS // A_KV_HEADS
A_WIDTH = A_HEADS * HEAD_DIM
A_KV_WIDTH = A_KV_HEADS * HEAD_DIM
A_IN = 2 * A_WIDTH + 2 * A_KV_WIDTH
A_WINDOW = 128
A_QBLOCK = 128

B_HEADS = D_MODEL // HEAD_DIM
B_KV_GROUPS = 4
B_GROUP = B_HEADS // B_KV_GROUPS
B_WIDTH = B_HEADS * HEAD_DIM
B_KV_WIDTH = B_KV_GROUPS * HEAD_DIM
B_N_BRANCH = 3
B_IN = 2 * B_WIDTH + 6 * B_KV_WIDTH + B_N_BRANCH * B_HEADS
CMP_BLOCK = 32
CMP_STRIDE = 16
CMP_HIDDEN = 4 * HEAD_DIM
SLC_BLOCK = 64
SLC_TOPK = 16
B_WINDOW = 512
B_QBLOCK = 64
WIN_QBLOCK = 128

C_WIDTH = D_MODEL
C_IN = 4 * C_WIDTH
CONV_WIDTH = 3

N_A = (DEPTH_2 + 2) // N_MIXERS
N_B = (DEPTH_2 + 1) // N_MIXERS
N_C = DEPTH_2 // N_MIXERS


def rmsnorm_2(x, g):
    xf = x.astype(jnp.float32)
    y = xf * lax.rsqrt(jnp.mean(xf * xf, axis=-1, keepdims=True) + NORM_EPS)
    return (y * g.astype(jnp.float32)).astype(x.dtype)

def rope_tables(positions):
    inv_freq = ROPE_THETA_2 ** (-jnp.arange(0, ROPE_DIM, 2, dtype=jnp.float32) / ROPE_DIM)
    ang = positions.astype(jnp.float32)[..., None] * inv_freq
    return jnp.cos(ang)[:, :, None, :], jnp.sin(ang)[:, :, None, :]

def apply_rope(x, cos, sin):
    half = ROPE_DIM // 2
    x1 = x[..., :half].astype(jnp.float32)
    x2 = x[..., half:ROPE_DIM].astype(jnp.float32)
    r1 = x1 * cos - x2 * sin
    r2 = x2 * cos + x1 * sin
    return jnp.concatenate([r1.astype(x.dtype), r2.astype(x.dtype), x[..., ROPE_DIM:]], axis=-1)

def banded_attention(q, k, v, window, qblock, sinks=None):
    Bn, S, G, Hg, hd = q.shape
    nqb = S // qblock
    span = window + qblock
    scale = hd ** -0.5
    k_pad = jnp.pad(k, ((0, 0), (window, 0), (0, 0), (0, 0)))
    v_pad = jnp.pad(v, ((0, 0), (window, 0), (0, 0), (0, 0)))
    q_blocks = q.reshape(Bn, nqb, qblock, G, Hg, hd).swapaxes(0, 1)
    starts = jnp.arange(nqb, dtype=jnp.int32) * qblock
    rel = jnp.arange(qblock)[:, None] - jnp.arange(span)[None, :] + window
    band = (rel >= 0) & (rel < window)

    def step(args):
        qb, s0 = args
        kb = lax.dynamic_slice_in_dim(k_pad, s0, span, axis=1).astype(jnp.float32)
        vb = lax.dynamic_slice_in_dim(v_pad, s0, span, axis=1).astype(jnp.float32)
        s = jnp.einsum('bqghd,bkgd->bghqk', qb.astype(jnp.float32), kb) * scale
        valid = band & ((s0 - window + jnp.arange(span)) >= 0)[None, :]
        s = jnp.where(valid, s, -jnp.inf)
        if sinks is None:
            p = jax.nn.softmax(s, axis=-1)
        else:
            sk = sinks.astype(jnp.float32)[None, :, :, None, None]
            m = jnp.maximum(jnp.max(s, axis=-1, keepdims=True), sk)
            e = jnp.exp(s - m)
            p = e / (jnp.sum(e, axis=-1, keepdims=True) + jnp.exp(sk - m))
        o = jnp.einsum('bghqk,bkgd->bqghd', p, vb)
        return o.astype(q.dtype)

    o = lax.map(step, (q_blocks, starts))
    return o.swapaxes(0, 1).reshape(Bn, S, G, Hg, hd)

def mixer_a(h, w_in, sinks, w_out, cos, sin):
    Bn, S, _ = h.shape
    proj = h @ w_in
    q, k, v, z = jnp.split(proj, [A_WIDTH, A_WIDTH + A_KV_WIDTH, A_WIDTH + 2 * A_KV_WIDTH], axis=-1)
    q = apply_rope(q.reshape(Bn, S, A_HEADS, HEAD_DIM), cos, sin).reshape(Bn, S, A_KV_HEADS, A_GROUP, HEAD_DIM)
    k = apply_rope(k.reshape(Bn, S, A_KV_HEADS, HEAD_DIM), cos, sin)
    v = v.reshape(Bn, S, A_KV_HEADS, HEAD_DIM)
    o = banded_attention(q, k, v, A_WINDOW, A_QBLOCK, sinks.reshape(A_KV_HEADS, A_GROUP))
    o = o.reshape(Bn, S, A_WIDTH)
    return (o * jax.nn.silu(z)) @ w_out

def compress(k, pos, w1, w2):
    Bn, S, G, hd = k.shape
    nc = (S - CMP_BLOCK) // CMP_STRIDE + 1
    idx = np.arange(nc)[:, None] * CMP_STRIDE + np.arange(CMP_BLOCK)[None, :]
    blocks = k[:, idx] + pos[None, None, :, None, :]
    blocks = jnp.moveaxis(blocks, 3, 2).reshape(Bn, nc, G, CMP_BLOCK * hd)
    return jax.nn.gelu(blocks @ w1) @ w2

def nsa_cmp_slc(q, kcmp, vcmp, ks, vs):
    Bn, S, G, Hg, hd = q.shape
    nc = kcmp.shape[1]
    nsel = S // SLC_BLOCK
    n_top = min(SLC_TOPK, nsel)
    nqb = S // B_QBLOCK
    scale = hd ** -0.5
    c_start = np.arange(nc) * CMP_STRIDE
    c_end = c_start + CMP_BLOCK
    s_start = np.arange(nsel) * SLC_BLOCK
    s_end = s_start + SLC_BLOCK
    overlap = np.clip(np.minimum(c_end[:, None], s_end[None, :]) - np.maximum(c_start[:, None], s_start[None, :]), 0, None)
    overlap = jnp.asarray(overlap / CMP_BLOCK, jnp.float32)
    c_last = jnp.asarray(c_end - 1, jnp.int32)
    kcmp_f = kcmp.astype(jnp.float32)
    vcmp_f = vcmp.astype(jnp.float32)
    ks_blk = ks.reshape(Bn, nsel, SLC_BLOCK, G, hd).transpose(0, 1, 3, 2, 4)
    vs_blk = vs.reshape(Bn, nsel, SLC_BLOCK, G, hd).transpose(0, 1, 3, 2, 4)
    q_blocks = q.reshape(Bn, nqb, B_QBLOCK, G, Hg, hd).swapaxes(0, 1)
    starts = jnp.arange(nqb, dtype=jnp.int32) * B_QBLOCK
    bi = jnp.arange(Bn)[:, None, None, None]
    gi = jnp.arange(G)[None, None, :, None]
    blk = jnp.arange(nsel)

    def step(args):
        qb, s0 = args
        t = s0 + jnp.arange(B_QBLOCK)
        qf = qb.astype(jnp.float32)
        sc = jnp.einsum('bqghd,bcgd->bghqc', qf, kcmp_f) * scale
        sc = jnp.where(c_last[None, :] <= t[:, None], sc, -jnp.inf)
        m = jnp.max(sc, axis=-1, keepdims=True)
        m = jnp.where(jnp.isfinite(m), m, 0.0)
        e = jnp.exp(sc - m)
        p_cmp = e / jnp.maximum(jnp.sum(e, axis=-1, keepdims=True), 1e-30)
        o_cmp = jnp.einsum('bghqc,bcgd->bqghd', p_cmp, vcmp_f)
        imp = jnp.einsum('bghqc,cn->bgqn', p_cmp, overlap)
        cur = t // SLC_BLOCK
        forced = (blk[None, :] == 0) | (blk[None, :] == cur[:, None]) | (blk[None, :] == cur[:, None] - 1)
        future = blk[None, :] * SLC_BLOCK > t[:, None]
        imp = jnp.where(forced, jnp.inf, imp)
        imp = jnp.where(future, -jnp.inf, imp)
        _, sel = lax.top_k(imp, n_top)
        sel = sel.transpose(0, 2, 1, 3)
        kg = ks_blk[bi, sel, gi].astype(jnp.float32)
        vg = vs_blk[bi, sel, gi].astype(jnp.float32)
        ss = jnp.einsum('bqghd,bqgnld->bghqnl', qf, kg) * scale
        kpos = sel[..., None] * SLC_BLOCK + jnp.arange(SLC_BLOCK)
        valid = (kpos <= t[None, :, None, None, None]).transpose(0, 2, 1, 3, 4)[:, :, None]
        ss = jnp.where(valid, ss, -jnp.inf)
        shp = ss.shape
        p_slc = jax.nn.softmax(ss.reshape(shp[:4] + (n_top * SLC_BLOCK,)), axis=-1).reshape(shp)
        o_slc = jnp.einsum('bghqnl,bqgnld->bqghd', p_slc, vg)
        return o_cmp.astype(q.dtype), o_slc.astype(q.dtype)

    o_cmp, o_slc = lax.map(step, (q_blocks, starts))
    o_cmp = o_cmp.swapaxes(0, 1).reshape(Bn, S, G, Hg, hd)
    o_slc = o_slc.swapaxes(0, 1).reshape(Bn, S, G, Hg, hd)
    return o_cmp, o_slc

def mixer_b(h, w_in, kc_pos, kc_w1, kc_w2, vc_pos, vc_w1, vc_w2, w_out, cos, sin):
    Bn, S, _ = h.shape
    proj = h @ w_in
    cuts = [B_WIDTH + i * B_KV_WIDTH for i in range(7)] + [B_WIDTH + 6 * B_KV_WIDTH + B_N_BRANCH * B_HEADS]
    q, kc, vc, ks, vs, kw, vw, gates, z = jnp.split(proj, cuts, axis=-1)
    q = apply_rope(q.reshape(Bn, S, B_HEADS, HEAD_DIM), cos, sin).reshape(Bn, S, B_KV_GROUPS, B_GROUP, HEAD_DIM)
    kv_shape = (Bn, S, B_KV_GROUPS, HEAD_DIM)
    ks = apply_rope(ks.reshape(kv_shape), cos, sin)
    kw = apply_rope(kw.reshape(kv_shape), cos, sin)
    kcmp = compress(kc.reshape(kv_shape), kc_pos, kc_w1, kc_w2)
    vcmp = compress(vc.reshape(kv_shape), vc_pos, vc_w1, vc_w2)
    o_cmp, o_slc = nsa_cmp_slc(q, kcmp, vcmp, ks, vs.reshape(kv_shape))
    o_win = banded_attention(q, kw, vw.reshape(kv_shape), B_WINDOW, WIN_QBLOCK)
    g = jax.nn.sigmoid(gates.astype(jnp.float32)).reshape(Bn, S, B_N_BRANCH, B_KV_GROUPS, B_GROUP, 1)
    o = (g[:, :, 0] * o_cmp.astype(jnp.float32) + g[:, :, 1] * o_slc.astype(jnp.float32)
         + g[:, :, 2] * o_win.astype(jnp.float32)).astype(h.dtype)
    o = o.reshape(Bn, S, B_WIDTH)
    return (o * jax.nn.silu(z)) @ w_out

def mixer_c(h, w_in, conv_w, w_out):
    u, b_gate, c_gate, z = jnp.split(h @ w_in, 4, axis=-1)
    v = c_gate * u
    y = lax.conv_general_dilated(v, conv_w[:, None, :], window_strides=(1,), padding=[(CONV_WIDTH - 1, 0)],
                                 dimension_numbers=('NWC', 'WIO', 'NWC'), feature_group_count=C_WIDTH)
    y = b_gate * y
    return (y * jax.nn.silu(z)) @ w_out

def second_inputs(seed: int = 0) -> dict:
    key = jax.random.key(seed)
    ks = jax.random.split(key, 20)

    def dense(k, shape, fan_in):
        return jax.random.normal(k, shape, jnp.float32) * fan_in ** -0.5

    x = jax.random.normal(ks[0], (BATCH, SEQ, D_MODEL), jnp.float32)
    positions = (jnp.arange(SEQ, dtype=jnp.int32)[None, :]
                 + jax.random.randint(ks[1], (BATCH, 1), 0, 1024, dtype=jnp.int32))
    norm_w = 1.0 + 0.02 * jax.random.normal(ks[2], (DEPTH_2, D_MODEL), jnp.float32)
    final_norm_w = 1.0 + 0.02 * jax.random.normal(ks[3], (D_MODEL,), jnp.float32)
    a_w_in = dense(ks[4], (N_A, D_MODEL, A_IN), D_MODEL)
    a_sinks = jax.random.normal(ks[5], (N_A, A_HEADS), jnp.float32)
    a_w_out = dense(ks[6], (N_A, A_WIDTH, D_MODEL), A_WIDTH)
    b_w_in = dense(ks[7], (N_B, D_MODEL, B_IN), D_MODEL)
    b_cmp_k_pos = 0.1 * jax.random.normal(ks[8], (N_B, CMP_BLOCK, HEAD_DIM), jnp.float32)
    b_cmp_k_w1 = dense(ks[9], (N_B, CMP_BLOCK * HEAD_DIM, CMP_HIDDEN), CMP_BLOCK * HEAD_DIM)
    b_cmp_k_w2 = dense(ks[10], (N_B, CMP_HIDDEN, HEAD_DIM), CMP_HIDDEN)
    b_cmp_v_pos = 0.1 * jax.random.normal(ks[11], (N_B, CMP_BLOCK, HEAD_DIM), jnp.float32)
    b_cmp_v_w1 = dense(ks[12], (N_B, CMP_BLOCK * HEAD_DIM, CMP_HIDDEN), CMP_BLOCK * HEAD_DIM)
    b_cmp_v_w2 = dense(ks[13], (N_B, CMP_HIDDEN, HEAD_DIM), CMP_HIDDEN)
    b_w_out = dense(ks[14], (N_B, B_WIDTH, D_MODEL), B_WIDTH)
    c_w_in = dense(ks[15], (N_C, D_MODEL, C_IN), D_MODEL)
    c_conv_w = dense(ks[16], (N_C, CONV_WIDTH, C_WIDTH), CONV_WIDTH)
    c_w_out = dense(ks[17], (N_C, C_WIDTH, D_MODEL), C_WIDTH)
    return {"x": x, "positions": positions, "norm_w": norm_w, "final_norm_w": final_norm_w,
            "a_w_in": a_w_in, "a_sinks": a_sinks, "a_w_out": a_w_out,
            "b_w_in": b_w_in, "b_cmp_k_pos": b_cmp_k_pos, "b_cmp_k_w1": b_cmp_k_w1, "b_cmp_k_w2": b_cmp_k_w2,
            "b_cmp_v_pos": b_cmp_v_pos, "b_cmp_v_w1": b_cmp_v_w1, "b_cmp_v_w2": b_cmp_v_w2, "b_w_out": b_w_out,
            "c_w_in": c_w_in, "c_conv_w": c_conv_w, "c_w_out": c_w_out}

def second_block(x, positions, norm_w, final_norm_w, a_w_in, a_sinks, a_w_out,
              b_w_in, b_cmp_k_pos, b_cmp_k_w1, b_cmp_k_w2, b_cmp_v_pos, b_cmp_v_w1, b_cmp_v_w2, b_w_out,
              c_w_in, c_conv_w, c_w_out):
    cos, sin = rope_tables(positions)
    for i in range(DEPTH_2):
        h = rmsnorm_2(x, norm_w[i])
        kind, j = i % N_MIXERS, i // N_MIXERS
        if kind == 0:
            out = mixer_a(h, a_w_in[j], a_sinks[j], a_w_out[j], cos, sin)
        elif kind == 1:
            out = mixer_b(h, b_w_in[j], b_cmp_k_pos[j], b_cmp_k_w1[j], b_cmp_k_w2[j],
                          b_cmp_v_pos[j], b_cmp_v_w1[j], b_cmp_v_w2[j], b_w_out[j], cos, sin)
        else:
            out = mixer_c(h, c_w_in[j], c_conv_w[j], c_w_out[j])
        x = x + out.astype(x.dtype)
    return rmsnorm_2(x, final_norm_w)


def setup_inputs(seed=0):
    out = dict(first_inputs(seed))
    for name, value in second_inputs(seed + 1).items():
        if name != "x":
            out[name + "_2"] = value
    return out


def reference(
    x, c, ctx, c_ctx, w_mod, b_mod, norm_attn_w, w_in, q_norm_w, k_norm_w, lambda_q1, lambda_k1,
    lambda_q2, lambda_k2, subln_w, pool_w, pool_scale, w_a_up, w_b_up, w_o, norm_mlp_w, w_ff1,
    w_ff2, positions_2, norm_w_2, final_norm_w_2, a_w_in_2, a_sinks_2, a_w_out_2, b_w_in_2,
    b_cmp_k_pos_2, b_cmp_k_w1_2, b_cmp_k_w2_2, b_cmp_v_pos_2, b_cmp_v_w1_2, b_cmp_v_w2_2,
    b_w_out_2, c_w_in_2, c_conv_w_2, c_w_out_2,
):
    x = first_block(
        x, c, ctx, c_ctx, w_mod, b_mod, norm_attn_w, w_in, q_norm_w, k_norm_w, lambda_q1,
        lambda_k1, lambda_q2, lambda_k2, subln_w, pool_w, pool_scale, w_a_up, w_b_up, w_o,
        norm_mlp_w, w_ff1, w_ff2,
    )
    return second_block(
        x, positions_2, norm_w_2, final_norm_w_2, a_w_in_2, a_sinks_2, a_w_out_2, b_w_in_2,
        b_cmp_k_pos_2, b_cmp_k_w1_2, b_cmp_k_w2_2, b_cmp_v_pos_2, b_cmp_v_w1_2, b_cmp_v_w2_2,
        b_w_out_2, c_w_in_2, c_conv_w_2, c_w_out_2,
    )


_drawn_inputs = setup_inputs


def setup_inputs(seed=0):
    import zlib

    import numpy as np

    out = dict(_drawn_inputs(seed))
    spreads = {}
    factors = {'q_norm_w': 4.414,
     'k_norm_w': 3.638,
     'lambda_q1': 8.0,
     'lambda_q2': 3.935,
     'norm_w_2': 8.0,
     'final_norm_w_2': 2.784,
     'a_sinks_2': 8.0,
     'b_cmp_k_pos_2': 8.0,
     'b_cmp_k_w1_2': 3.632,
     'b_cmp_k_w2_2': 3.637,
     'b_cmp_v_pos_2': 6.603}
    for name, (base, spread) in spreads.items():
        noise = np.random.default_rng([zlib.crc32(name.encode()), seed]).standard_normal(out[name].shape)
        drawn = base * np.exp(spread * noise) if base else spread * noise
        out[name] = __import__('jax').numpy.asarray(drawn.astype(out[name].dtype))
    for name, factor in factors.items():
        out[name] = (out[name] * factor).astype(out[name].dtype)
    return out
```

```python
from contextlib import ExitStack

import concourse.bass as bass
import concourse.mybir as mybir
import numpy as np

F32, F32R, I32 = mybir.dt.float32, mybir.dt.float32r, mybir.dt.int32
ACT = mybir.ActivationFunctionType
ALU = mybir.AluOpType
AX = mybir.AxisListType

P = 128
D = 2048
KT = D // P
NW = 512
UK = 4
L = 256
T = L // P
HEADS1, VD = 8, 128
W1 = 1024
EPS1, EPS2 = 1e-6, 1e-5
LAM_INIT = 0.8 - 0.6
HD = 64
KVG = 4
HG = 8
NC = 15
NEG = -1.0e30
B_GATES = 96
ROT = 8

PHASES = [("mod1", 32, 8), ("ctx", 16, 4), ("in", 64, 16), ("up", 16, 8), ("mod2", 64, 16), ("wo", 16, 4),
          ("mlp", 128, 48), ("a_in", 36, 9), ("a_out", 16, 4), ("b_att", 32, 8), ("b_z", 16, 4),
          ("b_out", 16, 4)]
UNIT, GROUP = {}, {}
UNITS = _g = 0
for _name, _nu, _ng in PHASES:
    UNIT[_name], GROUP[_name] = UNITS, _g
    UNITS, _g = UNITS + _nu, _g + _ng

BUILDS = [("ctx", 8), ("x", 8), ("pool", 4), ("heads", 4), ("mix", 8), ("mlp", 8), ("hidden", 32),
          ("a", 8), ("a_o", 8), ("b", 8), ("b_o", 8)]
BUILD = {}
_b = 0
for _name, _nb in BUILDS:
    BUILD[_name] = _b
    _b += _nb

RMS = {"rows": 0, "att1": 4, "mlp": 28, "a": 29, "b": 30, "final": 31}
ROUND_A, ROUND_B = 0, 8
KEYS_A = (P, 2 * P)
KEYS_B = (NC, P, P, NC, 2 * P, 2 * P)
V_NORM1, V_NORM2, V_NORM_A, V_NORM_B, V_POOL, V_SUBLN, V_KPOS, V_VPOS, V_END = 0, 16, 32, 48, 64, 72, 73, 89, 105


def plus(base, step, i):
    return base if i is None else base + step * i


def dit_kernel(nc, a, out):
    ctx = ExitStack()
    sb = lambda n, s, d=F32: ctx.enter_context(nc.sbuf_tensor(n, s, d))
    sem = lambda n: ctx.enter_context(nc.semaphore(n))
    v3 = lambda ap, n: ap.rearrange("p (t n) -> p t n", n=n)

    raw = sb("raw", [P, 4, UK, NW])
    whi = sb("whi", [P, 2, UK, NW], F32R)
    wlo = sb("wlo", [P, 2, UK, NW], F32R)
    xhi = sb("xhi", [P, KT, L], F32R)
    xlo = sb("xlo", [P, KT, L], F32R)
    with nc.sbuf_tensor("hhi", [P, 8, L], F32R) as hhi, nc.sbuf_tensor("hlo", [P, 8, L], F32R) as hlo:
        pass
    qkv = sb("qkv", [P, 10240])
    arena = sb("arena", [P, 16384])
    res, rows, big = arena[:, 0:4096], arena[:, 4096:8192], arena[:, 8192:16384]
    res3, rows3 = v3(res, D), v3(rows, D)
    ident = sb("ident", [P, P])
    cols1 = sb("cols1", [P, P])
    cols2 = sb("cols2", [P, V_END])
    modcol = sb("modcol", [P, 64])
    scale_ctx, shift_ctx = sb("scale_ctx", [P, KT]), sb("shift_ctx", [P, KT])
    scale_x, shift_x = sb("scale_x", [P, KT]), sb("shift_x", [P, KT])
    sel = sb("sel", [4, P + 2])
    tab = sb("tab", [P, 768])
    sinks = sb("sinks", [P, 32])
    silu_c = sb("silu_c", [P, 2, KT])
    mean, rstd, neghalf = sb("mean", [P, 12]), sb("rstd", [P, 12]), sb("neghalf", [P, 12])
    lam = sb("lam", [P, 8])
    m8, s8 = sb("m8", [P, 2, 8]), sb("s8", [P, 2, 8])
    ropc, rops = sb("ropc", [P, T, ROT]), sb("rops", [P, T, ROT])
    gate_b = sb("gate_b", [P, T, B_GATES])
    cmpk = sb("cmpk", [HD, KVG * NC])
    pos2 = sb("pos2", [P, T], I32)

    modrow = v3(big[:, 0:1024], NW)
    mtmp = v3(big[:, 1024:2048], NW)
    vec1, vec2 = big[:, 2048:2176], big[:, 2176:2304]
    lamv = v3(big[:, 2304:2560], HD)
    qkw = v3(big[:, 2560:2688], HD)
    qkws = v3(big[:, 2688:2816], HD)
    rcos, rsin = v3(big[:, 2816:3200], HD), v3(big[:, 3200:3584], HD)
    posf, ang, angk, invf = (v3(big[:, 3584 + 16 * n:3600 + 16 * n], ROT) for n in range(4))
    junk = big[:, 4096:6144]
    qk6 = v3(qkv[:, 0:6144], W1)
    kv_out = qkv[:, 2048:10240].rearrange("p (w t n) -> p w t n", w=2, t=4)
    v1 = v3(qkv[:, 6144:10240], W1)
    gates = v3(big, 2 * D)
    u_rows = v3(res[:, 0:2048], W1)
    dT = v3(res[:, 2048:4096], L)
    band = rows[:, 0:2048].rearrange("p (s g n) -> p s g n", s=2, g=4)
    poolw = rows[:, 2048:4096].rearrange("p (g c n) -> p g c n", g=4, c=2)
    cosw, sinw = v3(tab[:, 0:384], HD), v3(tab[:, 384:768], HD)
    heads = v3(res[:, 0:2048], W1)
    prob = v3(res[:, 2048:3072], NW)
    probT = res[:, 3072:3584]
    slab, slab2, slab3 = v3(rows[:, 0:768], P), v3(rows[:, 768:1536], P), v3(rows[:, 1536:2304], P)
    slabT = rows[:, 2304:3072]
    orow, osq = rows[:, 3072:3200], rows[:, 3200:3328]
    upa, upb = v3(res[:, 0:1024], NW), v3(res[:, 1024:2048], NW)
    yacc = v3(big[:, 0:4096], D)
    ga_b, gm_b = big[:, 4096:6144], big[:, 6144:8192]
    hid = v3(rows[:, 0:2048], W1)
    q2, z2 = v3(big[:, 0:4096], D), v3(big[:, 4096:8192], D)
    kv_a = v3(qkv[:, 0:1024], NW)
    kv6 = v3(qkv[:, 0:3072], 1536)
    qs = v3(qkv[:, 3072:4096], NW)
    qT = qkv[0:HD, 4096:6144].rearrange("p (h t n) -> p h t n", h=HG, t=T)
    sm = v3(qkv[:, 6144:8192], L)
    pT = v3(qkv[:, 8192:9216], NW)
    kTs = qkv[0:HD, 9216:10240]
    kTw = z2[0:HD, 0, 0:1024]
    kdup = z2[:, 0, 1024:2048].rearrange("p (t g n) -> p t g n", t=T, g=KVG)
    kcT = z2[:, 1, 0:1024]
    cmpv = z2[0:NC, 1, 0:256]
    blkT = z2[:, 1, 1024:1984].rearrange("p (l g c) -> p l g c", l=16, g=KVG)
    w1c = v3(rows, 256)
    w2c = qkv[:, 8192:8448].rearrange("p (w k n) -> p w k n", w=2, k=2)
    hx, hy, hz = sm[0:60, 0, :], sm[0:60, 1, :], sm[0:60, 2, :]
    hT = v3(qkv[:, 6144 + 768:6144 + 888], 60)
    rope_t = [qkv[:, 6144 + 512 * n:6144 + 512 * (n + 1)] for n in range(4)]
    causal, windowed = tab[:, 0:384], tab[:, 384:640]
    cmp_mask, cmp_any = tab[:, 640:670], tab[:, 670:672]
    sk = silu_c[:, :, 0:8]
    sm2 = v3(qkv[:, 1024:3072], L)
    sm_a = [[x[:, h, :] for h in range(HG)] for x in (sm, sm2)]
    sm3 = v3(z2[:, 0, 1024:2048], L), v3(z2[:, 1, 1024:2048], L)
    sm_b = [sm_a[0], [sm3[h // 4][:, h % 4, :] for h in range(HG)]]
    otmp = z2[:, 1, 512:1024]
    fin_w = big[:, 0:2048]

    acc = ctx.enter_context(nc.psum_tensor("acc", [P, 4, NW], F32))
    turn = ctx.enter_context(nc.psum_tensor("turn", [P, 2, NW], F32))
    aux = ctx.enter_context(nc.psum_tensor("aux", [P, 2, NW], F32))
    aux_flat = aux[:, :, :].rearrange("p b n -> p (b n)")
    turn_flat = turn[:, :, :].rearrange("p b n -> p (b n)")

    raw_in = [sem(f"raw_in{i}") for i in range(4)]
    hi_ready, lo_ready = sem("hi_ready"), sem("lo_ready")
    units_used = sem("units_used")
    acc_freed = sem("acc_freed")
    turned = sem("turned")
    hi_rounded, xt_ready = sem("hi_rounded"), sem("xt_ready")
    act_chain, dve_chain = sem("act_chain"), sem("dve_chain")
    params_in, setup_turned, cols_ready = sem("params_in"), sem("setup_turned"), sem("cols_ready")
    silu_exp, modw_ready = sem("silu_exp"), sem("modw_ready")
    sumsq_ready, mean_ready, rstd_ready = sem("sumsq_ready"), sem("mean_ready"), sem("rstd_ready")
    normed = sem("normed")
    modcol_ready, modcol_taken = sem("modcol_ready"), sem("modcol_taken")
    bcast_ready, bcast_taken, bias_in = sem("bcast_ready"), sem("bcast_taken"), sem("bias_in")
    cond_ready, lam_done, sin_arg, sin_done = sem("cond_ready"), sem("lam_done"), sem("sin_arg"), sem("sin_done")
    pe_passed, dve_passed = sem("pe_passed"), sem("dve_passed")
    lam_sum, half_set = sem("lam_sum"), sem("half_set")
    pool_in, pooled, pooled_copied = sem("pool_in"), sem("pooled"), sem("pooled_copied")
    slab_ready, slab_turned, slabT_ready = sem("slab_ready"), sem("slab_turned"), sem("slabT_ready")
    scores1, max1, exp1, attn1 = sem("scores1"), sem("max1"), sem("exp1"), sem("attn1")
    attn_turned, attnT_ready, head_out, head_done = sem("attn_turned"), sem("attnT_ready"), sem("head_out"), sem("head_done")
    head_sq = sem("head_sq")
    mixed, x_in, squared, res_done, norm_done = sem("mixed"), sem("x_in"), sem("squared"), sem("res_done"), sem("norm_done")
    masks_in, roped, kT_turned, kT_ready = sem("masks_in"), sem("roped"), sem("kT_turned"), sem("kT_ready")
    qs_ready, q_turned, qT_ready = sem("qs_ready"), sem("q_turned"), sem("qT_ready")
    scores2, masked2, max2, exp2, sink_arg, sink_exp = (sem(n) for n in ("scores2", "masked2", "max2", "exp2", "sink_arg", "sink_exp"))
    probs_turned, out2, out2_taken = (sem(n) for n in ("probs_turned", "out2", "out2_taken"))
    probsT_ready = sem("probsT_act"), sem("probsT_dve")
    cmp_w_in, dup_ready, cmp_turned, cmp_copied, blk_ready, hid_ready = (sem(n) for n in (
        "cmp_w_in", "dup_ready", "cmp_turned", "cmp_copied", "blk_ready", "hid_ready"))
    gelu_x, gelu_arg, gelu_tanh, gelu_done, hT_turned, hT_ready, cmp_out, cmp_stored = (sem(n) for n in (
        "gelu_x", "gelu_arg", "gelu_tanh", "gelu_done", "hT_turned", "hT_ready", "cmp_out", "cmp_stored"))
    gates_done, gated, fin_in, out_sent = sem("gates_done"), sem("gated"), sem("fin_in"), sem("out_sent")

    def apart(eng, signal, value, passed):
        eng.wait_ge(signal, value)
        eng.sem_inc(passed, 1)

    def chained(eng, signal):
        count = [0, 0]

        def link(ins, i=None):
            count[0] += 1
            ins.then_inc(signal, 1)
            eng.wait_ge(signal, plus(count[0], count[1], i))

        def looped(per, turns):
            count[1] = per
            start = count[0]

            def end():
                assert count[0] - start == per, (count[0] - start, per)
                count[0], count[1] = start + per * turns, 0
            return end
        return link, looped

    block = ctx.enter_context(nc.Block())

    @block.sync
    def _(sp):
        def load(u, src, i=None, per=0):
            if not (u < 4 and i is None):
                sp.wait_ge(lo_ready, plus(u - 3, per, i))
            sp.dma_start(raw[:, u % 4], src.rearrange("(k p) n -> p k n", p=P)).then_inc(raw_in[u % 4], 16)

        def column_blocks(name, w, first, blocks, c0=0, k_units=4, skip=0):
            with sp.Fori(0, blocks) as j:
                for k in range(k_units):
                    load(UNIT[name] + first + k, w[k * 512:(k + 1) * 512, bass.ds(c0 + j * NW, NW)], j, k_units)

        for k in range(4):
            load(k, a["w_mod"][k * 512:(k + 1) * 512, 0:NW])
        with sp.Fori(1, 8) as j:
            for k in range(4):
                sp.wait_ge(lo_ready, 4 * j + (k - 3))
                sp.dma_start(raw[:, k], a["w_mod"][k * 512:(k + 1) * 512, bass.ds(j * NW, NW)]
                             .rearrange("(k p) n -> p k n", p=P)).then_inc(raw_in[k], 16)
        column_blocks("ctx", a["w_in"], 0, 4, c0=W1)
        column_blocks("in", a["w_in"], 0, 16)
        with sp.Fori(0, 4) as j:
            for n, w in enumerate((a["w_a_up"], a["w_b_up"])):
                for k in range(2):
                    load(UNIT["up"] + 2 * n + k, w[k * 512:(k + 1) * 512, bass.ds(j * NW, NW)], j, 4)
        column_blocks("mod2", a["w_mod"], 0, 16, c0=2 * D)
        column_blocks("wo", a["w_o"], 0, 4)
        with sp.Fori(0, 8) as e:
            for n in range(2):
                for k in range(4):
                    load(UNIT["mlp"] + 4 * n + k,
                         a["w_ff1"][k * 512:(k + 1) * 512, bass.ds(e * W1 + n * NW, NW)], e, 16)
            for n in range(4):
                for k in range(2):
                    load(UNIT["mlp"] + 8 + 2 * n + k,
                         a["w_ff2"][bass.ds(e * W1 + k * 512, 512), n * NW:(n + 1) * NW], e, 16)
        column_blocks("a_in", a["a_w_in"], 0, 9)
        column_blocks("a_out", a["a_w_out"], 0, 4)
        column_blocks("b_att", a["b_w_in"], 0, 8)
        column_blocks("b_z", a["b_w_in"], 0, 4, c0=D + 6 * KVG * HD + B_GATES)
        column_blocks("b_out", a["b_w_out"], 0, 4)
        sp.wait_ge(norm_done, 1)
        sp.dma_start(out.rearrange("(t p) n -> p t n", p=P), rows3).then_inc(out_sent, 16)
        sp.wait_ge(out_sent, 16)

    @block.gpsimd
    def _(pool):
        pool.memset(neghalf[:, :], -0.5).then_inc(half_set, 1)
        small = [
            (ident[:, :], a["c_ident"]), (sel[:, :], a["c_sel"]),
            (vec1[0:96, :], a["b_mod"].rearrange("(r n) -> r n", n=P)),
            (vec1[96:112, :], a["c"].rearrange("(r n) -> r n", n=P)),
            (vec1[112:128, :], a["c_ctx"].rearrange("(r n) -> r n", n=P)),
            (vec2[V_NORM1:V_NORM2, :], a["norm_attn_w"].rearrange("(r n) -> r n", n=P)),
            (vec2[V_NORM2:V_NORM_A, :], a["norm_mlp_w"].rearrange("(r n) -> r n", n=P)),
            (vec2[V_NORM_A:V_POOL, :], a["norm_w"].rearrange("l (r n) -> (l r) n", n=P)),
            (vec2[V_POOL:V_SUBLN, :], a["pool_scale"].rearrange("(r n) -> r n", n=P)),
            (vec2[V_SUBLN:V_KPOS, :], a["subln_w"].rearrange("(r n) -> r n", n=P)),
            (vec2[V_KPOS:V_VPOS, :], a["kpos"].rearrange("(l two) d -> l (two d)", two=2)),
            (vec2[V_VPOS:V_END, :], a["vpos"].rearrange("(l two) d -> l (two d)", two=2)),
            (rows3, a["ctx"].rearrange("(t p) n -> p t n", p=P)),
            (res3, a["x"].rearrange("(t p) n -> p t n", p=P)),
            (qkw[:, 0, :], a["q_norm_w"].partition_broadcast(P)), (qkw[:, 1, :], a["k_norm_w"].partition_broadcast(P)),
            (rcos, a["c_cos"]), (rsin, a["c_sin"]), (invf[:, 0, :], a["c_invf"]),
            (pos2[:, :], a["positions"].rearrange("(t p) -> p t", p=P)),
            (sinks[:, :], a["sinks"].partition_broadcast(P)),
        ] + [(lamv[:, n, :], a[f"lam{n}"].partition_broadcast(P)) for n in range(4)]
        assert len(small) == 25
        for dst, src in small:
            slow = {"allow_slow_non_contiguous": True} if dst.dtype == I32 else {}
            pool.dma_start(dst, src, **slow).then_inc(params_in, 16)
        pool.wait_ge(half_set, 1)

        def root(n, width, i=None, per=0):
            pool.wait_ge(mean_ready, plus(n + 1, per, i))
            pool.tensor_tensor(rstd[:, 0:width], mean[:, 0:width], neghalf[:, 0:width], ALU.pow).then_inc(rstd_ready, 1)

        with pool.Fori(0, 4) as i:
            root(RMS["rows"], 1, i, 1)
        pool.wait_ge(turned, BUILD["x"])
        pool.dma_start(band, a["c_band"]).then_inc(pool_in, 16)
        pool.dma_start(poolw, a["pool_w"].rearrange("g (c p) n -> p g c n", p=P)).then_inc(pool_in, 16)
        with pool.Fori(0, HEADS1) as h:
            root(RMS["att1"], 12, h, 3)
            for t in range(T):
                root(RMS["att1"] + 1 + t, 1, h, 3)
        pool.wait_ge(turned, BUILD["mix"])
        pool.dma_start(tab[:, 0:672], a["c_masks"]).then_inc(masks_in, 16)
        pool.wait_ge(acc_freed, GROUP["mod2"])
        pool.dma_start(ga_b, a["b_mod"][2 * D:3 * D].partition_broadcast(P)).then_inc(bias_in, 16)
        pool.dma_start(gm_b, a["b_mod"][5 * D:6 * D].partition_broadcast(P)).then_inc(bias_in, 16)
        pool.dma_start(res3, a["x"].rearrange("(t p) n -> p t n", p=P)).then_inc(x_in, 16)
        root(RMS["mlp"], 2)
        root(RMS["a"], 2)
        root(RMS["b"], 2)
        pool.wait_ge(turned, BUILD["b"] + 8)
        for n, (w1, w2) in enumerate((("kw1", "kw2"), ("vw1", "vw2"))):
            if n:
                pool.wait_ge(hid_ready, n)
            else:
                pool.wait_ge(out2, 2 + 4 * ROUND_B)
            pool.dma_start(w1c, a[w1].rearrange("(k p) n -> p k n", p=P)).then_inc(cmp_w_in, 16)
            pool.dma_start(w2c[:, n], a[w2].rearrange("(k p) n -> p k n", p=P)).then_inc(cmp_w_in, 16)
        pool.wait_ge(acc_freed, GROUP["b_z"] + 1)
        pool.dma_start(fin_w, a["final_norm_w"].partition_broadcast(P)).then_inc(fin_in, 16)
        root(RMS["final"], 2)

    @block.scalar
    def _(act):
        for signal in (head_sq, exp1):
            act.sem_inc(signal, 1)
        link, looped = chained(act, act_chain)

        def split(u, n, i=None, per=0):
            for k in range(u, u + n):
                if k < UNITS:
                    act.wait_ge(raw_in[k % 4], plus(16 * (k // 4 + 1), 4 * per, i))
                    if k >= 2:
                        act.wait_ge(units_used, plus(k - 1, per, i))
                    act.activation(whi[:, k % 2], raw[:, k % 4], ACT.Copy).then_inc(hi_ready, 1)

        def group_done(last, i=None, per=0):
            act.wait_ge(units_used, plus(last + 1, per, i))

        def banks(g):
            return acc[:, 2 * (g % 2):2 * (g % 2) + 2, :]

        def build(g, k, dst, scale=None, shift=None, i=None, per=0):
            bank = turn[:, g % 2, :]
            act.wait_ge(turned, plus(g + 1, per, i))
            out2 = dst[:, k:k + 2, :].rearrange("p k n -> p (k n)")
            if scale is None:
                act.activation(out2, bank, ACT.Copy).then_inc(hi_rounded, 1)
            elif shift is None:
                for n in range(2):
                    ins = act.activation(dst[:, k + n, :], bank[:, n * L:(n + 1) * L], ACT.Copy, scale=scale(k + n))
                ins.then_inc(hi_rounded, 1)
            else:
                if g % 8 >= 2:
                    act.wait_ge(xt_ready, g - 1)
                for n in range(2):
                    ins = act.activation(mtmp[:, g % 2, n * L:(n + 1) * L], bank[:, n * L:(n + 1) * L],
                                         ACT.Identity, scale=scale(k + n), bias=shift(k + n))
                link(ins)
                act.activation(out2, mtmp[:, g % 2, :], ACT.Copy).then_inc(hi_rounded, 1)

        act.wait_ge(setup_turned, 1)
        act.activation(cols1[:, :], aux[:, 0, 0:P], ACT.Copy)
        act.activation(cols2[:, :], aux[:, 0, P:P + V_END], ACT.Copy).then_inc(cols_ready, 1)
        act.wait_ge(cols_ready, 1)
        act.activation(silu_c[:, :, :].rearrange("p c k -> p (c k)"), cols1[:, 96:128], ACT.Silu).then_inc(silu_exp, 1)
        act.wait_ge(lam_sum, 1)
        act.activation(lam[:, 2:4], lam[:, 0:2], ACT.Exp).then_inc(lam_done, 1)
        act.wait_ge(sin_arg, 1)
        act.activation(rops[:, :, :], ang, ACT.Sin)
        act.activation(ropc[:, :, :], angk, ACT.Sin).then_inc(sin_done, 1)

        split(0, 2)
        u0 = UNIT["mod1"]
        with act.Fori(0, 4) as i:
            act.activation(junk, arena[:, bass.ds(i * D, D)], ACT.Square, accum_out=lam[:, 6:7]).then_inc(sumsq_ready, 1)
            for n in range(2):
                split(u0 + 4 * n + 2, 4, i, 8)
                if n == 0:
                    act.wait_ge(modcol_ready, 1 + i)
                group_done(u0 + 4 * n + 3, i, 8)
                act.activation(modrow[0:4, n, :], acc[0:4, 2 * n, :], ACT.Copy).then_inc(acc_freed, 1)
        act.wait_ge(cond_ready, 1)
        for g in range(8):
            build(BUILD["ctx"] + g, 2 * g, xhi, lambda k: scale_ctx[:, k:k + 1], lambda k: shift_ctx[:, k:k + 1])
        u0 = UNIT["ctx"]
        with act.Fori(0, 2) as i:
            for n in range(2):
                split(u0 + 4 * n + 2, 4, i, 8)
                group_done(u0 + 4 * n + 3, i, 8)
                act.activation(kv_out[:, i, 2:4, n * NW:(n + 1) * NW], banks(n), ACT.Copy).then_inc(acc_freed, 1)
        for g in range(8):
            build(BUILD["x"] + g, 2 * g, xhi, lambda k: scale_x[:, k:k + 1], lambda k: shift_x[:, k:k + 1])
        u0 = UNIT["in"]
        dst = [qk6[:, 0:2, :], qk6[:, 2:4, :], v1[:, 0:2, :], u_rows]
        for g in range(8):
            split(u0 + 4 * g + 2, 4)
            group_done(u0 + 4 * g + 3)
            if g == 6:
                act.wait_ge(turned, BUILD["pool"])
            act.activation(dst[g // 2][:, :, (g % 2) * NW:(g % 2 + 1) * NW], banks(g), ACT.Copy).then_inc(acc_freed, 1)
        with act.Fori(0, 4) as i:
            for n in range(2):
                split(u0 + 32 + 4 * n + 2, 4, i, 8)
                group_done(u0 + 32 + 4 * n + 3, i, 8)
                act.activation(gates[:, :, bass.ds(i * W1 + n * NW, NW)], banks(n), ACT.Sigmoid).then_inc(acc_freed, 1)
        for b in range(4):
            act.wait_ge(pooled, b + 1)
            act.activation(dT[:, 2 * b:2 * b + 2, :].rearrange("p k n -> p (k n)"), turn[:, b % 2, :], ACT.Copy)\
               .then_inc(pooled_copied, 1)
        for g in range(4):
            build(BUILD["pool"] + g, 8 + 2 * g, xhi, lambda k: cols2[:, V_POOL + k - 8:V_POOL + k - 7])
        with act.Fori(0, HEADS1) as h:
            act.wait_ge(slab_turned, 1 + (h + 1))
            act.activation(slabT, aux_flat[:, 0:768], ACT.Copy).then_inc(slabT_ready, 1)
            for t in range(T):
                act.wait_ge(max1, plus(t + 1, T, h))
                for c in range(2):
                    ins = act.activation(prob[:, c, :], turn[:, c, :], ACT.Exp, scale=HD ** -0.5,
                                         bias=lam[:, c:c + 1], accum_out=lam[:, 2 + c:3 + c])
                ins.then_inc(exp1, 1)
                act.wait_ge(attn_turned, plus(t + 1, T, h))
                act.activation(probT, aux[:, 0, :], ACT.Copy).then_inc(attnT_ready, 1)
                act.wait_ge(head_out, plus(t + 1, T, h))
                act.activation(orow, aux[:, 1, 0:VD], ACT.Copy).then_inc(head_sq, 1)
        for g in range(4):
            build(BUILD["heads"] + g, 2 * g, xhi, lambda k: cols2[:, V_SUBLN:V_SUBLN + 1])
        with act.Fori(0, 4) as i:
            split(UNIT["up"] + 2, 4, i, 4)
        u0 = UNIT["mod2"]
        with act.Fori(0, 8) as i:
            for n in range(2):
                split(u0 + 4 * n + 2, 4, i, 8)
                if n == 0:
                    act.wait_ge(modcol_taken, 1 + (plus(4, 1, i)))
                group_done(u0 + 4 * n + 3, i, 8)
                act.activation(modrow[0:4, n, :], acc[0:4, 2 * n, :], ACT.Copy).then_inc(acc_freed, 1)
        for g in range(8):
            build(BUILD["mix"] + g, 2 * g, xhi)
        with act.Fori(0, 4) as i:
            split(UNIT["wo"] + 2, 4, i, 4)
        for g in range(8):
            build(BUILD["mlp"] + g, 2 * g, xhi, lambda k: scale_x[:, k:k + 1], lambda k: shift_x[:, k:k + 1])
        u0 = UNIT["mlp"]
        with act.Fori(0, 8) as e:
            for n in range(2):
                split(u0 + 4 * n + 2, 4, e, 16)
                group_done(u0 + 4 * n + 3, e, 16)
                act.activation(hid[:, :, n * NW:(n + 1) * NW], banks(n), ACT.Relu).then_inc(acc_freed, 1)
            for g in range(4):
                build(BUILD["hidden"] + g, 2 * g, hhi, i=e, per=4)
            for n in range(4):
                split(u0 + 10 + 2 * n, 2, e, 16)
        for g in range(8):
            build(BUILD["a"] + g, 2 * g, xhi, lambda k: cols2[:, V_NORM_A + k:V_NORM_A + k + 1])
        u0 = UNIT["a_in"]
        with act.Fori(0, 2) as i:
            for n in range(2):
                split(u0 + 4 * n + 2, 4, i, 8)
                group_done(u0 + 4 * n + 3, i, 8)
                act.activation(q2[:, :, bass.ds(i * W1 + n * NW, NW)], banks(n), ACT.Copy, scale=HD ** -0.5)\
                   .then_inc(acc_freed, 1)
        split(u0 + 16 + 2, 4)
        group_done(u0 + 16 + 3)
        act.activation(kv_a, banks(0), ACT.Copy).then_inc(acc_freed, 1)
        with act.Fori(0, 2) as i:
            for n in range(2):
                split(u0 + 20 + 4 * n + 2, 4, i, 8)
                group_done(u0 + 20 + 4 * n + 3, i, 8)
                act.activation(z2[:, :, bass.ds(i * W1 + n * NW, NW)], banks(1 + n), ACT.Silu).then_inc(acc_freed, 1)

        def turn_keys(n, dst):
            act.wait_ge(kT_turned, n + 1)
            act.activation(dst, turn_flat[0:HD, :], ACT.Copy).then_inc(kT_ready, 1)

        def queries(n, g, per):
            act.wait_ge(q_turned, 1 + (plus(4 * n, 4, g)))
            act.activation(qs, q2[:, :, bass.ds(g * NW, NW)], ACT.Copy).then_inc(qs_ready, 1)
            for b in range(4):
                act.wait_ge(q_turned, 1 + (plus(4 * n + b + 1, 4, g)))
                act.activation(qT[:, 2 * b:2 * b + 2].rearrange("p h t n -> p (h t n)"), turn[0:HD, b % 2, :], ACT.Copy)\
                   .then_inc(qT_ready, 1)

        def exponentials(r, g, per, sm, keys, sink, pairs):
            act.wait_ge(max2, plus(r + 1, per, g))
            for p in pairs:
                for h in (2 * p, 2 * p + 1):
                    x = sm[r % 2][h][:, 0:keys]
                    ins = act.activation(x, x, ACT.Exp, bias=m8[:, r % 2, h:h + 1], accum_out=s8[:, r % 2, h:h + 1])
                ins.then_inc(exp2, 1)
            if sink and 3 in pairs:
                act.wait_ge(sink_arg, plus(r + 1, per, g))
                act.activation(sk[:, r % 2, :], sk[:, r % 2, :], ACT.Exp).then_inc(sink_exp, 1)

        def copy_probs(r, g, per, p, keys):
            act.wait_ge(probs_turned, plus(4 * r + p + 1, 4 * per, g))
            act.wait_ge(out2, 2 + (plus(4 * r + p - 1, 4 * per, g)))
            n, w = min(keys, P), 2 * -(-keys // P) * P
            act.activation(pT[0:n, p % 2, 0:w], turn[0:n, p % 2, 0:w], ACT.Copy).then_inc(probsT_ready[0], 1)

        def rounds(r0, keys, g, sm, sink=False):
            per = len(keys)
            exponentials(r0, g, per, sm, keys[0], sink, range(4))
            for j in range(per):
                for half in range(2):
                    copy_probs(r0 + j, g, per, 2 * half, keys[j])
                    if j + 1 < per:
                        exponentials(r0 + j + 1, g, per, sm, keys[j + 1], sink, range(2 * half, 2 * half + 2))

        turn_keys(0, kTs)
        with act.Fori(0, KVG) as g:
            queries(0, g, 1)
            rounds(ROUND_A, KEYS_A, g, sm_a, sink=True)
        for g in range(8):
            build(BUILD["a_o"] + g, 2 * g, xhi)
        with act.Fori(0, 4) as i:
            split(UNIT["a_out"] + 2, 4, i, 4)
        for g in range(8):
            build(BUILD["b"] + g, 2 * g, xhi, lambda k: cols2[:, V_NORM_B + k:V_NORM_B + k + 1])
        u0, g0 = UNIT["b_att"], GROUP["b_att"]
        with act.Fori(0, 2) as i:
            for n in range(2):
                split(u0 + 4 * n + 2, 4, i, 8)
                group_done(u0 + 4 * n + 3, i, 8)
                act.activation(q2[:, :, bass.ds(i * W1 + n * NW, NW)], banks(g0 + n), ACT.Copy, scale=HD ** -0.5)\
                   .then_inc(acc_freed, 1)
        for n in range(3):
            split(u0 + 16 + 4 * n + 2, 4)
            group_done(u0 + 16 + 4 * n + 3)
            act.activation(kv6[:, :, n * NW:(n + 1) * NW], banks(g0 + n), ACT.Copy).then_inc(acc_freed, 1)
        split(u0 + 28 + 2, 4)
        group_done(u0 + 28 + 3)
        act.activation(gate_b[:, :, :], banks(g0 + 3)[:, :, 0:B_GATES], ACT.Sigmoid).then_inc(acc_freed, 1)
        for n in range(2):
            act.wait_ge(cmp_turned, n + 1)
            act.activation(kcT, turn_flat, ACT.Copy).then_inc(cmp_copied, 1)
            act.wait_ge(hid_ready, n + 1)
            act.activation(hx, aux[0:60, 0, 0:256], ACT.Copy).then_inc(gelu_x, 1)
            act.wait_ge(gelu_arg, n + 1)
            act.activation(hy, hy, ACT.Tanh, scale=0.7978845608028654).then_inc(gelu_tanh, 1)
            act.wait_ge(hT_turned, n + 1)
            act.activation(hT, v3(aux[:, 1, 0:120], 60), ACT.Copy).then_inc(hT_ready, 1)
            act.wait_ge(cmp_out, n + 1)
            if n == 0:
                act.activation(cmpk[:, :], aux[0:HD, 0, 0:60], ACT.Copy).then_inc(cmp_stored, 1)
            else:
                act.activation(cmpv, aux[0:NC, 0, 0:256], ACT.Copy).then_inc(cmp_stored, 1)
        turn_keys(1, kTs)
        turn_keys(2, kTw)
        with act.Fori(0, KVG) as g:
            queries(4, g, 1)
            rounds(ROUND_B, KEYS_B, g, sm_b)
        u0, g0 = UNIT["b_z"], GROUP["b_z"]
        with act.Fori(0, 2) as i:
            for n in range(2):
                split(u0 + 4 * n + 2, 4, i, 8)
                group_done(u0 + 4 * n + 3, i, 8)
                act.activation(z2[:, :, bass.ds(i * W1 + n * NW, NW)], banks(g0 + n), ACT.Silu).then_inc(acc_freed, 1)
        for g in range(8):
            build(BUILD["b_o"] + g, 2 * g, xhi)
        with act.Fori(0, 3) as i:
            split(UNIT["b_out"] + 2, 4, i, 4)
        split(UNIT["b_out"] + 14, 2)

    @block.vector
    def _(dve):
        for signal, n in ((modcol_taken, 1), (masked2, 4), (out2_taken, 2)):
            dve.sem_inc(signal, n)
        link, looped = chained(dve, dve_chain)
        bc = lambda ap, shape: ap.to_broadcast(shape)

        def split(u, n, i=None, per=0):
            for k in range(u, u + n):
                if k < UNITS:
                    dve.wait_ge(hi_ready, plus(k + 1, per, i))
                    dve.tensor_tensor(wlo[:, k % 2], raw[:, k % 4], whi[:, k % 2].bitcast(F32), ALU.subtract)\
                       .then_inc(lo_ready, 1)

        def group_done(last, i=None, per=0):
            dve.wait_ge(units_used, plus(last + 1, per, i))

        def banks(g):
            return acc[:, 2 * (g % 2):2 * (g % 2) + 2, :]

        def build(g, k, hi, lo, scale=None, shift=False, i=None, per=0):
            dve.wait_ge(hi_rounded, plus(g + 1, per, i))
            bank = turn[:, g % 2, :]
            flat = lambda x: x[:, k:k + 2, :].rearrange("p k n -> p (k n)")
            if shift:
                dve.tensor_tensor(flat(lo), mtmp[:, g % 2, :], flat(hi).bitcast(F32), ALU.subtract).then_inc(xt_ready, 1)
            elif scale is None:
                dve.tensor_tensor(flat(lo), bank, flat(hi).bitcast(F32), ALU.subtract).then_inc(xt_ready, 1)
            else:
                for n in range(2):
                    ins = dve.scalar_tensor_tensor(lo[:, k + n, :], bank[:, n * L:(n + 1) * L], scale(k + n),
                                                   hi[:, k + n, :].bitcast(F32), ALU.mult, ALU.subtract)
                ins.then_inc(xt_ready, 1)

        def left_operand_of_conditions():
            link(dve.memset(xhi[:, :, 0:P].bitcast(F32), 0.0))
            sc = silu_c[:, :, :].rearrange("p c k -> p k c")
            link(dve.tensor_copy(xhi[:, :, 0:2], sc))
            dve.tensor_tensor(xhi[:, :, 2:4], sc, xhi[:, :, 0:2].bitcast(F32), ALU.subtract).then_inc(modw_ready, 1)

        def rms_rows(n, eps, dst, src, width):
            for t in range(T):
                ins = dve.tensor_tensor_reduce(out=dst[:, t], in0=src[:, t], in1=src[:, t], scale=1.0, scalar=0.0,
                                               op0=ALU.mult, op1=ALU.add, accum_out=mean[:, t:t + 1])
            link(ins)
            dve.tensor_scalar(mean[:, 0:T], mean[:, 0:T], 1.0 / width, eps, ALU.mult, ALU.add).then_inc(mean_ready, 1)
            dve.wait_ge(rstd_ready, n + 1)
            for t in range(T):
                ins = dve.tensor_scalar(dst[:, t], src[:, t], rstd[:, t:t + 1], None, ALU.mult)
            return ins

        dve.wait_ge(silu_exp, 1)
        left_operand_of_conditions()
        dve.wait_ge(params_in, 16 * 25)
        for n in range(2):
            ins = dve.tensor_tensor_reduce(out=junk[:, 0:HD], in0=lamv[:, 2 * n, :], in1=lamv[:, 2 * n + 1, :], scale=1.0,
                                           scalar=0.0, op0=ALU.mult, op1=ALU.add, accum_out=lam[:, n:n + 1])
            link(ins) if n == 0 else ins.then_inc(lam_sum, 1)
        dve.wait_ge(lam_done, 1)
        link(dve.tensor_tensor(lam[:, 4:5], lam[:, 2:3], lam[:, 3:4], ALU.subtract))
        link(dve.tensor_scalar(lam[:, 5:6], lam[:, 4:5], LAM_INIT, None, ALU.add))
        for n in range(2):
            w = qkw[:, n, :].rearrange("p (f two d) -> p f two d", f=2, two=2)
            ws = qkws[:, n, :].rearrange("p (f two d) -> p f two d", f=2, two=2)
            dve.tensor_copy(ws[:, :, 0, :], w[:, :, 1, :])
            link(dve.tensor_copy(ws[:, :, 1, :], w[:, :, 0, :]))
        for n, s0, s1 in ((0, 0, 2), (1, 2, 6)):
            dve.tensor_tensor(cosw[:, s0:s1, :], rcos[:, s0:s1, :], bc(qkw[:, n:n + 1, :], [P, s1 - s0, HD]), ALU.mult)
            dve.tensor_tensor(sinw[:, s0:s1, :], rsin[:, s0:s1, :], bc(qkws[:, n:n + 1, :], [P, s1 - s0, HD]), ALU.mult)
        link(dve.tensor_copy(posf[:, 0, 0:T], pos2[:, :]))
        for t in range(T):
            ins = dve.tensor_scalar(ang[:, t, :], invf[:, 0, :], posf[:, 0, t:t + 1], None, ALU.mult)
        link(ins)
        link(dve.tensor_scalar(angk, ang, 1.0 / (2 * np.pi), None, ALU.mult))
        link(dve.tensor_scalar(angk, angk, 12582912.0, None, ALU.add))
        link(dve.tensor_scalar(angk, angk, -12582912.0, None, ALU.add))
        for part in (6.28125, 0.0019350051879882812, 3.0199159819567e-07):
            link(dve.scalar_tensor_tensor(ang, angk, -part, ang, ALU.mult, ALU.add))
        link(dve.tensor_scalar(ang, ang, 3.1415925, -3.1415925, ALU.min, ALU.max))
        link(dve.tensor_scalar(angk, ang, -1.0, None, ALU.mult))
        link(dve.tensor_tensor(angk, ang, angk, ALU.max))
        dve.tensor_scalar(angk, angk, -1.0, float(np.float32(np.pi / 2)), ALU.mult, ALU.add).then_inc(sin_arg, 1)

        dve.wait_ge(sin_done, 1)
        split(0, 2)
        u0 = UNIT["mod1"]
        with dve.Fori(0, 4) as i:
            end = looped(0, 4)
            split(u0 + 2, 4, i, 8)
            dve.wait_ge(sumsq_ready, i + 1)
            dve.tensor_scalar(mean[:, 0:1], lam[:, 6:7], 1.0 / D, EPS1, ALU.mult, ALU.add).then_inc(mean_ready, 1)
            split(u0 + 6, 2, i, 8)
            dve.wait_ge(rstd_ready, i + 1)
            part = arena[:, bass.ds(i * D, D)]
            dve.tensor_scalar(part, part, rstd[:, 0:1], None, ALU.mult).then_inc(normed, 1)
            split(u0 + 8, 2, i, 8)
            dve.wait_ge(modcol_ready, 1 + (i + 1))
            dve.tensor_copy(modcol[:, bass.ds(i * 16, 16)], aux[:, 1, 0:16]).then_inc(modcol_taken, 1)
            end()
        mc = modcol[:, :].rearrange("p (s c) -> p c s", c=2)
        dve.wait_ge(modcol_taken, 1 + 4)
        for c, (sc, sh) in enumerate(((scale_x, shift_x), (scale_ctx, shift_ctx))):
            link(dve.tensor_tensor(sc[:, :], mc[:, c, 16:32], cols1[:, 16:32], ALU.add))
            ins = dve.scalar_tensor_tensor(sc[:, :], sc[:, :], 1.0, cols2[:, V_NORM1:V_NORM1 + KT], ALU.add, ALU.mult)
            link(ins)
            ins = dve.tensor_tensor(sh[:, :], mc[:, c, 0:16], cols1[:, 0:16], ALU.add)
        ins.then_inc(cond_ready, 1)
        for g in range(8):
            build(BUILD["ctx"] + g, 2 * g, xhi, xlo, shift=True)
        with dve.Fori(0, 4) as i:
            split(UNIT["ctx"] + 2, 4, i, 4)
        for g in range(8):
            build(BUILD["x"] + g, 2 * g, xhi, xlo, shift=True)
        with dve.Fori(0, 16) as i:
            split(UNIT["in"] + 2, 4, i, 4)
        for g in range(4):
            build(BUILD["pool"] + g, 8 + 2 * g, xhi, xlo, lambda k: cols2[:, V_POOL + k - 8:V_POOL + k - 7])

        dve.wait_ge(pooled, 4)
        with dve.Fori(0, HEADS1) as h:
            end = looped(13, HEADS1)
            src = qk6[:, :, bass.ds(h * P, P)]
            link(dve.tensor_tensor(slab2, src, src, ALU.mult), h)
            link(dve.tensor_reduce(mean[:, 0:12], slab2.rearrange("p s (c d) -> p (s c) d", c=2), AX.X, ALU.add), h)
            dve.tensor_scalar(mean[:, 0:12], mean[:, 0:12], 1.0 / HD, EPS1, ALU.mult, ALU.add).then_inc(mean_ready, 1)
            dve.wait_ge(rstd_ready, plus(RMS["att1"] + 1, 3, h))
            link(dve.tensor_tensor(slab3.rearrange("p s (c d) -> p s c d", c=2), src.rearrange("p s (c d) -> p s c d", c=2),
                                   bc(rstd[:, 0:12].rearrange("p (s c) -> p s c", c=2).unsqueeze(3), [P, 6, 2, HD]), ALU.mult), h)
            dve.wait_ge(slab_turned, 1 + h)
            dve.tensor_tensor(slab.rearrange("p s (c d) -> p s c d", c=2), slab3.rearrange("p s (c d) -> p s c d", c=2),
                              bc(cosw.unsqueeze(2), [P, 6, 2, HD]), ALU.mult)
            halves = lambda x: x.rearrange("p s (c f two d) -> p s c f two d", c=2, f=2, two=2)
            sw = sinw.rearrange("p s (f two d) -> p s f two d", f=2, two=2)
            for c in range(2):
                for two in range(2):
                    ins = dve.tensor_tensor(halves(slab2)[:, :, c, :, two, :], halves(slab3)[:, :, c, :, 1 - two, :],
                                            sw[:, :, :, two, :], ALU.mult)
            link(ins, h)
            dve.tensor_tensor(slab, slab, slab2, ALU.add).then_inc(slab_ready, 1)
            for t in range(T):
                dve.wait_ge(scores1, plus(t + 1, T, h))
                link(dve.tensor_reduce(lam[:, 0:2], turn[:, :, :], AX.X, ALU.max), h)
                dve.tensor_scalar(lam[:, 0:2], lam[:, 0:2], -(HD ** -0.5), None, ALU.mult).then_inc(max1, 1)
                dve.wait_ge(exp1, 1 + (plus(t + 1, T, h)))
                link(dve.reciprocal(s8[:, 0, 0:2], lam[:, 2:4]), h)
                link(dve.tensor_scalar(prob[:, 1, :], prob[:, 1, :], s8[:, 0, 1:2], lam[:, 5:6], ALU.mult, ALU.mult), h)
                dve.scalar_tensor_tensor(prob[:, 0, :], prob[:, 0, :], s8[:, 0, 0:1], prob[:, 1, :], ALU.mult, ALU.subtract)\
                   .then_inc(attn1, 1)
                dve.wait_ge(head_sq, 1 + (plus(t + 1, T, h)))
                link(dve.tensor_tensor_reduce(out=osq, in0=orow, in1=orow, scale=1.0, scalar=0.0, op0=ALU.mult,
                                              op1=ALU.add, accum_out=mean[:, 0:1]), h)
                dve.tensor_scalar(mean[:, 0:1], mean[:, 0:1], 1.0 / VD, EPS1, ALU.mult, ALU.add).then_inc(mean_ready, 1)
                dve.wait_ge(rstd_ready, plus(RMS["att1"] + 2 + t, 3, h))
                ins = dve.tensor_scalar(heads[:, t, bass.ds(h * VD, VD)], orow, rstd[:, 0:1], 1.0 - LAM_INIT,
                                        ALU.mult, ALU.mult)
                if t == 0:
                    link(ins, h)
                else:
                    ins.then_inc(head_done, 1)
            end()
        for g in range(4):
            build(BUILD["heads"] + g, 2 * g, xhi, xlo, lambda k: cols2[:, V_SUBLN:V_SUBLN + 1])

        u0 = UNIT["up"]
        with dve.Fori(0, 4) as i:
            end = looped(1, 4)
            split(u0 + 2, 4, i, 4)
            group_done(u0 + 3, i, 4)
            dve.tensor_tensor(upa, banks(0), gates[:, :, bass.ds(i * NW, NW)], ALU.mult).then_inc(acc_freed, 1)
            link(dve.tensor_tensor(upb, banks(1), gates[:, :, bass.ds(D + i * NW, NW)], ALU.mult), i)
            dve.tensor_tensor(rows3[:, :, bass.ds(i * NW, NW)], upa, upb, ALU.add).then_inc(acc_freed, 1)
            end()
        left_operand_of_conditions()
        dve.wait_ge(bias_in, 32)
        u0 = UNIT["mod2"]

        def broadcast(dst, first, n0):
            with dve.Fori(0, 2) as i:
                for n in range(2):
                    split(u0 + first + 4 * n + 2, 4, i, 8)
                dve.wait_ge(modcol_ready, 1 + (plus(n0 + 1, 1, i)))
                part = dst[:, bass.ds(i * W1, W1)]
                dve.tensor_tensor(part, aux_flat, part, ALU.add).then_inc(modcol_taken, 1)
        broadcast(ga_b, 0, 4)
        with dve.Fori(0, 4) as i:
            for n in range(2):
                split(u0 + 16 + 4 * n + 2, 4, i, 8)
            dve.wait_ge(modcol_ready, 1 + (plus(7, 1, i)))
            dve.tensor_copy(modcol[:, bass.ds(i * 16, 16)], aux[:, 1, 0:16]).then_inc(modcol_taken, 1)
        broadcast(gm_b, 48, 10)
        link(dve.tensor_tensor(scale_x[:, :], mc[:, 0, 16:32], cols1[:, 64:80], ALU.add))
        link(dve.scalar_tensor_tensor(scale_x[:, :], scale_x[:, :], 1.0, cols2[:, V_NORM2:V_NORM2 + KT], ALU.add, ALU.mult))
        dve.tensor_tensor(shift_x[:, :], mc[:, 0, 0:16], cols1[:, 48:64], ALU.add).then_inc(cond_ready, 1)
        for g in range(8):
            build(BUILD["mix"] + g, 2 * g, xhi, xlo)
        dve.wait_ge(x_in, 16)
        u0, g0 = UNIT["wo"], GROUP["wo"]
        with dve.Fori(0, 2) as i:
            end = looped(2, 2)
            for n in range(2):
                split(u0 + 4 * n + 2, 4, i, 8)
                group_done(u0 + 4 * n + 3, i, 8)
                cols = bass.ds(i * W1 + n * NW, NW)
                link(dve.tensor_tensor(mtmp, banks(n), bc(ga_b[:, cols].unsqueeze(1), [P, T, NW]), ALU.mult), i)
                dve.tensor_tensor(res3[:, :, cols], res3[:, :, cols], mtmp, ALU.add).then_inc(acc_freed, 1)
            end()
        dve.wait_ge(acc_freed, GROUP["mlp"])
        rms_rows(RMS["mlp"], EPS1, rows3, res3, D).then_inc(normed, 1)
        for g in range(8):
            build(BUILD["mlp"] + g, 2 * g, xhi, xlo, shift=True)
        dve.wait_ge(xt_ready, BUILD["hidden"])
        link(dve.memset(yacc, 0.0))
        u0, g0 = UNIT["mlp"], GROUP["mlp"]
        with dve.Fori(0, 8) as e:
            for n in range(2):
                split(u0 + 4 * n + 2, 4, e, 16)
                dve.wait_ge(acc_freed, plus(g0 + n + 1, 6, e))
                part = hid[:, :, n * NW:(n + 1) * NW]
                dve.tensor_tensor(part, part, part, ALU.mult).then_inc(squared, 1)
            for g in range(4):
                build(BUILD["hidden"] + g, 2 * g, hhi, hlo, i=e, per=4)
            for n in range(4):
                split(u0 + 10 + 2 * n, 2, e, 16)
                group_done(u0 + 9 + 2 * n, e, 16)
                part = yacc[:, :, n * NW:(n + 1) * NW]
                dve.tensor_tensor(part, banks(n), part, ALU.add).then_inc(acc_freed, 1)
        dve.wait_ge(acc_freed, GROUP["a_in"])
        link(dve.tensor_tensor(yacc, yacc, bc(gm_b.unsqueeze(1), [P, T, D]), ALU.mult))
        link(dve.tensor_tensor(res3, res3, yacc, ALU.add))

        rms_rows(RMS["a"], EPS2, rows3, res3, D).then_inc(normed, 1)
        for g in range(8):
            build(BUILD["a"] + g, 2 * g, xhi, xlo, lambda k: cols2[:, V_NORM_A + k:V_NORM_A + k + 1])
        with dve.Fori(0, 9) as i:
            split(UNIT["a_in"] + 2, 4, i, 4)
        dve.wait_ge(acc_freed, GROUP["a_out"])

        def rotate(x, n_heads):
            x1, x2 = x[:, :, :, 0:ROT], x[:, :, :, ROT:2 * ROT]
            shape = [P, T, n_heads, ROT]
            cos, sin = (bc(w[:, :, :].unsqueeze(2), shape) for w in (ropc, rops))
            tmp = [r[:, 0:T * n_heads * ROT].rearrange("p (t h d) -> p t h d", t=T, d=ROT) for r in rope_t]
            for dst, src, w in ((tmp[0], x1, cos), (tmp[1], x2, sin), (tmp[2], x2, cos), (tmp[3], x1, sin)):
                ins = dve.tensor_tensor(dst, src, w, ALU.mult)
            link(ins)
            dve.tensor_tensor(x1, tmp[0], tmp[1], ALU.subtract)
            ins = dve.tensor_tensor(x2, tmp[2], tmp[3], ALU.add)
            return ins

        heads_of = lambda x, n: x.rearrange("p t (h d) -> p t h d", h=n)
        link(rotate(heads_of(q2, 32), 32))
        rotate(heads_of(kv_a[:, :, 0:256], KVG), KVG).then_inc(roped, 1)

        def maxima(r, g, per, sm, keys, mask, sink, any_key):
            top = m8[:, r % 2, :]
            for p in range(4):
                apart(dve, scores2, plus(4 * r + p + 1, 4 * per, g), dve_passed)
                for h in (2 * p, 2 * p + 1):
                    ins = dve.tensor_tensor_reduce(out=sm[r % 2][h][:, 0:keys], in0=acc[:, p, (h % 2) * L:(h % 2) * L + keys],
                                                   in1=mask, scale=1.0, scalar=3 * NEG, op0=ALU.add, op1=ALU.max,
                                                   accum_out=top[:, h:h + 1])
                ins.then_inc(masked2, 1)
            dve.wait_ge(masked2, 4 + plus(4 * r + 4, 4 * per, g))
            if sink:
                link(dve.tensor_tensor(top, top, sinks[:, bass.ds(g * HG, HG)], ALU.max), g)
            if any_key is not None:
                link(dve.tensor_scalar(top, top, any_key, None, ALU.mult), g)
            dve.tensor_scalar(top, top, -1.0, None, ALU.mult).then_inc(max2, 1)
            if sink:
                dve.wait_ge(max2, plus(r + 1, per, g))
                dve.tensor_tensor(sk[:, r % 2, :], top, sinks[:, bass.ds(g * HG, HG)], ALU.add).then_inc(sink_arg, 1)

        def copy_probs(r, g, per, p, keys):
            dve.wait_ge(probs_turned, plus(4 * r + p + 1, 4 * per, g))
            dve.wait_ge(out2, 2 + (plus(4 * r + p - 1, 4 * per, g)))
            n, w = min(keys, P), 2 * -(-keys // P) * P
            dve.tensor_copy(pT[0:n, p % 2, 0:w], turn[0:n, p % 2, 0:w]).then_inc(probsT_ready[1], 1)

        def outputs(r, g, per, t, sink, any_key, gate):
            total = s8[:, r % 2, :]
            dve.wait_ge(exp2, plus(4 * r + 4, 4 * per, g))
            if sink:
                dve.wait_ge(sink_exp, plus(r + 1, per, g))
                link(dve.tensor_tensor(total, total, sk[:, r % 2, :], ALU.add), g)
            if any_key is not None:
                link(dve.tensor_scalar(total, total, 1.0e-30, None, ALU.max), g)
            link(dve.reciprocal(total, total), g)
            if gate is not None:
                link(dve.tensor_tensor(total, total, gate_b[:, t, bass.ds(gate * 32 + g * HG, HG)], ALU.mult), g)
            dve.wait_ge(out2, 2 + (plus(4 * r + 4, 4 * per, g)))
            o = aux[:, r % 2, :].rearrange("p (h d) -> p h d", h=HG)
            dst = rows3[:, t, bass.ds(g * NW, NW)]
            w = bc(total.unsqueeze(2), [P, HG, HD])
            if not gate:
                dve.tensor_tensor(dst.rearrange("p (h d) -> p h d", h=HG), o, w, ALU.mult).then_inc(out2_taken, 1)
            else:
                dve.tensor_tensor(otmp.rearrange("p (h d) -> p h d", h=HG), o, w, ALU.mult).then_inc(out2_taken, 1)
                dve.wait_ge(out2_taken, 2 + plus(r + 1, per, g))
                link(dve.tensor_tensor(dst, dst, otmp, ALU.add), g)

        def rounds(r0, kinds, g, sm, sink=False):
            per = len(kinds)
            for j in range(-1, per):
                if j + 1 < per:
                    keys, mask, _, any_key, _ = kinds[j + 1]
                    maxima(r0 + j + 1, g, per, sm, keys, mask, sink, any_key)
                if j >= 0:
                    keys, _, t, any_key, gate = kinds[j]
                    for p in (1, 3):
                        copy_probs(r0 + j, g, per, p, keys)
                    outputs(r0 + j, g, per, t, sink, any_key, gate)

        dve.wait_ge(masks_in, 16)
        with dve.Fori(0, KVG) as g:
            end = looped(6, KVG)
            rounds(ROUND_A, [(P, causal[:, 0:P], 0, None, None), (L, windowed, 1, None, None)], g, sm_a, sink=True)
            end()
        dve.wait_ge(out2_taken, 2 + ROUND_B)
        dve.tensor_tensor(rows3, rows3, z2, ALU.mult).then_inc(gated, 1)
        for g in range(8):
            build(BUILD["a_o"] + g, 2 * g, xhi, xlo)

        def residual(name, turns):
            u0, g0 = UNIT[name], GROUP[name]
            with dve.Fori(0, turns) as i:
                for n in range(2):
                    split(u0 + 4 * n + 2, 4, i, 8)
                    group_done(u0 + 4 * n + 3, i, 8)
                    part = res3[:, :, bass.ds(i * W1 + n * NW, NW)]
                    dve.tensor_tensor(part, banks(g0 + n), part, ALU.add).then_inc(acc_freed, 1)

        residual("a_out", 2)
        dve.wait_ge(acc_freed, GROUP["b_att"])
        rms_rows(RMS["b"], EPS2, rows3, res3, D).then_inc(normed, 1)
        for g in range(8):
            build(BUILD["b"] + g, 2 * g, xhi, xlo, lambda k: cols2[:, V_NORM_B + k:V_NORM_B + k + 1])
        with dve.Fori(0, 8) as i:
            split(UNIT["b_att"] + 2, 4, i, 4)
        dve.wait_ge(acc_freed, GROUP["b_z"])
        link(rotate(heads_of(q2, 32), 32))
        link(rotate(heads_of(kv6[:, :, 512:768], KVG), KVG))
        rotate(heads_of(kv6[:, :, 1024:1280], KVG), KVG).then_inc(roped, 1)
        for n in range(2):
            if n:
                dve.wait_ge(cmp_turned, n)
            src = kv6[:, :, n * 256:(n + 1) * 256].rearrange("p t (g d) -> p t g d", g=KVG)
            dve.tensor_copy(kdup[:, :, :, 0:HD], src)
            dve.tensor_copy(kdup[:, :, :, HD:P], src).then_inc(dup_ready, 1)
            dve.wait_ge(cmp_copied, n + 1)
            pos = cols2[:, V_KPOS + 16 * n:V_KPOS + 16 * n + 16]
            for half in range(2):
                on = slice(half * HD, (half + 1) * HD)
                kc = kcT[on, :].rearrange("p (g c m two) -> p two m g c", g=KVG, c=16, two=2)[:, half]
                for l in range(2):
                    ins = dve.tensor_tensor(blkT[on, 8 * l:8 * l + 8], kc[:, :, :, l:l + NC],
                                            bc(pos[on, 8 * l:8 * l + 8].unsqueeze(2).unsqueeze(3), [HD, 8, KVG, NC]), ALU.add)
            ins.then_inc(blk_ready, 1)
            dve.wait_ge(gelu_x, n + 1)
            link(dve.tensor_tensor(hy, hx, hx, ALU.mult))
            link(dve.tensor_scalar(hy, hy, 0.044715, 1.0, ALU.mult, ALU.add))
            dve.tensor_tensor(hy, hy, hx, ALU.mult).then_inc(gelu_arg, 1)
            dve.wait_ge(gelu_tanh, n + 1)
            link(dve.tensor_scalar(hy, hy, 0.5, 0.5, ALU.mult, ALU.add))
            dve.tensor_tensor(hz, hx, hy, ALU.mult).then_inc(gelu_done, 1)
        with dve.Fori(0, KVG) as g:
            end = looped(20, KVG)
            kinds = []
            for t in range(T):
                mask = causal[:, 0:P] if t == 0 else causal[:, P:3 * P]
                kinds += [(NC, cmp_mask[:, NC * t:NC * t + NC], t, cmp_any[:, t:t + 1], 0),
                          ((t + 1) * P, mask, t, None, 1), ((t + 1) * P, mask, t, None, 2)]
            rounds(ROUND_B, kinds, g, sm_b)
            end()
        with dve.Fori(0, 4) as i:
            split(UNIT["b_z"] + 2, 4, i, 4)
        dve.wait_ge(acc_freed, GROUP["b_out"])
        dve.tensor_tensor(rows3, rows3, z2, ALU.mult).then_inc(gated, 1)
        for g in range(8):
            build(BUILD["b_o"] + g, 2 * g, xhi, xlo)
        residual("b_out", 1)
        u0, g0 = UNIT["b_out"], GROUP["b_out"]
        for n in (2, 3):
            split(u0 + 4 * n + 2, 4)
            group_done(u0 + 4 * n + 3)
            part = res3[:, :, n * NW:(n + 1) * NW]
            dve.tensor_tensor(part, banks(g0 + n), part, ALU.add).then_inc(acc_freed, 1)
        dve.wait_ge(acc_freed, g0 + 4)
        link(rms_rows(RMS["final"], EPS2, rows3, res3, D))
        dve.wait_ge(fin_in, 16)
        dve.tensor_tensor(rows3, rows3, bc(fin_w.unsqueeze(1), [P, T, D]), ALU.mult).then_inc(norm_done, 1)

    @block.tensor
    def _(pe):
        for signal, n in ((modcol_ready, 1), (slab_turned, 1), (out2, 2), (q_turned, 1)):
            pe.sem_inc(signal, n)
        def product(u0, g, k_units, k_first=0, hi=xhi, lo=xlo, built=None, i=None, per=0, g_count=0, g_per=0, width=NW,
                    wait_build=None):
            if g_count >= 2:
                pe.wait_ge(acc_freed, plus(g_count - 1, g_per, i))
            for k in range(k_units):
                u = u0 + k
                pe.wait_ge(lo_ready, plus(u + 1, per, i))
                if built is not None:
                    built(k)
                for kk in range(UK):
                    kt = k_first + UK * k + kk
                    w_hi, w_lo = whi[:, u % 2, kk, 0:width], wlo[:, u % 2, kk, 0:width]
                    for t in range(T):
                        bank = acc[:, 2 * (g % 2) + t, 0:width]
                        tok = slice(t * P, (t + 1) * P)
                        pe.matmul(bank, hi[:, kt, tok], w_hi, start=kt == k_first, stop=False)
                        pe.matmul(bank, hi[:, kt, tok], w_lo, start=False, stop=False)
                        mm = pe.matmul(bank, lo[:, kt, tok], w_hi, start=False, stop=kt == k_first + UK * k_units - 1)
                mm.then_inc(units_used, 1)

        def condition(u0, g, i, per, g_count, g_per):
            if isinstance(g_count, int) and g_count >= 1:
                pe.wait_ge(acc_freed, plus(g_count - 1, g_per, i))
            for k in range(4):
                u = u0 + k
                pe.wait_ge(lo_ready, plus(u + 1, per, i))
                for kk in range(UK):
                    kt = UK * k + kk
                    pe.matmul(acc[:, 2 * (g % 2), :], xhi[:, kt, 0:P], whi[:, u % 2, kk], start=kt == 0, stop=False)
                    mm = pe.matmul(acc[:, 2 * (g % 2), :], xhi[:, kt, 0:P], wlo[:, u % 2, kk], start=False,
                                   stop=kt == KT - 1)
                mm.then_inc(units_used, 1)

        def condition_columns():
            for n in range(2):
                for s in range(4):
                    o = 2 * (4 * n + s)
                    mm = pe.matmul(aux[:, 1, o:o + 2], modrow[0:4, n, s * P:(s + 1) * P], sel[0:4, P:P + 2],
                                   start=True, stop=True)
            mm.then_inc(modcol_ready, 1)

        def turn_rows(name, src, pairs=8, i=None, per=0, ready=None):
            for g in range(pairs):
                n = BUILD[name] + g
                if ready is not None:
                    ready(g)
                if n >= 2:
                    pe.wait_ge(xt_ready, plus(n - 1, per, i))
                for k in range(2):
                    for t in range(T):
                        mm = pe.transpose(turn[:, n % 2, k * L + t * P:k * L + (t + 1) * P],
                                          src[:, t, (2 * g + k) * P:(2 * g + k + 1) * P], ident[:, :])
                mm.then_inc(turned, 1)

        def built(name, i=None, per=0):
            return lambda k: pe.wait_ge(xt_ready, plus(BUILD[name] + 2 * k + 2, per, i))

        def groups(name, turns, first=0, build=None, i_width=2):
            with pe.Fori(0, turns) as i:
                for n in range(2):
                    product(UNIT[name] + 4 * (first + n), GROUP[name] + first + n, 4, built=built(build), i=i, per=8,
                            g_count=GROUP[name] + first + n, g_per=2)

        pe.wait_ge(params_in, 16 * 25)
        pe.transpose(aux[:, 0, 0:P], vec1, ident[:, :])
        pe.transpose(aux[:, 0, P:P + V_END], vec2[0:V_END, :], ident[0:V_END, 0:V_END]).then_inc(setup_turned, 1)
        pe.wait_ge(modw_ready, 1)
        pe.wait_ge(cols_ready, 1)
        with pe.Fori(0, 4) as i:
            for n in range(2):
                condition(UNIT["mod1"] + 4 * n, n, i, 8, 0, 2)
            pe.wait_ge(acc_freed, plus(2, 2, i))
            pe.wait_ge(modcol_taken, 1 + i)
            condition_columns()
        pe.wait_ge(normed, 4)
        turn_rows("ctx", rows3)
        groups("ctx", 2, build="ctx")
        turn_rows("x", res3)
        groups("in", 8, build="x")
        pe.wait_ge(pool_in, 32)
        pe.wait_ge(acc_freed, GROUP["in"] + 8)
        for b in range(4):
            if b >= 2:
                pe.wait_ge(pooled_copied, b - 1)
            for n in range(2):
                s = 2 * b + n
                for t in range(T):
                    mm = pe.matmul(turn[:, b % 2, n * L:(n + 1) * L], u_rows[:, t, s * P:(s + 1) * P], band[:, t, s // 2, :],
                                   start=t == 0, stop=t == T - 1)
            mm.then_inc(pooled, 1)
        pe.wait_ge(pooled_copied, 4)
        for g in range(4):
            n = BUILD["pool"] + g
            if g >= 2:
                pe.wait_ge(xt_ready, n - 1)
            for d in range(2):
                for c in range(2):
                    mm = pe.matmul(turn[:, n % 2, d * L:(d + 1) * L], poolw[:, g, c, d * P:(d + 1) * P],
                                   dT[:, 2 * g + c, :], start=c == 0, stop=c == 1)
            mm.then_inc(turned, 1)
        pe.wait_ge(xt_ready, BUILD["heads"])
        with pe.Fori(0, HEADS1) as h:
            pe.wait_ge(slab_ready, h + 1)
            pe.wait_ge(head_sq, 1 + (2 * h))
            for s in range(6):
                mm = pe.transpose(aux_flat[:, s * P:(s + 1) * P], slab[:, s, :], ident[:, :])
            mm.then_inc(slab_turned, 1)
            pe.wait_ge(slabT_ready, h + 1)
            for t in range(T):
                pe.wait_ge(exp1, 1 + (plus(t, T, h)))
                for c in range(2):
                    on = slice(c * HD, (c + 1) * HD)
                    mm = pe.matmul(turn[:, c, :], slabT[on, t * P:(t + 1) * P], slabT[on, 256:768], start=True, stop=True)
                mm.then_inc(scores1, 1)
                pe.wait_ge(attn1, plus(t + 1, T, h))
                for k in range(4):
                    mm = pe.transpose(aux[:, 0, k * P:(k + 1) * P], prob[:, 0, k * P:(k + 1) * P], ident[:, :])
                mm.then_inc(attn_turned, 1)
                pe.wait_ge(attnT_ready, plus(t + 1, T, h))
                for k in range(4):
                    mm = pe.matmul(aux[:, 1, 0:VD], probT[:, k * P:(k + 1) * P], v1[:, k, bass.ds(h * VD, VD)],
                                   start=k == 0, stop=k == 3)
                mm.then_inc(head_out, 1)
        pe.wait_ge(head_done, HEADS1)
        turn_rows("heads", heads, pairs=4)
        u0, g0 = UNIT["up"], GROUP["up"]
        with pe.Fori(0, 4) as i:
            for n, (name, k_first) in enumerate((("heads", 0), ("pool", 8))):
                product(u0 + 2 * n, n, 2, k_first, built=built(name), i=i, per=4, g_count=g0 + n, g_per=2)
        pe.wait_ge(modw_ready, 2)
        u0, g0 = UNIT["mod2"], GROUP["mod2"]

        def conditions(first, turns, n0, post):
            with pe.Fori(0, turns) as i:
                for n in range(2):
                    condition(u0 + 4 * (first + n), n, i, 8, g0 + first + n, 2)
                pe.wait_ge(acc_freed, plus(g0 + first + 2, 2, i))
                pe.wait_ge(modcol_taken, 1 + (plus(n0, 1, i)))
                post()

        def broadcast_rows():
            for n in range(2):
                mm = pe.matmul(aux[:, n, :], sel[0:4, 0:P], modrow[0:4, n, :], start=True, stop=True)
            mm.then_inc(modcol_ready, 1)
        conditions(0, 2, 4, broadcast_rows)
        conditions(4, 4, 6, condition_columns)
        conditions(12, 2, 10, broadcast_rows)
        pe.wait_ge(acc_freed, GROUP["mod2"])
        turn_rows("mix", rows3)
        groups("wo", 2, build="mix")
        pe.wait_ge(cond_ready, 2)
        pe.wait_ge(normed, 5)
        turn_rows("mlp", rows3)
        u0, g0 = UNIT["mlp"], GROUP["mlp"]
        with pe.Fori(0, 8) as e:
            for n in range(2):
                product(u0 + 4 * n, n, 4, built=built("mlp"), i=e, per=16, g_count=g0 + n, g_per=6)
            turn_rows("hidden", hid, pairs=4, i=e, per=4,
                      ready=lambda g: pe.wait_ge(squared, plus(g // 2 + 1, 2, e)))
            for n in range(4):
                product(u0 + 8 + 2 * n, n, 2, 0, hhi, hlo, built("hidden", e, 4), e, 16, g0 + 2 + n, 6)
        pe.wait_ge(normed, 6)
        turn_rows("a", rows3)
        groups("a_in", 2, build="a")
        u0, g0 = UNIT["a_in"], GROUP["a_in"]
        product(u0 + 16, 0, 4, built=built("a"), g_count=g0 + 4)
        groups("a_in", 2, first=5, build="a")

        def turn_keys(keys, n):
            for g in range(KVG):
                for t in range(T):
                    mm = pe.transpose(turn_flat[0:HD, g * L + t * P:g * L + (t + 1) * P], keys[:, t, g * HD:(g + 1) * HD],
                                      ident[:, :])
            mm.then_inc(kT_turned, 1)
            pe.wait_ge(kT_ready, n + 1)

        def queries(n, g):
            apart(pe, qs_ready, plus(n + 1, 1, g), pe_passed)
            for b in range(4):
                if b >= 2:
                    apart(pe, qT_ready, plus(4 * n + b - 1, 4, g), pe_passed)
                for h in range(2):
                    for t in range(T):
                        o = (2 * h + t) * P
                        hh = 2 * b + h
                        mm = pe.transpose(turn[0:HD, b % 2, o:o + P], qs[:, t, hh * HD:(hh + 1) * HD], ident[:, :])
                mm.then_inc(q_turned, 1)
            pe.wait_ge(qT_ready, plus(4 * n + 4, 4, g))

        def scores(r, g, per, t, keys, kT):
            for p in range(4):
                apart(pe, masked2, 4 + plus(4 * r + p - 3, 4 * per, g), pe_passed)
                for h in range(2):
                    mm = pe.matmul(acc[:, p, h * L:h * L + keys], qT[:, 2 * p + h, t, :], kT, start=True, stop=True)
                mm.then_inc(scores2, 1)

        def outputs(r, g, per, sm, keys, v_of):
            kt, n = -(-keys // P), min(keys, P)

            def turn_probs(p):
                pe.wait_ge(exp2, plus(4 * r + p + 1, 4 * per, g))
                for h in range(2):
                    for k in range(kt):
                        o = (h * kt + k) * P
                        mm = pe.transpose(turn[0:n, p % 2, o:o + P], sm[r % 2][2 * p + h][:, k * P:k * P + n], ident[:, :])
                mm.then_inc(probs_turned, 1)

            pe.wait_ge(out2_taken, 2 + plus(r - 1, per, g))
            turn_probs(0)
            for p in range(4):
                if p < 3:
                    turn_probs(p + 1)
                apart(pe, probsT_ready[p % 2], plus(2 * r + p // 2 + 1, 2 * per, g), pe_passed)
                for h in range(2):
                    for k in range(kt):
                        o = (h * kt + k) * P
                        hh = 2 * p + h
                        mm = pe.matmul(aux[:, r % 2, hh * HD:(hh + 1) * HD], pT[0:n, p % 2, o:o + P], v_of(k),
                                       start=k == 0, stop=k == kt - 1)
                mm.then_inc(out2, 1)

        def rounds(r0, kinds, g, sm):
            per = len(kinds)
            for j in range(-1, per):
                if j + 1 < per:
                    keys, t, kT, _ = kinds[j + 1]
                    scores(r0 + j + 1, g, per, t, keys, kT)
                if j >= 0:
                    keys, _, _, v_of = kinds[j]
                    outputs(r0 + j, g, per, sm, keys, v_of)

        pe.wait_ge(roped, 1)
        turn_keys(kv_a, 0)
        with pe.Fori(0, KVG) as g:
            queries(0, g)
            v_of = lambda k: kv_a[:, k, bass.ds(256 + g * HD, HD)]
            rounds(ROUND_A, [(n * P, n - 1, kTs[:, bass.ds(g * L, n * P)], v_of) for n in (1, 2)], g, sm_a)
        pe.wait_ge(gated, 1)
        turn_rows("a_o", rows3)
        groups("a_out", 2, build="a_o")
        pe.wait_ge(normed, 7)
        turn_rows("b", rows3)
        groups("b_att", 2, build="b")
        u0, g0 = UNIT["b_att"], GROUP["b_att"]
        for n in range(4):
            product(u0 + 16 + 4 * n, g0 + n, 4, built=built("b"), g_count=g0 + 4 + n, width=NW if n < 3 else B_GATES)
        for n in range(2):
            pe.wait_ge(dup_ready, n + 1)
            pe.wait_ge(xt_ready, BUILD["b_o"])
            for g in range(KVG):
                for t in range(T):
                    mm = pe.transpose(turn_flat[:, g * L + t * P:g * L + (t + 1) * P], kdup[:, t, g, :], ident[:, :])
            mm.then_inc(cmp_turned, 1)
            pe.wait_ge(blk_ready, n + 1)
            pe.wait_ge(cmp_w_in, 32 * (n + 1))
            for l in range(16):
                mm = pe.matmul(aux[0:60, 0, 0:256], blkT[:, l].rearrange("p g c -> p (g c)"), w1c[:, l, :],
                               start=l == 0, stop=l == 15)
            mm.then_inc(hid_ready, 1)
            pe.wait_ge(gelu_done, n + 1)
            for k in range(2):
                mm = pe.transpose(aux[:, 1, k * 60:(k + 1) * 60], hz[:, k * P:(k + 1) * P], ident[0:60, 0:60])
            mm.then_inc(hT_turned, 1)
            pe.wait_ge(hT_ready, n + 1)
            if n == 0:
                for k in range(2):
                    mm = pe.matmul(aux[0:HD, 0, 0:60], w2c[:, 0, k, :], hT[:, k, :], start=k == 0, stop=k == 1)
            else:
                for g in range(KVG):
                    for k in range(2):
                        mm = pe.matmul(aux[0:NC, 0, g * HD:(g + 1) * HD], hT[:, k, g * NC:(g + 1) * NC], w2c[:, 1, k, :],
                                       start=k == 0, stop=k == 1)
            mm.then_inc(cmp_out, 1)
            pe.wait_ge(cmp_stored, n + 1)
        pe.wait_ge(roped, 2)
        turn_keys(kv6[:, :, 512:768], 1)
        turn_keys(kv6[:, :, 1024:1280], 2)
        with pe.Fori(0, KVG) as g:
            queries(4, g)
            v_of = [lambda k, v0=v0: kv6[:, k, bass.ds(v0 + g * HD, HD)] for v0 in (768, 1280)]
            kinds = []
            for t in range(T):
                kinds.append((NC, t, cmpk[:, bass.ds(g * NC, NC)], lambda k: cmpv[:, bass.ds(g * HD, HD)]))
                kinds += [((t + 1) * P, t, kT[:, bass.ds(g * L, (t + 1) * P)], v) for kT, v in zip((kTs, kTw), v_of)]
            rounds(ROUND_B, kinds, g, sm_b)
        groups("b_z", 2, build="b")
        pe.wait_ge(gated, 2)
        turn_rows("b_o", rows3)
        groups("b_out", 2, build="b_o")

    ctx.close()


def shape_constants():
    f = np.float32
    sel = np.zeros((4, P + 2), f)
    sel[0, 0:P] = sel[2, 0:P] = 1
    for c in range(2):
        sel[c, P + c] = sel[2 + c, P + c] = 1
    band = np.zeros((L, 4, L), f)
    for g, w in enumerate((2, 4, 8, 16)):
        for t in range(L):
            lo, hi = max(t - w // 2, 0), min(t + w - w // 2, L)
            band[lo:hi, g, t] = 1.0 / (hi - lo)
            band[t, g, t] -= 1
    band = band.reshape(T, P, 4, L).transpose(1, 0, 2, 3)
    half = HD // 2
    inv = (f(10000.0) ** (-np.arange(0, half, 2, dtype=f) / f(half))).astype(f)
    tok = np.arange(L)
    cos, sin = np.ones((6, P, HD), f), np.zeros((6, P, HD), f)
    for n, pos in enumerate((tok // 64, tok % 64)):
        ang = pos.astype(f)[:, None] * inv[None, :]
        c, s = np.cos(ang).reshape(T, P, 16), np.sin(ang).reshape(T, P, 16)
        for tiles in (slice(0, 2), slice(2, 4)):
            cos[tiles, :, n * 32:n * 32 + 16] = cos[tiles, :, n * 32 + 16:n * 32 + 32] = c
            sin[tiles, :, n * 32:n * 32 + 16], sin[tiles, :, n * 32 + 16:n * 32 + 32] = -s, s
    invf = (500000.0 ** (-np.arange(0, 16, 2) / 16.0)).astype(f)
    p = np.arange(P)
    masks = np.zeros((P, 672), f)
    k1, k2 = np.arange(P), np.arange(L)
    masks[:, 0:128] = np.where(k1[None] <= p[:, None], 0, NEG)
    q = P + p[:, None]
    masks[:, 128:384] = np.where(k2[None] <= q, 0, NEG)
    masks[:, 384:640] = np.where((k2[None] <= q) & (q - k2[None] < 128), 0, NEG)
    for t in range(T):
        valid = 16 * np.arange(NC)[None] + 31 <= (t * P + p)[:, None]
        masks[:, 640 + NC * t:640 + NC * t + NC] = np.where(valid, 0, NEG)
        masks[:, 670 + t] = valid.any(1)
    return {"c_ident": np.eye(P, dtype=f), "c_sel": sel, "c_band": np.ascontiguousarray(band),
            "c_cos": np.ascontiguousarray(cos.transpose(1, 0, 2)), "c_sin": np.ascontiguousarray(sin.transpose(1, 0, 2)),
            "c_invf": np.ascontiguousarray(np.broadcast_to(invf, (P, ROT))), "c_masks": masks}


NAMES = {
    "x": "x", "c": "c", "ctx": "ctx", "c_ctx": "c_ctx", "w_mod": "w_mod", "b_mod": "b_mod", "norm_attn_w": "norm_attn_w",
    "w_in": "w_in", "q_norm_w": "q_norm_w", "k_norm_w": "k_norm_w", "lam0": "lambda_q1", "lam1": "lambda_k1",
    "lam2": "lambda_q2", "lam3": "lambda_k2", "subln_w": "subln_w", "pool_w": "pool_w", "pool_scale": "pool_scale",
    "w_a_up": "w_a_up", "w_b_up": "w_b_up", "w_o": "w_o", "norm_mlp_w": "norm_mlp_w", "w_ff1": "w_ff1", "w_ff2": "w_ff2",
    "positions": "positions_2", "norm_w": "norm_w_2", "final_norm_w": "final_norm_w_2", "a_w_in": "a_w_in_2",
    "sinks": "a_sinks_2", "a_w_out": "a_w_out_2", "b_w_in": "b_w_in_2", "kpos": "b_cmp_k_pos_2", "kw1": "b_cmp_k_w1_2",
    "kw2": "b_cmp_k_w2_2", "vpos": "b_cmp_v_pos_2", "vw1": "b_cmp_v_w1_2", "vw2": "b_cmp_v_w2_2", "b_w_out": "b_w_out_2",
}


def kernel(**inputs):
    import concourse.bacc as bacc
    from concourse.bass_utils import run_bass_kernel_spmd

    nc = bacc.Bacc("TRN2", target_bir_lowering=False, num_devices=1)
    arrays = {}
    for name, given in NAMES.items():
        x = np.ascontiguousarray(inputs[given])
        if name not in ("norm_w", "c_ctx", "final_norm_w") and x.ndim > 1 and x.shape[0] == 1:
            x = x[0]
        arrays[name] = x
    arrays.update(shape_constants())
    aps = {n: nc.dram_tensor(f"in_{n}", x.shape, mybir.dt.from_np(x.dtype), kind="ExternalInput").ap()
           for n, x in arrays.items()}
    out = nc.dram_tensor("out_y", (L, D), F32, kind="ExternalOutput").ap()
    dit_kernel(nc, aps, out)
    r = run_bass_kernel_spmd(nc, [{f"in_{n}": x for n, x in arrays.items()}], core_ids=[0])
    return r.results[0]["out_y"].reshape(1, L, D)
```

```python
from contextlib import ExitStack

import concourse.bass as bass
import concourse.mybir as mybir
import numpy as np

F32, F32R, I32 = mybir.dt.float32, mybir.dt.float32r, mybir.dt.int32
ACT = mybir.ActivationFunctionType
ALU = mybir.AluOpType
AX = mybir.AxisListType

P = 128
D = 2048
KT = D // P
NW = 512
UK = 4
L = 256
T = L // P
HEADS1, VD = 8, 128
W1 = 1024
EPS1, EPS2 = 1e-6, 1e-5
LAM_INIT = 0.8 - 0.6
HD = 64
KVG = 4
HG = 8
NC = 15
NEG = -1.0e30
B_GATES = 96
ROT = 8

PHASES = [("mod1", 32, 8), ("ctx", 16, 4), ("in", 32, 8), ("att", 64, 8), ("up", 48, 8), ("wo", 16, 4),
          ("mlp", 128, 48), ("a_in", 20, 5), ("a_z", 16, 4), ("a_out", 16, 4), ("b_att", 32, 8), ("b_z", 16, 4),
          ("b_out", 16, 4)]
UNIT, GROUP = {}, {}
UNITS = _g = 0
for _name, _nu, _ng in PHASES:
    UNIT[_name], GROUP[_name] = UNITS, _g
    UNITS, _g = UNITS + _nu, _g + _ng

BUILDS = [("ctx", 8), ("x", 8), ("heads", 4), ("pool", 4), ("mix", 8), ("mlp", 8), ("hidden", 32),
          ("a", 8), ("a_o", 8), ("b", 8), ("b_o", 8)]
BUILD = {}
_b = 0
for _name, _nb in BUILDS:
    BUILD[_name] = _b
    _b += _nb

RMS = {"rows": 0, "att1": 4, "mlp": 28, "a": 29, "b": 30, "final": 31}
ROUND_A, ROUND_B = 0, 8
FILLS = {"a_z": ((1, 1, 2), (2, 0, 0, 2), (1, 1, 1, 1), (1, 1, 1, 1)),
         "b_z": ((1, 1, 1), (0, 0, 0, 1)) + 6 * ((1, 1, 0, 0),)}
GATES_BEFORE = {"a_z": 0, "b_z": KVG}
SMALL = 19
KEYS_A = (P, 2 * P)
KEYS_B = (NC, P, P, NC, 2 * P, 2 * P)
V_NORM1, V_NORM2, V_NORM_A, V_NORM_B, V_POOL, V_SUBLN, V_KPOS, V_VPOS, V_END = 0, 16, 32, 48, 64, 72, 73, 89, 105


def halves_filled(name, n):
    tiles = [sum(part) for part in FILLS[name]]
    before = sum(tiles[:n]) // 2
    return before, sum(tiles[:n + 1]) // 2 - before


def plus(base, step, i):
    return base if i is None else base + step * i


def dit_kernel(nc, a, out):
    ctx = ExitStack()
    sb = lambda n, s, d=F32: ctx.enter_context(nc.sbuf_tensor(n, s, d))
    sem = lambda n: ctx.enter_context(nc.semaphore(n))
    v3 = lambda ap, n: ap.rearrange("p (t n) -> p t n", n=n)

    raw = sb("raw", [P, 4, UK, NW])
    whi = sb("whi", [P, 2, UK, NW], F32R)
    wlo = sb("wlo", [P, 2, UK, NW], F32R)
    xhi = sb("xhi", [P, KT, L], F32R)
    xlo = sb("xlo", [P, KT, L], F32R)
    with nc.sbuf_tensor("hhi", [P, 8, L], F32R) as hhi, nc.sbuf_tensor("hlo", [P, 8, L], F32R) as hlo:
        pass
    qkv = sb("qkv", [P, 10240])
    arena = sb("arena", [P, 16384])
    res, rows, big = arena[:, 0:4096], arena[:, 4096:8192], arena[:, 8192:16384]
    res3, rows3 = v3(res, D), v3(rows, D)
    ident = sb("ident", [P, P])
    cols1 = sb("cols1", [P, P])
    cols2 = sb("cols2", [P, V_END])
    modcol = sb("modcol", [P, 64])
    scale_x, shift_x = sb("scale_x", [P, KT]), sb("shift_x", [P, KT])
    sel = sb("sel", [4, P + 2])
    tab = sb("tab", [P, 768])
    sinks = sb("sinks", [P, 32])
    silu_c = sb("silu_c", [P, 2, KT])
    mean, rstd, neghalf = sb("mean", [P, 12]), sb("rstd", [P, 12]), sb("neghalf", [P, 12])
    lam = sb("lam", [P, 8])
    m8, s8 = sb("m8", [P, 2, 8]), sb("s8", [P, 2, 8])
    ropc, rops = sb("ropc", [P, T, ROT]), sb("rops", [P, T, ROT])
    gate_b = sb("gate_b", [P, T, B_GATES])
    cmpk = sb("cmpk", [HD, KVG * NC])
    pos2 = sb("pos2", [P, T], I32)

    modrow1 = v3(big[:, 0:1024], NW)
    mtmp = v3(big[:, 1024:2048], NW)
    vec1, vec2 = big[:, 2048:2176], big[:, 2176:2304]
    lamv = v3(big[:, 2304:2560], HD)
    qkw = v3(big[:, 2560:2688], HD)
    qkws = v3(big[:, 2688:2816], HD)
    rcos, rsin = v3(big[:, 2816:3200], HD), v3(big[:, 3200:3584], HD)
    posf, ang, angk, invf = (v3(big[:, 3584 + 16 * n:3600 + 16 * n], ROT) for n in range(4))
    scale_ctx, shift_ctx = big[:, 3648:3664], big[:, 3664:3680]
    junk = big[:, 4096:6144]
    qk6 = v3(qkv[:, 0:6144], W1)
    kv_out = qkv[:, 2048:10240].rearrange("p (w t n) -> p w t n", w=2, t=4)
    v1 = v3(qkv[:, 6144:10240], W1)
    gates = v3(big, 2 * D)
    u_rows = v3(res[:, 0:2048], W1)
    dT = v3(res[:, 2048:4096], L)
    cflat = sb("cflat", [P, 4 * KT + P - 4], F32R)
    cvec = cflat[:, 0:4 * KT].rearrange("p (k c) -> p k c", c=4)
    band = rows[:, 2048:4096].rearrange("p (s g n) -> p s g n", s=2, g=4)
    poolw = rows[:, 2048:4096].rearrange("p (g c n) -> p g c n", g=4, c=2)
    cosw, sinw = v3(tab[:, 0:384], HD), v3(tab[:, 384:768], HD)
    heads = v3(res[:, 0:2048], W1)
    prob = v3(rows[:, 0:1024], NW)
    probT = rows[:, 1792:2304]
    slab2 = v3(rows[:, 0:768], P)
    slab = v3(rows[:, 1024:1792], P)
    slabT = rows[:, 2304:3072]
    orow, osq = v3(rows[:, 3840:4096], VD), rows[:, 3200:3328]
    modrow2 = rows[:, 3328:3840]
    upa, upb = v3(res[:, 0:1024], NW), v3(res[:, 1024:2048], NW)
    yacc = v3(big[:, 0:4096], D)
    ga_b, gm_b = qkv[:, 4096:6144], qkv[:, 6144:8192]
    modrow3 = v3(qkv[:, 8192:9216], NW)
    hid = v3(rows[:, 0:2048], W1)
    q2, z2 = v3(big[:, 0:4096], D), v3(big[:, 4096:8192], D)
    kv_a = v3(qkv[:, 0:1024], NW)
    kv6 = v3(qkv[:, 0:3072], 1536)
    qs = v3(qkv[:, 3072:4096], NW)
    qT = qkv[0:HD, 4096:6144].rearrange("p (h t n) -> p h t n", h=HG, t=T)
    sm = v3(qkv[:, 6144:8192], L)
    pT = v3(qkv[:, 8192:9216], NW)
    kTs = qkv[0:HD, 9216:10240]
    kTw = z2[0:HD, 0, 0:1024]
    kdup = z2[:, 0, 1024:2048].rearrange("p (t g n) -> p t g n", t=T, g=KVG)
    kcT = z2[:, 1, 0:1024]
    cmpv = z2[0:NC, 1, 0:256]
    cmpk_g, cmpv_g = cols1[0:HD, 0:NC], modcol[0:NC, :]
    v_g = z2[:, 1, 256:512].rearrange("p (w t n) -> p w t n", w=2, t=T)
    blkT = z2[:, 1, 1024:1984].rearrange("p (l g c) -> p l g c", l=16, g=KVG)
    w1c = v3(rows, 256)
    w2c = qkv[:, 8192:8448].rearrange("p (w k n) -> p w k n", w=2, k=2)
    hx, hy, hz = sm[0:60, 0, :], sm[0:60, 1, :], sm[0:60, 2, :]
    hT = v3(qkv[:, 6144 + 768:6144 + 888], 60)
    rope_t = [qkv[:, 6144 + 512 * n:6144 + 512 * (n + 1)] for n in range(4)]
    causal, windowed = tab[:, 0:384], tab[:, 384:640]
    cmp_mask, cmp_any = tab[:, 640:670], tab[:, 670:672]
    sk = silu_c[:, :, 0:8]
    sm2 = v3(qkv[:, 1024:3072], L)
    sm_a = [[x[:, h, :] for h in range(HG)] for x in (sm, sm2)]
    sm3 = v3(z2[:, 0, 1024:2048], L), v3(z2[:, 1, 1024:2048], L)
    sm_b = [sm_a[0], [sm3[h // 4][:, h % 4, :] for h in range(HG)]]
    otmp = z2[:, 1, 512:1024]
    fin_w = big[:, 0:2048]

    acc = ctx.enter_context(nc.psum_tensor("acc", [P, 4, NW], F32))
    turn = ctx.enter_context(nc.psum_tensor("turn", [P, 2, NW], F32))
    aux = ctx.enter_context(nc.psum_tensor("aux", [P, 2, NW], F32))
    aux_flat = aux[:, :, :].rearrange("p b n -> p (b n)")
    turn_flat = turn[:, :, :].rearrange("p b n -> p (b n)")

    raw_in = [sem(f"raw_in{i}") for i in range(4)]
    hi_ready, lo_ready = sem("hi_ready"), sem("lo_ready")
    units_used = sem("units_used")
    acc_freed = sem("acc_freed")
    turned = sem("turned")
    hi_rounded, xt_ready = sem("hi_rounded"), sem("xt_ready")
    act_chain, dve_chain = sem("act_chain"), sem("dve_chain")
    params_in, setup_turned, cols_ready = sem("params_in"), sem("setup_turned"), sem("cols_ready")
    silu_exp, modw_ready = sem("silu_exp"), sem("modw_ready")
    sumsq_ready, mean_ready, rstd_ready = sem("sumsq_ready"), sem("mean_ready"), sem("rstd_ready")
    normed = sem("normed")
    modcol_ready, modcol_taken = sem("modcol_ready"), sem("modcol_taken")
    modrow_ready, bias_in, c_in, rows_in = sem("modrow_ready"), sem("bias_in"), sem("c_in"), sem("rows_in")
    cond_ready, lam_done, sin_arg, sin_done = sem("cond_ready"), sem("lam_done"), sem("sin_arg"), sem("sin_done")
    pe_passed, act_passed, dve_passed = sem("pe_passed"), sem("act_passed"), sem("dve_passed")
    lam_sum, half_set = sem("lam_sum"), sem("half_set")
    pool_in, pooled, pooled_copied = sem("pool_in"), sem("pooled"), sem("pooled_copied")
    slab_ready, slab_turned, slabT_ready = sem("slab_ready"), sem("slab_turned"), sem("slabT_ready")
    scores1, max1, exp1, attn1 = sem("scores1"), sem("max1"), sem("exp1"), sem("attn1")
    attn_turned, attnT_ready, head_out, head_done = sem("attn_turned"), sem("attnT_ready"), sem("head_out"), sem("head_done")
    head_sq = sem("head_sq")
    mixed, x_in, squared, res_done, norm_done = sem("mixed"), sem("x_in"), sem("squared"), sem("res_done"), sem("norm_done")
    masks_in, roped, kT_turned, kT_ready = sem("masks_in"), sem("roped"), sem("kT_turned"), sem("kT_ready")
    qs_ready, q_turned, qT_ready = sem("qs_ready"), sem("q_turned"), sem("qT_ready")
    scores2, masked2, max2, exp2, sink_arg, sink_exp = (sem(n) for n in ("scores2", "masked2", "max2", "exp2", "sink_arg", "sink_exp"))
    probs_turned, out2, out2_taken = (sem(n) for n in ("probs_turned", "out2", "out2_taken"))
    probsT_ready = sem("probsT_act"), sem("probsT_dve")
    cmp_w_in, dup_ready, cmp_turned, cmp_copied, blk_ready, hid_ready = (sem(n) for n in (
        "cmp_w_in", "dup_ready", "cmp_turned", "cmp_copied", "blk_ready", "hid_ready"))
    gelu_x, gelu_arg, gelu_tanh, gelu_done, hT_turned, hT_ready, cmp_out, cmp_stored = (sem(n) for n in (
        "gelu_x", "gelu_arg", "gelu_tanh", "gelu_done", "hT_turned", "hT_ready", "cmp_out", "cmp_stored"))
    gate_ready, values_ready, gated, fin_in, out_sent = sem("gate_ready"), sem("values_ready"), sem("gated"), sem("fin_in"), sem("out_sent")

    def apart(eng, signal, value, passed):
        eng.wait_ge(signal, value)
        eng.sem_inc(passed, 1)

    def chained(eng, signal):
        count = [0, 0]

        def link(ins, i=None):
            count[0] += 1
            ins.then_inc(signal, 1)
            eng.wait_ge(signal, plus(count[0], count[1], i))

        def looped(per, turns):
            count[1] = per
            start = count[0]

            def end():
                assert count[0] - start == per, (count[0] - start, per)
                count[0], count[1] = start + per * turns, 0
            return end
        return link, looped

    block = ctx.enter_context(nc.Block())

    @block.sync
    def _(sp):
        def load(u, src, i=None, per=0):
            if not (u < 4 and i is None):
                sp.wait_ge(lo_ready, plus(2 * (u - 3), 2 * per, i))
            sp.dma_start(raw[:, u % 4], src.rearrange("(k p) n -> p k n", p=P)).then_inc(raw_in[u % 4], 16)

        def column_blocks(name, w, first, blocks, c0=0, k_units=4, skip=0):
            with sp.Fori(0, blocks) as j:
                for k in range(k_units):
                    load(UNIT[name] + first + k, w[k * 512:(k + 1) * 512, bass.ds(c0 + j * NW, NW)], j, k_units)

        for k in range(4):
            load(k, a["w_mod"][k * 512:(k + 1) * 512, 0:NW])
        with sp.Fori(1, 8) as j:
            for k in range(4):
                sp.wait_ge(lo_ready, 8 * j + 2 * (k - 3))
                sp.dma_start(raw[:, k], a["w_mod"][k * 512:(k + 1) * 512, bass.ds(j * NW, NW)]
                             .rearrange("(k p) n -> p k n", p=P)).then_inc(raw_in[k], 16)
        column_blocks("ctx", a["w_in"], 0, 4, c0=W1)
        column_blocks("in", a["w_in"], 0, 8)
        with sp.Fori(0, HEADS1) as h:
            for k in range(4):
                load(UNIT["att"] + 2 * k, a["w_in"][k * 512:(k + 1) * 512, bass.ds(2 * D + h * NW, NW)], h, 8)
                load(UNIT["att"] + 2 * k + 1, a["w_mod"][k * 512:(k + 1) * 512, bass.ds(3 * D + h * NW, NW)], h, 8)
        for half, c0 in ((0, 2 * D), (1, 5 * D)):
            with sp.Fori(0, 2) as j:
                for k in range(4):
                    up = (a["w_a_up"], a["w_b_up"])[k // 2]
                    u = UNIT["up"] + 24 * half + 3 * k
                    load(u, up[(k % 2) * 512:(k % 2 + 1) * 512, bass.ds(half * W1 + j * NW, NW)], j, 12)
                    for n in range(2):
                        m = 2 * k + n
                        load(u + 1 + n, a["w_mod"][(m % 4) * 512:(m % 4 + 1) * 512,
                                                   bass.ds(c0 + j * W1 + (m // 4) * NW, NW)], j, 12)
        column_blocks("wo", a["w_o"], 0, 4)
        with sp.Fori(0, 8) as e:
            for n in range(2):
                for k in range(4):
                    load(UNIT["mlp"] + 4 * n + k,
                         a["w_ff1"][k * 512:(k + 1) * 512, bass.ds(e * W1 + n * NW, NW)], e, 16)
            for n in range(4):
                for k in range(2):
                    load(UNIT["mlp"] + 8 + 2 * n + k,
                         a["w_ff2"][bass.ds(e * W1 + k * 512, 512), n * NW:(n + 1) * NW], e, 16)
        column_blocks("a_in", a["a_w_in"], 0, 5)
        column_blocks("a_z", a["a_w_in"], 0, 4, c0=D + 2 * KVG * HD)
        column_blocks("a_out", a["a_w_out"], 0, 4)
        column_blocks("b_att", a["b_w_in"], 0, 8)
        column_blocks("b_z", a["b_w_in"], 0, 4, c0=D + 6 * KVG * HD + B_GATES)
        column_blocks("b_out", a["b_w_out"], 0, 4)
        sp.wait_ge(norm_done, 1)
        sp.dma_start(out.rearrange("(t p) n -> p t n", p=P), rows3).then_inc(out_sent, 16)
        sp.wait_ge(out_sent, 16)

    @block.gpsimd
    def _(pool):
        pool.memset(neghalf[:, :], -0.5).then_inc(half_set, 1)
        pool.dma_start(rows3, a["ctx"].rearrange("(t p) n -> p t n", p=P)).then_inc(rows_in, 16)
        pool.dma_start(res3, a["x"].rearrange("(t p) n -> p t n", p=P)).then_inc(rows_in, 16)
        small = [
            (sel[:, :], a["c_sel"]),
            (vec2[V_NORM1:V_NORM2, :], a["norm_attn_w"].rearrange("(r n) -> r n", n=P)),
            (vec2[V_NORM2:V_NORM_A, :], a["norm_mlp_w"].rearrange("(r n) -> r n", n=P)),
            (vec2[V_NORM_A:V_POOL, :], a["norm_w"].rearrange("l (r n) -> (l r) n", n=P)),
            (vec2[V_POOL:V_SUBLN, :], a["pool_scale"].rearrange("(r n) -> r n", n=P)),
            (vec2[V_SUBLN:V_KPOS, :], a["subln_w"].rearrange("(r n) -> r n", n=P)),
            (vec2[V_KPOS:V_VPOS, :], a["kpos"].rearrange("(l two) d -> l (two d)", two=2)),
            (vec2[V_VPOS:V_END, :], a["vpos"].rearrange("(l two) d -> l (two d)", two=2)),
            (qkw[:, 0, :], a["q_norm_w"].partition_broadcast(P)), (qkw[:, 1, :], a["k_norm_w"].partition_broadcast(P)),
            (rcos, a["c_cos"]), (rsin, a["c_sin"]), (invf[:, 0, :], a["c_invf"]),
            (pos2[:, :], a["positions"].rearrange("(t p) -> p t", p=P)),
            (sinks[:, :], a["sinks"].partition_broadcast(P)),
        ] + [(lamv[:, n, :], a[f"lam{n}"].partition_broadcast(P)) for n in range(4)]
        assert len(small) == SMALL
        for dst, src in small:
            slow = {"allow_slow_non_contiguous": True} if dst.dtype == I32 else {}
            pool.dma_start(dst, src, **slow).then_inc(params_in, 16)
        pool.wait_ge(half_set, 1)

        def root(n, width, i=None, per=0):
            pool.wait_ge(mean_ready, plus(n + 1, per, i))
            pool.tensor_tensor(rstd[:, 0:width], mean[:, 0:width], neghalf[:, 0:width], ALU.pow).then_inc(rstd_ready, 1)

        with pool.Fori(0, 4) as i:
            root(RMS["rows"], 1, i, 1)
        pool.wait_ge(turned, BUILD["x"])
        pool.dma_start(band, a["c_band"]).then_inc(pool_in, 16)
        root(RMS["att1"], 12)
        with pool.Fori(0, HEADS1 - 1) as h:
            root(RMS["att1"] + 1, 1, h, 3)
            root(RMS["att1"] + 2, 12, h, 3)
            root(RMS["att1"] + 3, 1, h, 3)
        root(RMS["att1"] + 22, 1)
        root(RMS["att1"] + 23, 1)
        pool.wait_ge(modcol_taken, 1 + 12)
        pool.dma_start(poolw, a["pool_w"].rearrange("g (c p) n -> p g c n", p=P)).then_inc(pool_in, 16)
        pool.dma_start(ga_b, a["b_mod"][2 * D:3 * D].partition_broadcast(P)).then_inc(bias_in, 16)
        pool.dma_start(gm_b, a["b_mod"][5 * D:6 * D].partition_broadcast(P)).then_inc(bias_in, 16)
        pool.dma_start(tab[:, 0:672], a["c_masks"]).then_inc(masks_in, 16)
        pool.wait_ge(acc_freed, GROUP["wo"])
        pool.dma_start(res3, a["x"].rearrange("(t p) n -> p t n", p=P)).then_inc(x_in, 16)
        root(RMS["mlp"], 2)
        root(RMS["a"], 2)
        root(RMS["b"], 2)
        pool.wait_ge(turned, BUILD["b"] + 8)
        for n, (w1, w2) in enumerate((("kw1", "kw2"), ("vw1", "vw2"))):
            if n:
                pool.wait_ge(hid_ready, n)
            else:
                pool.wait_ge(out2, 2 + 4 * ROUND_B)
            pool.dma_start(w1c, a[w1].rearrange("(k p) n -> p k n", p=P)).then_inc(cmp_w_in, 16)
            pool.dma_start(w2c[:, n], a[w2].rearrange("(k p) n -> p k n", p=P)).then_inc(cmp_w_in, 16)
        pool.wait_ge(gated, 2 * KVG)
        pool.dma_start(fin_w, a["final_norm_w"].partition_broadcast(P)).then_inc(fin_in, 16)
        root(RMS["final"], 2)

    @block.scalar
    def _(act):
        for signal in (head_sq, exp1):
            act.sem_inc(signal, 1)
        link, looped = chained(act, act_chain)

        def split_halves(first, n, i=None, per=0):
            for k, half in ((h // 2, h % 2) for h in range(first, first + n)):
                if k < UNITS:
                    if half == 0:
                        act.wait_ge(raw_in[k % 4], plus(16 * (k // 4 + 1), 4 * per, i))
                    if k >= 2:
                        act.wait_ge(units_used, plus(2 * k - 3 + half, 2 * per, i))
                    on = slice(half * UK // 2, (half + 1) * UK // 2)
                    act.activation(whi[:, k % 2, on], raw[:, k % 4, on], ACT.Copy).then_inc(hi_ready, 1)

        def split(u, n, i=None, per=0):
            split_halves(2 * u, 2 * n, i, per)

        def split_filled(name, n, g):
            before, used = halves_filled(name, n)
            split_halves(2 * UNIT[name] + 4 + before, used, g, 4)

        def group_done(last, i=None, per=0):
            act.wait_ge(units_used, plus(2 * last + 2, 2 * per, i))

        def banks(g):
            return acc[:, 2 * (g % 2):2 * (g % 2) + 2, :]

        def build(g, k, dst, scale=None, shift=None, i=None, per=0):
            bank = turn[:, g % 2, :]
            act.wait_ge(turned, plus(g + 1, per, i))
            out2 = dst[:, k:k + 2, :].rearrange("p k n -> p (k n)")
            if scale is None:
                act.activation(out2, bank, ACT.Copy).then_inc(hi_rounded, 1)
            elif shift is None:
                for n in range(2):
                    ins = act.activation(dst[:, k + n, :], bank[:, n * L:(n + 1) * L], ACT.Copy, scale=scale(k + n))
                ins.then_inc(hi_rounded, 1)
            else:
                if g % 8 >= 2:
                    act.wait_ge(xt_ready, g - 1)
                for n in range(2):
                    ins = act.activation(mtmp[:, g % 2, n * L:(n + 1) * L], bank[:, n * L:(n + 1) * L],
                                         ACT.Identity, scale=scale(k + n), bias=shift(k + n))
                link(ins)
                act.activation(out2, mtmp[:, g % 2, :], ACT.Copy).then_inc(hi_rounded, 1)

        act.dma_start(ident[:, :], a["c_ident"]).then_inc(c_in, 16)
        act.dma_start(vec1[96:112, :], a["c"].rearrange("(r n) -> r n", n=P)).then_inc(c_in, 16)
        act.dma_start(vec1[112:128, :], a["c_ctx"].rearrange("(r n) -> r n", n=P)).then_inc(c_in, 16)
        act.dma_start(vec1[0:96, :], a["b_mod"].rearrange("(r n) -> r n", n=P)).then_inc(c_in, 16)
        act.wait_ge(setup_turned, 1)
        act.activation(cols1[:, :], aux[:, 0, 0:P], ACT.Copy).then_inc(cols_ready, 1)
        act.wait_ge(cols_ready, 1)
        act.activation(silu_c[:, :, :].rearrange("p c k -> p (c k)"), cols1[:, 96:128], ACT.Silu).then_inc(silu_exp, 1)

        split(0, 2)
        u0 = UNIT["mod1"]
        act.wait_ge(rows_in, 32)
        with act.Fori(0, 4) as i:
            act.activation(junk, arena[:, bass.ds(i * D, D)], ACT.Square, accum_out=lam[:, 6:7]).then_inc(sumsq_ready, 1)
            for n in range(2):
                split(u0 + 4 * n + 2, 4, i, 8)
                if n == 0:
                    act.wait_ge(modcol_ready, 1 + i)
                group_done(u0 + 4 * n + 3, i, 8)
                act.activation(modrow1[0:4, n, :], acc[0:4, 2 * n, :], ACT.Copy).then_inc(acc_freed, 1)
        act.wait_ge(setup_turned, 2)
        act.activation(cols2[:, :], aux[:, 0, 0:V_END], ACT.Copy).then_inc(cols_ready, 1)
        act.wait_ge(cond_ready, 1)
        for g in range(8):
            build(BUILD["ctx"] + g, 2 * g, xhi, lambda k: scale_ctx[:, k:k + 1], lambda k: shift_ctx[:, k:k + 1])
        act.wait_ge(lam_sum, 1)
        act.activation(lam[:, 2:4], lam[:, 0:2], ACT.Exp).then_inc(lam_done, 1)
        act.wait_ge(sin_arg, 1)
        act.activation(rops[:, :, :], ang, ACT.Sin)
        act.activation(ropc[:, :, :], angk, ACT.Sin).then_inc(sin_done, 1)
        u0 = UNIT["ctx"]
        with act.Fori(0, 2) as i:
            for n in range(2):
                split(u0 + 4 * n + 2, 4, i, 8)
                group_done(u0 + 4 * n + 3, i, 8)
                act.activation(kv_out[:, i, 2:4, n * NW:(n + 1) * NW], banks(n), ACT.Copy).then_inc(acc_freed, 1)
        for g in range(8):
            build(BUILD["x"] + g, 2 * g, xhi, lambda k: scale_x[:, k:k + 1], lambda k: shift_x[:, k:k + 1])
        u0 = UNIT["in"]
        dst = [qk6[:, 0:2, :], qk6[:, 2:4, :], v1[:, 0:2, :], u_rows]
        for g in range(8):
            split(u0 + 4 * g + 2, 4)
            group_done(u0 + 4 * g + 3)
            if g == 6:
                act.wait_ge(turned, BUILD["heads"])
            act.activation(dst[g // 2][:, :, (g % 2) * NW:(g % 2 + 1) * NW], banks(g), ACT.Copy).then_inc(acc_freed, 1)
        for b in range(4):
            act.wait_ge(pooled, b + 1)
            act.activation(dT[:, 2 * b:2 * b + 2, :].rearrange("p k n -> p (k n)"), turn[:, b % 2, :], ACT.Copy)\
               .then_inc(pooled_copied, 1)
        u0, g0 = UNIT["att"], GROUP["att"]
        with act.Fori(0, HEADS1) as h:
            act.wait_ge(slab_turned, 1 + (h + 1))
            act.activation(slabT, aux_flat[:, 0:768], ACT.Copy).then_inc(slabT_ready, 1)

            def exponentials(t):
                act.wait_ge(max1, plus(t + 1, T, h))
                for c in range(2):
                    ins = act.activation(prob[:, c, :], turn[:, c, :], ACT.Exp, scale=HD ** -0.5,
                                         bias=lam[:, c:c + 1], accum_out=lam[:, 2 + c:3 + c])
                ins.then_inc(exp1, 1)

            def copy_probs(t):
                act.wait_ge(attn_turned, plus(t + 1, T, h))
                act.activation(probT, aux[:, 0, :], ACT.Copy).then_inc(attnT_ready, 1)

            def copy_output(t):
                act.wait_ge(head_out, plus(t + 1, T, h))
                act.activation(orow[:, t, :], aux[:, 1, 0:VD], ACT.Copy).then_inc(head_sq, 1)

            split(u0 + 2, 2, h, 8)
            exponentials(0)
            split(u0 + 4, 2, h, 8)
            copy_probs(0)
            exponentials(1)
            split(u0 + 6, 2, h, 8)
            copy_output(0)
            copy_probs(1)
            split(u0 + 8, 1, h, 8)
            group_done(u0 + 6, h, 8)
            act.activation(gates[:, :, bass.ds(h * NW, NW)], banks(0), ACT.Tanh, scale=0.5).then_inc(acc_freed, 1)
            act.wait_ge(modcol_ready, 1 + plus(4, 1, h))
            group_done(u0 + 7, h, 8)
            act.activation(modrow2[0:4, :], acc[0:4, 2, :], ACT.Copy).then_inc(modrow_ready, 1)
            split(u0 + 9, 1, h, 8)
            copy_output(1)
        for g in range(4):
            build(BUILD["heads"] + g, 2 * g, xhi, lambda k: cols2[:, V_SUBLN:V_SUBLN + 1])
        for g in range(4):
            build(BUILD["pool"] + g, 8 + 2 * g, xhi, lambda k: cols2[:, V_POOL + k - 8:V_POOL + k - 7])
        u0 = UNIT["up"]
        with act.Fori(0, 4) as i:
            split(u0 + 2, 6, i, 12)
            for n in range(2):
                if n == 0:
                    act.wait_ge(modcol_ready, 1 + plus(12, 1, i))
                group_done(u0 + 5 + 6 * n, i, 12)
                act.activation(modrow3[0:4, n, :], turn[0:4, n, :], ACT.Copy).then_inc(modrow_ready, 1)
                split(u0 + 8 + 4 * n, 4 - 2 * n, i, 12)
        for g in range(8):
            build(BUILD["mix"] + g, 2 * g, xhi, lambda k: 0.5)
        with act.Fori(0, 4) as i:
            split(UNIT["wo"] + 2, 4, i, 4)
        for g in range(8):
            build(BUILD["mlp"] + g, 2 * g, xhi, lambda k: scale_x[:, k:k + 1], lambda k: shift_x[:, k:k + 1])
        u0 = UNIT["mlp"]
        with act.Fori(0, 8) as e:
            for n in range(2):
                split(u0 + 4 * n + 2, 4, e, 16)
                group_done(u0 + 4 * n + 3, e, 16)
                act.activation(hid[:, :, n * NW:(n + 1) * NW], banks(n), ACT.Relu).then_inc(acc_freed, 1)
            for g in range(4):
                build(BUILD["hidden"] + g, 2 * g, hhi, i=e, per=4)
            for n in range(4):
                split(u0 + 10 + 2 * n, 2, e, 16)
        for g in range(8):
            build(BUILD["a"] + g, 2 * g, xhi, lambda k: cols2[:, V_NORM_A + k:V_NORM_A + k + 1])
        u0 = UNIT["a_in"]
        with act.Fori(0, 2) as i:
            for n in range(2):
                split(u0 + 4 * n + 2, 4, i, 8)
                group_done(u0 + 4 * n + 3, i, 8)
                act.activation(q2[:, :, bass.ds(i * W1 + n * NW, NW)], banks(n), ACT.Copy, scale=HD ** -0.5)\
                   .then_inc(acc_freed, 1)
        split_halves(2 * (u0 + 18), 8)
        group_done(u0 + 16 + 3)
        act.activation(kv_a, banks(0), ACT.Copy).then_inc(acc_freed, 1)
        def turn_keys(n, dst):
            act.wait_ge(kT_turned, n + 1)
            act.activation(dst, turn_flat[0:HD, :], ACT.Copy).then_inc(kT_ready, 1)

        def queries(n, g, values, name):
            act.wait_ge(q_turned, 1 + (plus(4 * n, 4, g)))
            act.activation(qs, q2[:, :, bass.ds(g * NW, NW)], ACT.Copy).then_inc(qs_ready, 1)
            for b in range(4):
                if b == 2:
                    values()
                act.wait_ge(q_turned, 1 + (plus(4 * n + b + 1, 4, g)))
                act.activation(qT[:, 2 * b:2 * b + 2].rearrange("p h t n -> p (h t n)"), turn[0:HD, b % 2, :], ACT.Copy)\
                   .then_inc(qT_ready, 1)
            split_filled(name, 0, g)

        def exponentials(r, g, per, sm, keys, sink, pairs):
            act.wait_ge(max2, plus(r + 1, per, g))
            for p in pairs:
                for h in (2 * p, 2 * p + 1):
                    x = sm[r % 2][h][:, 0:keys]
                    ins = act.activation(x, x, ACT.Exp, bias=m8[:, r % 2, h:h + 1], accum_out=s8[:, r % 2, h:h + 1])
                ins.then_inc(exp2, 1)
            if sink and 3 in pairs:
                act.wait_ge(sink_arg, plus(r + 1, per, g))
                act.activation(sk[:, r % 2, :], sk[:, r % 2, :], ACT.Exp).then_inc(sink_exp, 1)

        def copy_probs(r, g, per, p, keys):
            act.wait_ge(probs_turned, plus(4 * r + p + 1, 4 * per, g))
            act.wait_ge(out2, 2 + (plus(4 * r + p - 1, 4 * per, g)))
            n, w = min(keys, P), 2 * -(-keys // P) * P
            act.activation(pT[0:n, p % 2, 0:w], turn[0:n, p % 2, 0:w], ACT.Copy).then_inc(probsT_ready[0], 1)

        def rounds(r0, keys, g, sm, name, sink=False):
            per = len(keys)
            for j in range(-1, per):
                if j >= 0:
                    exponentials(r0 + j, g, per, sm, keys[j], sink, (0, 1))
                    copy_probs(r0 + j, g, per, 0, keys[j])
                    exponentials(r0 + j, g, per, sm, keys[j], sink, (2, 3))
                    copy_probs(r0 + j, g, per, 2, keys[j])
                split_filled(name, j + 2, g)

        def gate(u0, g):
            apart(act, units_used, plus(2 * u0 + 8, 8, g), act_passed)
            act.activation(q2[:, :, bass.ds(g * NW, NW)], banks(1), ACT.Tanh, scale=0.5).then_inc(gate_ready, 1)

        turn_keys(0, kTs)
        with act.Fori(0, KVG) as g:
            def values():
                apart(act, out2, 2 + plus(4 * ROUND_A, 8, g), act_passed)
                act.activation(v_g[:, 0], kv_a[:, :, bass.ds(256 + g * HD, HD)], ACT.Copy).then_inc(values_ready, 1)

            queries(0, g, values, "a_z")
            rounds(ROUND_A, KEYS_A, g, sm_a, "a_z", sink=True)
            gate(UNIT["a_z"], g)
        for g in range(8):
            build(BUILD["a_o"] + g, 2 * g, xhi, lambda k: 0.5)
        with act.Fori(0, 4) as i:
            split(UNIT["a_out"] + 2, 4, i, 4)
        for g in range(8):
            build(BUILD["b"] + g, 2 * g, xhi, lambda k: cols2[:, V_NORM_B + k:V_NORM_B + k + 1])
        u0, g0 = UNIT["b_att"], GROUP["b_att"]
        with act.Fori(0, 2) as i:
            for n in range(2):
                split(u0 + 4 * n + 2, 4, i, 8)
                group_done(u0 + 4 * n + 3, i, 8)
                act.activation(q2[:, :, bass.ds(i * W1 + n * NW, NW)], banks(g0 + n), ACT.Copy, scale=HD ** -0.5)\
                   .then_inc(acc_freed, 1)
        for n in range(3):
            split(u0 + 16 + 4 * n + 2, 4)
            group_done(u0 + 16 + 4 * n + 3)
            act.activation(kv6[:, :, n * NW:(n + 1) * NW], banks(g0 + n), ACT.Copy).then_inc(acc_freed, 1)
        split_halves(2 * (u0 + 28 + 2), 8)
        group_done(u0 + 28 + 3)
        act.activation(gate_b[:, :, :], banks(g0 + 3)[:, :, 0:B_GATES], ACT.Sigmoid).then_inc(acc_freed, 1)
        for n in range(2):
            act.wait_ge(cmp_turned, n + 1)
            act.activation(kcT, turn_flat, ACT.Copy).then_inc(cmp_copied, 1)
            act.wait_ge(hid_ready, n + 1)
            act.activation(hx, aux[0:60, 0, 0:256], ACT.Copy).then_inc(gelu_x, 1)
            act.wait_ge(gelu_arg, n + 1)
            act.activation(hy, hy, ACT.Tanh, scale=0.7978845608028654).then_inc(gelu_tanh, 1)
            act.wait_ge(hT_turned, n + 1)
            act.activation(hT, v3(aux[:, 1, 0:120], 60), ACT.Copy).then_inc(hT_ready, 1)
            act.wait_ge(cmp_out, n + 1)
            if n == 0:
                act.activation(cmpk[:, :], aux[0:HD, 0, 0:60], ACT.Copy).then_inc(cmp_stored, 1)
            else:
                act.activation(cmpv, aux[0:NC, 0, 0:256], ACT.Copy).then_inc(cmp_stored, 1)
        turn_keys(1, kTs)
        turn_keys(2, kTw)
        with act.Fori(0, KVG) as g:
            def values():
                apart(act, out2, 2 + plus(4 * ROUND_B, 24, g), act_passed)
                act.activation(cmpk_g, cmpk[:, bass.ds(g * NC, NC)], ACT.Copy)
                act.activation(cmpv_g, cmpv[:, bass.ds(g * HD, HD)], ACT.Copy)
                for n, v0 in enumerate((768, 1280)):
                    ins = act.activation(v_g[:, n], kv6[:, :, bass.ds(v0 + g * HD, HD)], ACT.Copy)
                ins.then_inc(values_ready, 1)

            queries(4, g, values, "b_z")
            rounds(ROUND_B, KEYS_B, g, sm_b, "b_z")
            gate(UNIT["b_z"], g)
        for g in range(8):
            build(BUILD["b_o"] + g, 2 * g, xhi, lambda k: 0.5)
        with act.Fori(0, 3) as i:
            split(UNIT["b_out"] + 2, 4, i, 4)
        split(UNIT["b_out"] + 14, 2)

    @block.vector
    def _(dve):
        for signal, n in ((modcol_taken, 1), (masked2, 4), (out2_taken, 2)):
            dve.sem_inc(signal, n)
        link, looped = chained(dve, dve_chain)
        bc = lambda ap, shape: ap.to_broadcast(shape)

        def split_halves(first, n, i=None, per=0):
            for k, half in ((h // 2, h % 2) for h in range(first, first + n)):
                if k < UNITS:
                    on = slice(half * UK // 2, (half + 1) * UK // 2)
                    dve.wait_ge(hi_ready, plus(2 * k + 1 + half, 2 * per, i))
                    dve.tensor_tensor(wlo[:, k % 2, on], raw[:, k % 4, on], whi[:, k % 2, on].bitcast(F32), ALU.subtract)\
                       .then_inc(lo_ready, 1)

        def split(u, n, i=None, per=0):
            split_halves(2 * u, 2 * n, i, per)

        def split_filled(name, n, g):
            before, used = halves_filled(name, n)
            split_halves(2 * UNIT[name] + 4 + before, used, g, 4)

        def group_done(last, i=None, per=0):
            dve.wait_ge(units_used, plus(2 * last + 2, 2 * per, i))

        def banks(g):
            return acc[:, 2 * (g % 2):2 * (g % 2) + 2, :]

        def build(g, k, hi, lo, scale=None, shift=False, i=None, per=0):
            dve.wait_ge(hi_rounded, plus(g + 1, per, i))
            bank = turn[:, g % 2, :]
            flat = lambda x: x[:, k:k + 2, :].rearrange("p k n -> p (k n)")
            if shift:
                dve.tensor_tensor(flat(lo), mtmp[:, g % 2, :], flat(hi).bitcast(F32), ALU.subtract).then_inc(xt_ready, 1)
            elif scale is None:
                dve.tensor_tensor(flat(lo), bank, flat(hi).bitcast(F32), ALU.subtract).then_inc(xt_ready, 1)
            else:
                for n in range(2):
                    ins = dve.scalar_tensor_tensor(lo[:, k + n, :], bank[:, n * L:(n + 1) * L], scale(k + n),
                                                   hi[:, k + n, :].bitcast(F32), ALU.mult, ALU.subtract)
                ins.then_inc(xt_ready, 1)

        def left_operand_of_conditions():
            sc = silu_c[:, :, :].rearrange("p c k -> p k c")
            dve.memset(cflat[:, 4 * KT:].bitcast(F32), 0.0)
            link(dve.tensor_copy(cvec[:, :, 0:2], sc))
            dve.tensor_tensor(cvec[:, :, 2:4], sc, cvec[:, :, 0:2].bitcast(F32), ALU.subtract).then_inc(modw_ready, 1)

        def rms_rows(n, eps, dst, src, width):
            for t in range(T):
                ins = dve.tensor_tensor_reduce(out=dst[:, t], in0=src[:, t], in1=src[:, t], scale=1.0, scalar=0.0,
                                               op0=ALU.mult, op1=ALU.add, accum_out=mean[:, t:t + 1])
            link(ins)
            dve.tensor_scalar(mean[:, 0:T], mean[:, 0:T], 1.0 / width, eps, ALU.mult, ALU.add).then_inc(mean_ready, 1)
            dve.wait_ge(rstd_ready, n + 1)
            for t in range(T):
                ins = dve.tensor_scalar(dst[:, t], src[:, t], rstd[:, t:t + 1], None, ALU.mult)
            return ins

        dve.wait_ge(silu_exp, 1)
        left_operand_of_conditions()
        split(0, 2)
        u0 = UNIT["mod1"]
        with dve.Fori(0, 4) as i:
            end = looped(0, 4)
            split(u0 + 2, 4, i, 8)
            dve.wait_ge(sumsq_ready, i + 1)
            dve.tensor_scalar(mean[:, 0:1], lam[:, 6:7], 1.0 / D, EPS1, ALU.mult, ALU.add).then_inc(mean_ready, 1)
            split(u0 + 6, 2, i, 8)
            dve.wait_ge(rstd_ready, i + 1)
            part = arena[:, bass.ds(i * D, D)]
            dve.tensor_scalar(part, part, rstd[:, 0:1], None, ALU.mult).then_inc(normed, 1)
            split(u0 + 8, 2, i, 8)
            dve.wait_ge(modcol_ready, 1 + (i + 1))
            dve.tensor_copy(modcol[:, bass.ds(i * 16, 16)], aux[:, 1, 0:16]).then_inc(modcol_taken, 1)
            end()
        mc = modcol[:, :].rearrange("p (s c) -> p c s", c=2)
        dve.wait_ge(modcol_taken, 1 + 4)
        dve.wait_ge(cols_ready, 2)
        for c, (sc, sh) in enumerate(((scale_x, shift_x), (scale_ctx, shift_ctx))):
            link(dve.tensor_tensor(sc[:, :], mc[:, c, 16:32], cols1[:, 16:32], ALU.add))
            ins = dve.scalar_tensor_tensor(sc[:, :], sc[:, :], 1.0, cols2[:, V_NORM1:V_NORM1 + KT], ALU.add, ALU.mult)
            link(ins)
            ins = dve.tensor_tensor(sh[:, :], mc[:, c, 0:16], cols1[:, 0:16], ALU.add)
        ins.then_inc(cond_ready, 1)
        for g in range(8):
            build(BUILD["ctx"] + g, 2 * g, xhi, xlo, shift=True)
        dve.wait_ge(params_in, 16 * SMALL)
        for n in range(2):
            ins = dve.tensor_tensor_reduce(out=junk[:, 0:HD], in0=lamv[:, 2 * n, :], in1=lamv[:, 2 * n + 1, :], scale=1.0,
                                           scalar=0.0, op0=ALU.mult, op1=ALU.add, accum_out=lam[:, n:n + 1])
            link(ins) if n == 0 else ins.then_inc(lam_sum, 1)
        for n in range(2):
            w = qkw[:, n, :].rearrange("p (f two d) -> p f two d", f=2, two=2)
            ws = qkws[:, n, :].rearrange("p (f two d) -> p f two d", f=2, two=2)
            dve.tensor_copy(ws[:, :, 0, :], w[:, :, 1, :])
            link(dve.tensor_copy(ws[:, :, 1, :], w[:, :, 0, :]))
        for n, s0, s1 in ((0, 0, 2), (1, 2, 6)):
            dve.tensor_tensor(cosw[:, s0:s1, :], rcos[:, s0:s1, :], bc(qkw[:, n:n + 1, :], [P, s1 - s0, HD]), ALU.mult)
            dve.tensor_tensor(sinw[:, s0:s1, :], rsin[:, s0:s1, :], bc(qkws[:, n:n + 1, :], [P, s1 - s0, HD]), ALU.mult)
        link(dve.tensor_copy(posf[:, 0, 0:T], pos2[:, :]))
        for t in range(T):
            ins = dve.tensor_scalar(ang[:, t, :], invf[:, 0, :], posf[:, 0, t:t + 1], None, ALU.mult)
        link(ins)
        link(dve.tensor_scalar(angk, ang, 1.0 / (2 * np.pi), None, ALU.mult))
        link(dve.tensor_scalar(angk, angk, 12582912.0, None, ALU.add))
        link(dve.tensor_scalar(angk, angk, -12582912.0, None, ALU.add))
        for part in (6.28125, 0.0019350051879882812, 3.0199159819567e-07):
            link(dve.scalar_tensor_tensor(ang, angk, -part, ang, ALU.mult, ALU.add))
        link(dve.tensor_scalar(ang, ang, 3.1415925, -3.1415925, ALU.min, ALU.max))
        link(dve.tensor_scalar(angk, ang, -1.0, None, ALU.mult))
        link(dve.tensor_tensor(angk, ang, angk, ALU.max))
        dve.tensor_scalar(angk, angk, -1.0, float(np.float32(np.pi / 2)), ALU.mult, ALU.add).then_inc(sin_arg, 1)

        dve.wait_ge(lam_done, 1)
        link(dve.tensor_tensor(lam[:, 4:5], lam[:, 2:3], lam[:, 3:4], ALU.subtract))
        link(dve.tensor_scalar(lam[:, 5:6], lam[:, 4:5], LAM_INIT, None, ALU.add))
        with dve.Fori(0, 4) as i:
            split(UNIT["ctx"] + 2, 4, i, 4)
        for g in range(8):
            build(BUILD["x"] + g, 2 * g, xhi, xlo, shift=True)
        with dve.Fori(0, 8) as i:
            split(UNIT["in"] + 2, 4, i, 4)

        halves = lambda x: x.rearrange("p s (c f two d) -> p s c f two d", c=2, f=2, two=2)
        pairs_of = lambda x: x.rearrange("p s (c d) -> p s c d", c=2)

        def prepare(h, i, root):
            src = qk6[:, :, bass.ds(h * P, P)]
            link(dve.tensor_tensor(slab2, src, src, ALU.mult), i)
            link(dve.tensor_reduce(mean[:, 0:12], slab2.rearrange("p s (c d) -> p (s c) d", c=2), AX.X, ALU.add), i)
            dve.tensor_scalar(mean[:, 0:12], mean[:, 0:12], 1.0 / HD, EPS1, ALU.mult, ALU.add).then_inc(mean_ready, 1)
            dve.wait_ge(rstd_ready, root)
            link(dve.tensor_tensor(pairs_of(slab), pairs_of(src),
                                   bc(rstd[:, 0:12].rearrange("p (s c) -> p s c", c=2).unsqueeze(3), [P, 6, 2, HD]), ALU.mult), i)
            sw = sinw.rearrange("p s (f two d) -> p s f two d", f=2, two=2)
            for c in range(2):
                for two in range(2):
                    ins = dve.tensor_tensor(halves(slab2)[:, :, c, :, two, :], halves(slab)[:, :, c, :, 1 - two, :],
                                            sw[:, :, :, two, :], ALU.mult)
            link(ins, i)
            link(dve.tensor_tensor(pairs_of(slab), pairs_of(slab), bc(cosw.unsqueeze(2), [P, 6, 2, HD]), ALU.mult), i)
            dve.tensor_tensor(slab, slab, slab2, ALU.add).then_inc(slab_ready, 1)

        prepare(0, None, RMS["att1"] + 1)
        u0 = UNIT["att"]

        def head(h, i, last=False):
            def probabilities(t):
                dve.wait_ge(scores1, plus(t + 1, T, h))
                link(dve.tensor_reduce(lam[:, 0:2], turn[:, :, :], AX.X, ALU.max), i)
                dve.tensor_scalar(lam[:, 0:2], lam[:, 0:2], -(HD ** -0.5), None, ALU.mult).then_inc(max1, 1)
                dve.wait_ge(exp1, 1 + (plus(t + 1, T, h)))
                link(dve.reciprocal(s8[:, 0, 0:2], lam[:, 2:4]), i)
                link(dve.tensor_scalar(prob[:, 1, :], prob[:, 1, :], s8[:, 0, 1:2], lam[:, 5:6], ALU.mult, ALU.mult), i)
                dve.scalar_tensor_tensor(prob[:, 0, :], prob[:, 0, :], s8[:, 0, 0:1], prob[:, 1, :], ALU.mult, ALU.subtract)\
                   .then_inc(attn1, 1)

            def output(t):
                root = RMS["att1"] + (2 if t == 0 else 3 if last else 4)
                dve.wait_ge(head_sq, 1 + (plus(t + 1, T, h)))
                link(dve.tensor_tensor_reduce(out=osq, in0=orow[:, t, :], in1=orow[:, t, :], scale=1.0, scalar=0.0, op0=ALU.mult,
                                              op1=ALU.add, accum_out=mean[:, 0:1]), i)
                dve.tensor_scalar(mean[:, 0:1], mean[:, 0:1], 1.0 / VD, EPS1, ALU.mult, ALU.add).then_inc(mean_ready, 1)
                dve.wait_ge(rstd_ready, plus(root, 3, h))
                ins = dve.tensor_scalar(heads[:, t, bass.ds(h * VD, VD)], orow[:, t, :], rstd[:, 0:1], 1.0 - LAM_INIT,
                                        ALU.mult, ALU.mult)
                if t == 0:
                    link(ins, i)
                else:
                    ins.then_inc(head_done, 1)

            split(u0 + 2, 2, h, 8)
            probabilities(0)
            split(u0 + 4, 2, h, 8)
            probabilities(1)
            split(u0 + 6, 2, h, 8)
            output(0)
            dve.wait_ge(attn_turned, plus(2, T, h))
            if not last:
                prepare(h + 1, i, plus(RMS["att1"] + 3, 3, h))
            split(u0 + 8, 2, h, 8)
            output(1)
            dve.wait_ge(modcol_ready, 1 + plus(5, 1, h))
            dve.tensor_copy(modcol[:, bass.ds(h * 8, 8)], acc[:, 3, 0:8]).then_inc(modcol_taken, 1)

        with dve.Fori(0, HEADS1 - 1) as h:
            end = looped(14, HEADS1 - 1)
            head(h, h)
            end()
        head(HEADS1 - 1, None, last=True)
        for g in range(4):
            build(BUILD["heads"] + g, 2 * g, xhi, xlo, lambda k: cols2[:, V_SUBLN:V_SUBLN + 1])
        for g in range(4):
            build(BUILD["pool"] + g, 8 + 2 * g, xhi, xlo, lambda k: cols2[:, V_POOL + k - 8:V_POOL + k - 7])
        dve.wait_ge(modcol_taken, 1 + 12)
        link(dve.tensor_tensor(scale_x[:, :], mc[:, 0, 16:32], cols1[:, 64:80], ALU.add))
        link(dve.scalar_tensor_tensor(scale_x[:, :], scale_x[:, :], 1.0, cols2[:, V_NORM2:V_NORM2 + KT], ALU.add, ALU.mult))
        dve.tensor_tensor(shift_x[:, :], mc[:, 0, 0:16], cols1[:, 48:64], ALU.add).then_inc(cond_ready, 1)

        dve.wait_ge(bias_in, 32)
        for half, gate in enumerate((ga_b, gm_b)):
            u0 = UNIT["up"] + 24 * half
            with dve.Fori(0, 2) as i:
                end = looped(1, 2)
                split(u0 + 2, 10, i, 12)
                group_done(u0 + 9, i, 12)
                cols = bass.ds(half * W1 + i * NW, NW)
                for n, (dst, g) in enumerate(((upa, cols), (upb, bass.ds(D + half * W1 + i * NW, NW)))):
                    for t in range(T):
                        ins = dve.scalar_tensor_tensor(dst[:, t, :], gates[:, t, g], 1.0, acc[:, 2 * n + t, :], ALU.add, ALU.mult)
                    ins.then_inc(acc_freed, 1) if n == 0 else link(ins, i)
                dve.tensor_tensor(rows3[:, :, cols], upa, upb, ALU.add).then_inc(acc_freed, 1)
                split(u0 + 12, 2, i, 12)
                dve.wait_ge(modcol_ready, 1 + plus(13 + 2 * half, 1, i))
                part = gate[:, bass.ds(i * W1, W1)]
                dve.tensor_tensor(part, aux_flat, part, ALU.add).then_inc(modcol_taken, 1)
                end()
        for g in range(8):
            build(BUILD["mix"] + g, 2 * g, xhi, xlo, lambda k: 0.5)
        dve.wait_ge(x_in, 16)
        u0, g0 = UNIT["wo"], GROUP["wo"]
        with dve.Fori(0, 2) as i:
            end = looped(2, 2)
            for n in range(2):
                split(u0 + 4 * n + 2, 4, i, 8)
                group_done(u0 + 4 * n + 3, i, 8)
                cols = bass.ds(i * W1 + n * NW, NW)
                link(dve.tensor_tensor(mtmp, banks(n), bc(ga_b[:, cols].unsqueeze(1), [P, T, NW]), ALU.mult), i)
                dve.tensor_tensor(res3[:, :, cols], res3[:, :, cols], mtmp, ALU.add).then_inc(acc_freed, 1)
            end()
        dve.wait_ge(acc_freed, GROUP["mlp"])
        rms_rows(RMS["mlp"], EPS1, rows3, res3, D).then_inc(normed, 1)
        for g in range(8):
            build(BUILD["mlp"] + g, 2 * g, xhi, xlo, shift=True)
        dve.wait_ge(xt_ready, BUILD["hidden"])
        link(dve.memset(yacc, 0.0))
        u0, g0 = UNIT["mlp"], GROUP["mlp"]
        with dve.Fori(0, 8) as e:
            for n in range(2):
                split(u0 + 4 * n + 2, 4, e, 16)
                dve.wait_ge(acc_freed, plus(g0 + n + 1, 6, e))
                part = hid[:, :, n * NW:(n + 1) * NW]
                dve.tensor_tensor(part, part, part, ALU.mult).then_inc(squared, 1)
            for g in range(4):
                build(BUILD["hidden"] + g, 2 * g, hhi, hlo, i=e, per=4)
            for n in range(4):
                split(u0 + 10 + 2 * n, 2, e, 16)
                group_done(u0 + 9 + 2 * n, e, 16)
                part = yacc[:, :, n * NW:(n + 1) * NW]
                dve.tensor_tensor(part, banks(n), part, ALU.add).then_inc(acc_freed, 1)
        dve.wait_ge(acc_freed, GROUP["a_in"])
        link(dve.tensor_tensor(yacc, yacc, bc(gm_b.unsqueeze(1), [P, T, D]), ALU.mult))
        link(dve.tensor_tensor(res3, res3, yacc, ALU.add))

        rms_rows(RMS["a"], EPS2, rows3, res3, D).then_inc(normed, 1)
        for g in range(8):
            build(BUILD["a"] + g, 2 * g, xhi, xlo, lambda k: cols2[:, V_NORM_A + k:V_NORM_A + k + 1])
        with dve.Fori(0, 4) as i:
            split(UNIT["a_in"] + 2, 4, i, 4)
        split_halves(2 * (UNIT["a_in"] + 18), 8)
        dve.wait_ge(acc_freed, GROUP["a_z"])

        def rotate(x, n_heads):
            x1, x2 = x[:, :, :, 0:ROT], x[:, :, :, ROT:2 * ROT]
            shape = [P, T, n_heads, ROT]
            cos, sin = (bc(w[:, :, :].unsqueeze(2), shape) for w in (ropc, rops))
            tmp = [r[:, 0:T * n_heads * ROT].rearrange("p (t h d) -> p t h d", t=T, d=ROT) for r in rope_t]
            for dst, src, w in ((tmp[0], x1, cos), (tmp[1], x2, sin), (tmp[2], x2, cos), (tmp[3], x1, sin)):
                ins = dve.tensor_tensor(dst, src, w, ALU.mult)
            link(ins)
            dve.tensor_tensor(x1, tmp[0], tmp[1], ALU.subtract)
            ins = dve.tensor_tensor(x2, tmp[2], tmp[3], ALU.add)
            return ins

        heads_of = lambda x, n: x.rearrange("p t (h d) -> p t h d", h=n)
        link(rotate(heads_of(q2, 32), 32))
        rotate(heads_of(kv_a[:, :, 0:256], KVG), KVG).then_inc(roped, 1)

        def maxima(r, g, per, sm, keys, mask, pairs):
            for p in pairs:
                apart(dve, scores2, plus(4 * r + p + 1, 4 * per, g), dve_passed)
                for h in (2 * p, 2 * p + 1):
                    ins = dve.tensor_tensor_reduce(out=sm[r % 2][h][:, 0:keys], in0=acc[:, p % 2, (h % 2) * L:(h % 2) * L + keys],
                                                   in1=mask, scale=1.0, scalar=3 * NEG, op0=ALU.add, op1=ALU.max,
                                                   accum_out=m8[:, r % 2, h:h + 1])
                ins.then_inc(masked2, 1)

        def less_maxima(r, g, per, sink, any_key):
            top = m8[:, r % 2, :]
            dve.wait_ge(masked2, 4 + plus(4 * r + 4, 4 * per, g))
            if sink:
                link(dve.tensor_tensor(top, top, sinks[:, bass.ds(g * HG, HG)], ALU.max), g)
            if any_key is not None:
                link(dve.tensor_scalar(top, top, any_key, None, ALU.mult), g)
            dve.tensor_scalar(top, top, -1.0, None, ALU.mult).then_inc(max2, 1)
            if sink:
                dve.wait_ge(max2, plus(r + 1, per, g))
                dve.tensor_tensor(sk[:, r % 2, :], top, sinks[:, bass.ds(g * HG, HG)], ALU.add).then_inc(sink_arg, 1)

        def copy_probs(r, g, per, p, keys):
            dve.wait_ge(probs_turned, plus(4 * r + p + 1, 4 * per, g))
            dve.wait_ge(out2, 2 + (plus(4 * r + p - 1, 4 * per, g)))
            n, w = min(keys, P), 2 * -(-keys // P) * P
            dve.tensor_copy(pT[0:n, p % 2, 0:w], turn[0:n, p % 2, 0:w]).then_inc(probsT_ready[1], 1)

        def outputs(r, g, per, t, sink, any_key, gate):
            total = s8[:, r % 2, :]
            dve.wait_ge(exp2, plus(4 * r + 4, 4 * per, g))
            if sink:
                dve.wait_ge(sink_exp, plus(r + 1, per, g))
                link(dve.tensor_tensor(total, total, sk[:, r % 2, :], ALU.add), g)
            if any_key is not None:
                link(dve.tensor_scalar(total, total, 1.0e-30, None, ALU.max), g)
            link(dve.reciprocal(total, total), g)
            if gate is not None:
                link(dve.tensor_tensor(total, total, gate_b[:, t, bass.ds(gate * 32 + g * HG, HG)], ALU.mult), g)
            dve.wait_ge(out2, 2 + (plus(4 * r + 4, 4 * per, g)))
            o = aux[:, r % 2, :].rearrange("p (h d) -> p h d", h=HG)
            dst = rows3[:, t, bass.ds(g * NW, NW)]
            w = bc(total.unsqueeze(2), [P, HG, HD])
            if not gate:
                dve.tensor_tensor(dst.rearrange("p (h d) -> p h d", h=HG), o, w, ALU.mult).then_inc(out2_taken, 1)
            else:
                dve.tensor_tensor(otmp.rearrange("p (h d) -> p h d", h=HG), o, w, ALU.mult).then_inc(out2_taken, 1)
                dve.wait_ge(out2_taken, 2 + plus(r + 1, per, g))
                link(dve.tensor_tensor(dst, dst, otmp, ALU.add), g)

        def rounds(r0, kinds, g, sm, name, sink=False):
            per = len(kinds)
            split_filled(name, 0, g)
            for j in range(-1, per):
                if j + 1 < per:
                    keys, mask, _, any_key, _ = kinds[j + 1]
                    maxima(r0 + j + 1, g, per, sm, keys, mask, (0, 1))
                if j >= 0:
                    copy_probs(r0 + j, g, per, 1, kinds[j][0])
                if j + 1 < per:
                    maxima(r0 + j + 1, g, per, sm, keys, mask, (2, 3))
                    less_maxima(r0 + j + 1, g, per, sink, any_key)
                if j >= 0:
                    keys, _, t, any_key, gate = kinds[j]
                    copy_probs(r0 + j, g, per, 3, keys)
                    outputs(r0 + j, g, per, t, sink, any_key, gate)
                split_filled(name, j + 2, g)
            cols = bass.ds(g * NW, NW)
            dve.wait_ge(gate_ready, plus(GATES_BEFORE[name] + 1, 1, g))
            dve.scalar_tensor_tensor(q2[:, :, cols], q2[:, :, cols], 1.0, banks(1), ALU.add, ALU.mult).then_inc(acc_freed, 1)
            dve.wait_ge(acc_freed, plus(GROUP[name] + 1, 1, g))
            dve.wait_ge(out2_taken, 2 + plus(r0 + per, per, g))
            dve.tensor_tensor(rows3[:, :, cols], rows3[:, :, cols], q2[:, :, cols], ALU.mult).then_inc(gated, 1)

        dve.wait_ge(masks_in, 16)
        with dve.Fori(0, KVG) as g:
            end = looped(6, KVG)
            rounds(ROUND_A, [(P, causal[:, 0:P], 0, None, None), (L, windowed, 1, None, None)], g, sm_a, "a_z",
                   sink=True)
            end()
        for g in range(8):
            build(BUILD["a_o"] + g, 2 * g, xhi, xlo, lambda k: 0.5)

        def residual(name, turns):
            u0, g0 = UNIT[name], GROUP[name]
            with dve.Fori(0, turns) as i:
                for n in range(2):
                    split(u0 + 4 * n + 2, 4, i, 8)
                    group_done(u0 + 4 * n + 3, i, 8)
                    part = res3[:, :, bass.ds(i * W1 + n * NW, NW)]
                    dve.tensor_tensor(part, banks(g0 + n), part, ALU.add).then_inc(acc_freed, 1)

        residual("a_out", 2)
        dve.wait_ge(acc_freed, GROUP["b_att"])
        rms_rows(RMS["b"], EPS2, rows3, res3, D).then_inc(normed, 1)
        for g in range(8):
            build(BUILD["b"] + g, 2 * g, xhi, xlo, lambda k: cols2[:, V_NORM_B + k:V_NORM_B + k + 1])
        with dve.Fori(0, 7) as i:
            split(UNIT["b_att"] + 2, 4, i, 4)
        split_halves(2 * (UNIT["b_att"] + 30), 8)
        dve.wait_ge(acc_freed, GROUP["b_z"])
        link(rotate(heads_of(q2, 32), 32))
        link(rotate(heads_of(kv6[:, :, 512:768], KVG), KVG))
        rotate(heads_of(kv6[:, :, 1024:1280], KVG), KVG).then_inc(roped, 1)
        for n in range(2):
            if n:
                dve.wait_ge(cmp_turned, n)
            src = kv6[:, :, n * 256:(n + 1) * 256].rearrange("p t (g d) -> p t g d", g=KVG)
            dve.tensor_copy(kdup[:, :, :, 0:HD], src)
            dve.tensor_copy(kdup[:, :, :, HD:P], src).then_inc(dup_ready, 1)
            dve.wait_ge(cmp_copied, n + 1)
            pos = cols2[:, V_KPOS + 16 * n:V_KPOS + 16 * n + 16]
            for half in range(2):
                on = slice(half * HD, (half + 1) * HD)
                kc = kcT[on, :].rearrange("p (g c m two) -> p two m g c", g=KVG, c=16, two=2)[:, half]
                for l in range(2):
                    ins = dve.tensor_tensor(blkT[on, 8 * l:8 * l + 8], kc[:, :, :, l:l + NC],
                                            bc(pos[on, 8 * l:8 * l + 8].unsqueeze(2).unsqueeze(3), [HD, 8, KVG, NC]), ALU.add)
            ins.then_inc(blk_ready, 1)
            dve.wait_ge(gelu_x, n + 1)
            link(dve.tensor_tensor(hy, hx, hx, ALU.mult))
            link(dve.tensor_scalar(hy, hy, 0.044715, 1.0, ALU.mult, ALU.add))
            dve.tensor_tensor(hy, hy, hx, ALU.mult).then_inc(gelu_arg, 1)
            dve.wait_ge(gelu_tanh, n + 1)
            link(dve.tensor_scalar(hy, hy, 0.5, 0.5, ALU.mult, ALU.add))
            dve.tensor_tensor(hz, hx, hy, ALU.mult).then_inc(gelu_done, 1)
        with dve.Fori(0, KVG) as g:
            end = looped(20, KVG)
            kinds = []
            for t in range(T):
                mask = causal[:, 0:P] if t == 0 else causal[:, P:3 * P]
                kinds += [(NC, cmp_mask[:, NC * t:NC * t + NC], t, cmp_any[:, t:t + 1], 0),
                          ((t + 1) * P, mask, t, None, 1), ((t + 1) * P, mask, t, None, 2)]
            rounds(ROUND_B, kinds, g, sm_b, "b_z")
            end()
        for g in range(8):
            build(BUILD["b_o"] + g, 2 * g, xhi, xlo, lambda k: 0.5)
        residual("b_out", 1)
        u0, g0 = UNIT["b_out"], GROUP["b_out"]
        for n in (2, 3):
            split(u0 + 4 * n + 2, 4)
            group_done(u0 + 4 * n + 3)
            part = res3[:, :, n * NW:(n + 1) * NW]
            dve.tensor_tensor(part, banks(g0 + n), part, ALU.add).then_inc(acc_freed, 1)
        dve.wait_ge(acc_freed, g0 + 4)
        link(rms_rows(RMS["final"], EPS2, rows3, res3, D))
        dve.wait_ge(fin_in, 16)
        dve.tensor_tensor(rows3, rows3, bc(fin_w.unsqueeze(1), [P, T, D]), ALU.mult).then_inc(norm_done, 1)

    @block.tensor
    def _(pe):
        for signal, n in ((modcol_ready, 1), (slab_turned, 1), (out2, 2), (q_turned, 1)):
            pe.sem_inc(signal, n)
        def multiply(u, k, k_units, bank0, k_first=0, hi=xhi, lo=xlo, i=None, per=0, width=NW, tiles=range(UK)):
            for kk in tiles:
                if kk % 2 == 0:
                    pe.wait_ge(lo_ready, plus(2 * u + 1 + kk // 2, 2 * per, i))
                kt = k_first + UK * k + kk
                w_hi, w_lo = whi[:, u % 2, kk, 0:width], wlo[:, u % 2, kk, 0:width]
                for t in range(T):
                    bank = acc[:, bank0 + t, 0:width]
                    tok = slice(t * P, (t + 1) * P)
                    pe.matmul(bank, hi[:, kt, tok], w_hi, start=kt == k_first, stop=False, skip_group_check=True)
                    pe.matmul(bank, hi[:, kt, tok], w_lo, start=False, stop=False, skip_group_check=True)
                    mm = pe.matmul(bank, lo[:, kt, tok], w_hi, start=False, stop=kt == k_first + UK * k_units - 1,
                                   skip_group_check=True)
                if kk % 2 == 1:
                    mm.then_inc(units_used, 1)

        def product(u0, g, k_units, k_first=0, hi=xhi, lo=xlo, built=None, i=None, per=0, g_count=0, g_per=0, width=NW):
            if g_count >= 2:
                pe.wait_ge(acc_freed, plus(g_count - 1, g_per, i))
            for k in range(k_units):
                if built is not None:
                    built(k)
                multiply(u0 + k, k, k_units, 2 * (g % 2), k_first, hi, lo, i, per, width)

        def condition(u, k, bank, i, per):
            for kk in range(UK):
                if kk % 2 == 0:
                    pe.wait_ge(lo_ready, plus(2 * u + 1 + kk // 2, 2 * per, i))
                kt = UK * k + kk
                left = cflat[:, 4 * kt:4 * kt + P]
                pe.matmul(bank, left, whi[:, u % 2, kk], start=kt == 0, stop=False, skip_group_check=True)
                mm = pe.matmul(bank, left, wlo[:, u % 2, kk], start=False, stop=kt == KT - 1, skip_group_check=True)
                if kk % 2 == 1:
                    mm.then_inc(units_used, 1)

        def condition_columns():
            for n in range(2):
                for s in range(4):
                    o = 2 * (4 * n + s)
                    mm = pe.matmul(aux[:, 1, o:o + 2], modrow1[0:4, n, s * P:(s + 1) * P], sel[0:4, P:P + 2],
                                   start=True, stop=True)
            mm.then_inc(modcol_ready, 1)

        def turn_rows(name, src, pairs=8, i=None, per=0, ready=None):
            for g in range(pairs):
                n = BUILD[name] + g
                if ready is not None:
                    ready(g)
                if n >= 2:
                    pe.wait_ge(xt_ready, plus(n - 1, per, i))
                for k in range(2):
                    for t in range(T):
                        mm = pe.transpose(turn[:, n % 2, k * L + t * P:k * L + (t + 1) * P],
                                          src[:, t, (2 * g + k) * P:(2 * g + k + 1) * P], ident[:, :])
                mm.then_inc(turned, 1)

        def built(name, i=None, per=0):
            return lambda k: pe.wait_ge(xt_ready, plus(BUILD[name] + 2 * k + 2, per, i))

        def groups(name, turns, first=0, build=None, i_width=2):
            with pe.Fori(0, turns) as i:
                for n in range(2):
                    product(UNIT[name] + 4 * (first + n), GROUP[name] + first + n, 4, built=built(build), i=i, per=8,
                            g_count=GROUP[name] + first + n, g_per=2)

        pe.wait_ge(c_in, 64)
        pe.transpose(aux[:, 0, 0:P], vec1, ident[:, :]).then_inc(setup_turned, 1)
        pe.wait_ge(modw_ready, 1)
        with pe.Fori(0, 4) as i:
            for n in range(2):
                for k in range(4):
                    condition(UNIT["mod1"] + 4 * n + k, k, acc[:, 2 * n, :], i, 8)
            pe.wait_ge(acc_freed, plus(2, 2, i))
            pe.wait_ge(modcol_taken, 1 + i)
            pe.wait_ge(params_in, 16 * SMALL)
            condition_columns()
        pe.transpose(aux[:, 0, 0:V_END], vec2[0:V_END, :], ident[0:V_END, 0:V_END]).then_inc(setup_turned, 1)
        pe.wait_ge(normed, 4)
        turn_rows("ctx", rows3)
        groups("ctx", 2, build="ctx")
        turn_rows("x", res3)
        groups("in", 4, build="x")
        pe.wait_ge(pool_in, 16)
        pe.wait_ge(acc_freed, GROUP["att"])
        for b in range(4):
            if b >= 2:
                pe.wait_ge(pooled_copied, b - 1)
            for n in range(2):
                s = 2 * b + n
                for t in range(T):
                    mm = pe.matmul(turn[:, b % 2, n * L:(n + 1) * L], u_rows[:, t, s * P:(s + 1) * P], band[:, t, s // 2, :],
                                   start=t == 0, stop=t == T - 1)
            mm.then_inc(pooled, 1)
        pe.wait_ge(pooled_copied, 4)
        u0, g0 = UNIT["att"], GROUP["att"]
        with pe.Fori(0, HEADS1) as h:
            def fill(k):
                if k == 0:
                    pe.wait_ge(acc_freed, plus(g0, 1, h))
                multiply(u0 + 2 * k, k, 4, 0, i=h, per=8)
                condition(u0 + 2 * k + 1, k, acc[:, 2, :], h, 8)

            def scores(t):
                pe.wait_ge(exp1, 1 + (plus(t, T, h)))
                for c in range(2):
                    on = slice(c * HD, (c + 1) * HD)
                    mm = pe.matmul(turn[:, c, :], slabT[on, t * P:(t + 1) * P], slabT[on, 256:768], start=True, stop=True)
                mm.then_inc(scores1, 1)

            def turn_probs(t):
                pe.wait_ge(attn1, plus(t + 1, T, h))
                for k in range(4):
                    mm = pe.transpose(aux[:, 0, k * P:(k + 1) * P], prob[:, 0, k * P:(k + 1) * P], ident[:, :])
                mm.then_inc(attn_turned, 1)

            def output(t):
                pe.wait_ge(attnT_ready, plus(t + 1, T, h))
                pe.wait_ge(head_sq, 1 + plus(t, T, h))
                for k in range(4):
                    mm = pe.matmul(aux[:, 1, 0:VD], probT[:, k * P:(k + 1) * P], v1[:, k, bass.ds(h * VD, VD)],
                                   start=k == 0, stop=k == 3)
                mm.then_inc(head_out, 1)

            pe.wait_ge(slab_ready, h + 1)
            pe.wait_ge(head_sq, 1 + (2 * h))
            for s in range(6):
                mm = pe.transpose(aux_flat[:, s * P:(s + 1) * P], slab[:, s, :], ident[:, :])
            mm.then_inc(slab_turned, 1)
            fill(0)
            pe.wait_ge(slabT_ready, h + 1)
            scores(0)
            fill(1)
            turn_probs(0)
            scores(1)
            fill(2)
            output(0)
            turn_probs(1)
            fill(3)
            output(1)
            pe.wait_ge(modrow_ready, h + 1)
            pe.wait_ge(modcol_taken, 1 + plus(4, 1, h))
            for s in range(4):
                mm = pe.matmul(acc[:, 3, 2 * s:2 * s + 2], modrow2[0:4, s * P:(s + 1) * P], sel[0:4, P:P + 2],
                               start=True, stop=True)
            mm.then_inc(modcol_ready, 1)
        pe.wait_ge(head_done, HEADS1)
        turn_rows("heads", heads, pairs=4)
        pe.wait_ge(pool_in, 32)
        for g in range(4):
            n = BUILD["pool"] + g
            pe.wait_ge(xt_ready, n - 1)
            for d in range(2):
                for c in range(2):
                    mm = pe.matmul(turn[:, n % 2, d * L:(d + 1) * L], poolw[:, g, c, d * P:(d + 1) * P],
                                   dT[:, 2 * g + c, :], start=c == 0, stop=c == 1)
            mm.then_inc(turned, 1)
        pe.wait_ge(xt_ready, BUILD["mix"])
        pe.wait_ge(acc_freed, GROUP["up"])
        u0, g0 = UNIT["up"], GROUP["up"]
        with pe.Fori(0, 4) as i:
            for k in range(4):
                if k % 2 == 0:
                    pe.wait_ge(acc_freed, plus(g0 + k // 2 - 1, 2, i))
                multiply(u0 + 3 * k, k % 2, 2, 2 * (k // 2), 8 * (k // 2), i=i, per=12)
                for n in range(2):
                    m = 2 * k + n
                    if m % 4 == 0:
                        pe.wait_ge(modrow_ready, plus(8 + m // 4 - 1, 2, i))
                    condition(u0 + 3 * k + 1 + n, m % 4, turn[:, m // 4, :], i, 12)
            pe.wait_ge(modrow_ready, plus(8 + 2, 2, i))
            pe.wait_ge(modcol_taken, 1 + plus(12, 1, i))
            for n in range(2):
                mm = pe.matmul(aux[:, n, :], sel[0:4, 0:P], modrow3[0:4, n, :], start=True, stop=True)
            mm.then_inc(modcol_ready, 1)
        pe.wait_ge(acc_freed, GROUP["wo"])
        turn_rows("mix", rows3)
        groups("wo", 2, build="mix")
        pe.wait_ge(cond_ready, 2)
        pe.wait_ge(normed, 5)
        turn_rows("mlp", rows3)
        u0, g0 = UNIT["mlp"], GROUP["mlp"]
        with pe.Fori(0, 8) as e:
            for n in range(2):
                product(u0 + 4 * n, n, 4, built=built("mlp"), i=e, per=16, g_count=g0 + n, g_per=6)
            turn_rows("hidden", hid, pairs=4, i=e, per=4,
                      ready=lambda g: pe.wait_ge(squared, plus(g // 2 + 1, 2, e)))
            for n in range(4):
                product(u0 + 8 + 2 * n, n, 2, 0, hhi, hlo, built("hidden", e, 4), e, 16, g0 + 2 + n, 6)
        pe.wait_ge(normed, 6)
        turn_rows("a", rows3)
        groups("a_in", 2, build="a")
        u0, g0 = UNIT["a_in"], GROUP["a_in"]
        product(u0 + 16, 0, 4, built=built("a"), g_count=g0 + 4)

        def turn_keys(keys, n):
            for g in range(KVG):
                for t in range(T):
                    mm = pe.transpose(turn_flat[0:HD, g * L + t * P:g * L + (t + 1) * P], keys[:, t, g * HD:(g + 1) * HD],
                                      ident[:, :])
            mm.then_inc(kT_turned, 1)
            pe.wait_ge(kT_ready, n + 1)

        def queries(n, g, fill):
            apart(pe, qs_ready, plus(n + 1, 1, g), pe_passed)
            for b in range(4):
                if b >= 2:
                    fill(0, b - 2)
                    apart(pe, qT_ready, plus(4 * n + b - 1, 4, g), pe_passed)
                for h in range(2):
                    for t in range(T):
                        o = (2 * h + t) * P
                        hh = 2 * b + h
                        mm = pe.transpose(turn[0:HD, b % 2, o:o + P], qs[:, t, hh * HD:(hh + 1) * HD], ident[:, :])
                mm.then_inc(q_turned, 1)
            fill(0, 2)
            pe.wait_ge(qT_ready, plus(4 * n + 4, 4, g))

        def scores(r, g, per, p, kind):
            keys, t, kT, _ = kind
            apart(pe, masked2, 4 + plus(4 * r + p - 1, 4 * per, g), pe_passed)
            for h in range(2):
                mm = pe.matmul(acc[:, p % 2, h * L:h * L + keys], qT[:, 2 * p + h, t, :], kT, start=True, stop=True)
            mm.then_inc(scores2, 1)

        def turn_probs(r, g, per, p, kind, sm):
            kt, n = -(-kind[0] // P), min(kind[0], P)
            pe.wait_ge(exp2, plus(4 * r + p + 1, 4 * per, g))
            for h in range(2):
                for k in range(kt):
                    o = (h * kt + k) * P
                    mm = pe.transpose(turn[0:n, p % 2, o:o + P], sm[r % 2][2 * p + h][:, k * P:k * P + n], ident[:, :])
            mm.then_inc(probs_turned, 1)

        def outputs(r, g, per, p, kind):
            keys, _, _, v_of = kind
            kt, n = -(-keys // P), min(keys, P)
            apart(pe, probsT_ready[p % 2], plus(2 * r + p // 2 + 1, 2 * per, g), pe_passed)
            for h in range(2):
                for k in range(kt):
                    o = (h * kt + k) * P
                    hh = 2 * p + h
                    mm = pe.matmul(aux[:, r % 2, hh * HD:(hh + 1) * HD], pT[0:n, p % 2, o:o + P], v_of(k),
                                   start=k == 0, stop=k == kt - 1)
            mm.then_inc(out2, 1)

        def rounds(r0, kinds, g, sm, fill):
            per = len(kinds)
            for j in range(-1, per):
                ahead = lambda p: scores(r0 + j + 1, g, per, p, kinds[j + 1]) if j + 1 < per else None
                turn_pair = lambda p: turn_probs(r0 + j, g, per, p, kinds[j], sm) if j >= 0 else None
                output = lambda p: outputs(r0 + j, g, per, p, kinds[j]) if j >= 0 else None
                ahead(0)
                ahead(1)
                fill(j + 2, 0)
                if j >= 0:
                    pe.wait_ge(out2_taken, 2 + plus(r0 + j - 1, per, g))
                turn_pair(0)
                turn_pair(1)
                fill(j + 2, 1)
                output(0)
                ahead(2)
                turn_pair(2)
                fill(j + 2, 2)
                output(1)
                ahead(3)
                turn_pair(3)
                fill(j + 2, 3)
                output(2)
                output(3)

        def filler(name, g):
            done = [0]

            def fill(part, n):
                for _ in range(FILLS[name][part][n]):
                    k, kk = divmod(done[0], UK)
                    done[0] += 1
                    if k == 0 and kk == 0:
                        pe.wait_ge(acc_freed, plus(GROUP[name], 1, g))
                    multiply(UNIT[name] + k, k, 4, 2, i=g, per=4, tiles=(kk,))
            return fill

        pe.wait_ge(roped, 1)
        turn_keys(kv_a, 0)
        with pe.Fori(0, KVG) as g:
            fill = filler("a_z", g)
            queries(0, g, fill)
            pe.wait_ge(values_ready, g + 1)
            v_of = lambda k: v_g[:, 0, k]
            rounds(ROUND_A, [(n * P, n - 1, kTs[:, bass.ds(g * L, n * P)], v_of) for n in (1, 2)], g, sm_a,
                   fill)
        pe.wait_ge(gated, KVG)
        turn_rows("a_o", rows3)
        groups("a_out", 2, build="a_o")
        pe.wait_ge(normed, 7)
        turn_rows("b", rows3)
        groups("b_att", 2, build="b")
        u0, g0 = UNIT["b_att"], GROUP["b_att"]
        for n in range(4):
            product(u0 + 16 + 4 * n, g0 + n, 4, built=built("b"), g_count=g0 + 4 + n, width=NW if n < 3 else B_GATES)
        for n in range(2):
            pe.wait_ge(dup_ready, n + 1)
            pe.wait_ge(xt_ready, BUILD["b_o"])
            for g in range(KVG):
                for t in range(T):
                    mm = pe.transpose(turn_flat[:, g * L + t * P:g * L + (t + 1) * P], kdup[:, t, g, :], ident[:, :])
            mm.then_inc(cmp_turned, 1)
            pe.wait_ge(blk_ready, n + 1)
            pe.wait_ge(cmp_w_in, 32 * (n + 1))
            for l in range(16):
                mm = pe.matmul(aux[0:60, 0, 0:256], blkT[:, l].rearrange("p g c -> p (g c)"), w1c[:, l, :],
                               start=l == 0, stop=l == 15)
            mm.then_inc(hid_ready, 1)
            pe.wait_ge(gelu_done, n + 1)
            for k in range(2):
                mm = pe.transpose(aux[:, 1, k * 60:(k + 1) * 60], hz[:, k * P:(k + 1) * P], ident[0:60, 0:60])
            mm.then_inc(hT_turned, 1)
            pe.wait_ge(hT_ready, n + 1)
            if n == 0:
                for k in range(2):
                    mm = pe.matmul(aux[0:HD, 0, 0:60], w2c[:, 0, k, :], hT[:, k, :], start=k == 0, stop=k == 1)
            else:
                for g in range(KVG):
                    for k in range(2):
                        mm = pe.matmul(aux[0:NC, 0, g * HD:(g + 1) * HD], hT[:, k, g * NC:(g + 1) * NC], w2c[:, 1, k, :],
                                       start=k == 0, stop=k == 1)
            mm.then_inc(cmp_out, 1)
            pe.wait_ge(cmp_stored, n + 1)
        pe.wait_ge(roped, 2)
        turn_keys(kv6[:, :, 512:768], 1)
        turn_keys(kv6[:, :, 1024:1280], 2)
        with pe.Fori(0, KVG) as g:
            fill = filler("b_z", g)
            queries(4, g, fill)
            pe.wait_ge(values_ready, g + (KVG + 1))
            v_of = [lambda k, n=n: v_g[:, n, k] for n in range(2)]
            kinds = []
            for t in range(T):
                kinds.append((NC, t, cmpk_g, lambda k: cmpv_g))
                kinds += [((t + 1) * P, t, kT[:, bass.ds(g * L, (t + 1) * P)], v) for kT, v in zip((kTs, kTw), v_of)]
            rounds(ROUND_B, kinds, g, sm_b, fill)
        pe.wait_ge(gated, 2 * KVG)
        turn_rows("b_o", rows3)
        groups("b_out", 2, build="b_o")

    ctx.close()


def shape_constants():
    f = np.float32
    sel = np.zeros((4, P + 2), f)
    sel[0, 0:P] = sel[2, 0:P] = 1
    for c in range(2):
        sel[c, P + c] = sel[2 + c, P + c] = 1
    band = np.zeros((L, 4, L), f)
    for g, w in enumerate((2, 4, 8, 16)):
        for t in range(L):
            lo, hi = max(t - w // 2, 0), min(t + w - w // 2, L)
            band[lo:hi, g, t] = 1.0 / (hi - lo)
            band[t, g, t] -= 1
    band = band.reshape(T, P, 4, L).transpose(1, 0, 2, 3)
    half = HD // 2
    inv = (f(10000.0) ** (-np.arange(0, half, 2, dtype=f) / f(half))).astype(f)
    tok = np.arange(L)
    cos, sin = np.ones((6, P, HD), f), np.zeros((6, P, HD), f)
    for n, pos in enumerate((tok // 64, tok % 64)):
        ang = pos.astype(f)[:, None] * inv[None, :]
        c, s = np.cos(ang).reshape(T, P, 16), np.sin(ang).reshape(T, P, 16)
        for tiles in (slice(0, 2), slice(2, 4)):
            cos[tiles, :, n * 32:n * 32 + 16] = cos[tiles, :, n * 32 + 16:n * 32 + 32] = c
            sin[tiles, :, n * 32:n * 32 + 16], sin[tiles, :, n * 32 + 16:n * 32 + 32] = -s, s
    invf = (500000.0 ** (-np.arange(0, 16, 2) / 16.0)).astype(f)
    p = np.arange(P)
    masks = np.zeros((P, 672), f)
    k1, k2 = np.arange(P), np.arange(L)
    masks[:, 0:128] = np.where(k1[None] <= p[:, None], 0, NEG)
    q = P + p[:, None]
    masks[:, 128:384] = np.where(k2[None] <= q, 0, NEG)
    masks[:, 384:640] = np.where((k2[None] <= q) & (q - k2[None] < 128), 0, NEG)
    for t in range(T):
        valid = 16 * np.arange(NC)[None] + 31 <= (t * P + p)[:, None]
        masks[:, 640 + NC * t:640 + NC * t + NC] = np.where(valid, 0, NEG)
        masks[:, 670 + t] = valid.any(1)
    return {"c_ident": np.eye(P, dtype=f), "c_sel": sel, "c_band": np.ascontiguousarray(band),
            "c_cos": np.ascontiguousarray(cos.transpose(1, 0, 2)), "c_sin": np.ascontiguousarray(sin.transpose(1, 0, 2)),
            "c_invf": np.ascontiguousarray(np.broadcast_to(invf, (P, ROT))), "c_masks": masks}


NAMES = {
    "x": "x", "c": "c", "ctx": "ctx", "c_ctx": "c_ctx", "w_mod": "w_mod", "b_mod": "b_mod", "norm_attn_w": "norm_attn_w",
    "w_in": "w_in", "q_norm_w": "q_norm_w", "k_norm_w": "k_norm_w", "lam0": "lambda_q1", "lam1": "lambda_k1",
    "lam2": "lambda_q2", "lam3": "lambda_k2", "subln_w": "subln_w", "pool_w": "pool_w", "pool_scale": "pool_scale",
    "w_a_up": "w_a_up", "w_b_up": "w_b_up", "w_o": "w_o", "norm_mlp_w": "norm_mlp_w", "w_ff1": "w_ff1", "w_ff2": "w_ff2",
    "positions": "positions_2", "norm_w": "norm_w_2", "final_norm_w": "final_norm_w_2", "a_w_in": "a_w_in_2",
    "sinks": "a_sinks_2", "a_w_out": "a_w_out_2", "b_w_in": "b_w_in_2", "kpos": "b_cmp_k_pos_2", "kw1": "b_cmp_k_w1_2",
    "kw2": "b_cmp_k_w2_2", "vpos": "b_cmp_v_pos_2", "vw1": "b_cmp_v_w1_2", "vw2": "b_cmp_v_w2_2", "b_w_out": "b_w_out_2",
}


def kernel(**inputs):
    import concourse.bacc as bacc
    from concourse.bass_utils import run_bass_kernel_spmd

    nc = bacc.Bacc("TRN2", target_bir_lowering=False, num_devices=1)
    arrays = {}
    for name, given in NAMES.items():
        x = np.ascontiguousarray(inputs[given])
        if name not in ("norm_w", "c_ctx", "final_norm_w") and x.ndim > 1 and x.shape[0] == 1:
            x = x[0]
        arrays[name] = x
    arrays.update(shape_constants())
    aps = {n: nc.dram_tensor(f"in_{n}", x.shape, mybir.dt.from_np(x.dtype), kind="ExternalInput").ap()
           for n, x in arrays.items()}
    out = nc.dram_tensor("out_y", (L, D), F32, kind="ExternalOutput").ap()
    dit_kernel(nc, aps, out)
    r = run_bass_kernel_spmd(nc, [{f"in_{n}": x for n, x in arrays.items()}], core_ids=[0])
    return r.results[0]["out_y"].reshape(1, L, D)
```

```python
from contextlib import ExitStack

import concourse.bass as bass
import concourse.mybir as mybir
import numpy as np

F32, F32R, I32 = mybir.dt.float32, mybir.dt.float32r, mybir.dt.int32
ACT = mybir.ActivationFunctionType
ALU = mybir.AluOpType
AX = mybir.AxisListType

P = 128
D = 2048
KT = D // P
NW = 512
UK = 4
L = 256
T = L // P
HEADS1, VD = 8, 128
W1 = 1024
EPS1, EPS2 = 1e-6, 1e-5
LAM_INIT = 0.8 - 0.6
HD = 64
KVG = 4
HG = 8
NC = 15
NEG = -1.0e30
B_GATES = 96
ROT = 8

PHASES = [("mod1", 32, 8), ("ctx", 16, 4), ("in", 32, 8), ("att", 64, 8), ("up", 48, 8), ("wo", 16, 4),
          ("mlp", 128, 48), ("a_in", 20, 5), ("a_z", 16, 4), ("a_out", 16, 4), ("b_att", 32, 8), ("b_z", 16, 4),
          ("b_out", 16, 4)]
UNIT, GROUP = {}, {}
UNITS = _g = 0
for _name, _nu, _ng in PHASES:
    UNIT[_name], GROUP[_name] = UNITS, _g
    UNITS, _g = UNITS + _nu, _g + _ng

BUILDS = [("ctx", 8), ("x", 8), ("heads", 4), ("pool", 4), ("mix", 8), ("mlp", 8), ("hidden", 32),
          ("a", 8), ("a_o", 8), ("b", 8), ("b_o", 8)]
BUILD = {}
_b = 0
for _name, _nb in BUILDS:
    BUILD[_name] = _b
    _b += _nb

RMS = {"rows": 0, "att1": 4, "mlp": 28, "a": 29, "b": 30, "final": 31}
ROUND_A, ROUND_B = 0, 8
FILLS = {"a_z": ((1, 1, 2), (2, 0, 0, 2), (1, 1, 1, 1), (1, 1, 1, 1)),
         "b_z": ((1, 1, 1), (0, 0, 0, 1)) + 6 * ((1, 1, 0, 0),)}
GATES_BEFORE = {"a_z": 0, "b_z": KVG}
SMALL = 19
KEYS_A = (P, 2 * P)
KEYS_B = (NC, P, P, NC, 2 * P, 2 * P)
V_NORM1, V_NORM2, V_NORM_A, V_NORM_B, V_POOL, V_SUBLN, V_KPOS, V_VPOS, V_END = 0, 16, 32, 48, 64, 72, 73, 89, 105


STEPS = {0: ("turn", 0), 2: ("hidden", 0), 4: ("turn_hidden", 0), 5: ("out", 0), 6: ("turn", 1), 8: ("hidden", 1),
         10: ("turn_hidden", 1), 11: ("out", 1), 12: ("keys", 1), 14: ("keys", 2)}


def halves_filled(name, n):
    tiles = [sum(part) for part in FILLS[name]]
    before = sum(tiles[:n]) // 2
    return before, sum(tiles[:n + 1]) // 2 - before


def plus(base, step, i):
    return base if i is None else base + step * i


def dit_kernel(nc, a, out):
    ctx = ExitStack()
    sb = lambda n, s, d=F32: ctx.enter_context(nc.sbuf_tensor(n, s, d))
    sem = lambda n: ctx.enter_context(nc.semaphore(n))
    v3 = lambda ap, n: ap.rearrange("p (t n) -> p t n", n=n)

    raw = sb("raw", [P, 4, UK, NW])
    whi = sb("whi", [P, 2, UK, NW], F32R)
    wlo = sb("wlo", [P, 2, UK, NW], F32R)
    xhi = sb("xhi", [P, KT, L], F32R)
    xlo = sb("xlo", [P, KT, L], F32R)
    with nc.sbuf_tensor("hhi", [P, 8, L], F32R) as hhi, nc.sbuf_tensor("hlo", [P, 8, L], F32R) as hlo:
        pass
    qkv = sb("qkv", [P, 10240])
    with nc.sbuf_tensor("front", [P, 8192], F32), nc.sbuf_tensor("ghi", [P, KT, L], F32R) as ghi, \
            nc.sbuf_tensor("glo", [P, KT, L], F32R) as glo:
        pass
    arena = sb("arena", [P, 16384])
    res, rows, big = arena[:, 0:4096], arena[:, 4096:8192], arena[:, 8192:16384]
    res3, rows3 = v3(res, D), v3(rows, D)
    ident = sb("ident", [P, P])
    cols1 = sb("cols1", [P, P])
    cols2 = sb("cols2", [P, V_END])
    modcol = sb("modcol", [P, 64])
    scale_x, shift_x = sb("scale_x", [P, KT]), sb("shift_x", [P, KT])
    sel = sb("sel", [4, P + 2])
    tab = sb("tab", [P, 768])
    sinks = sb("sinks", [P, 32])
    silu_c = sb("silu_c", [P, 2, KT])
    mean, rstd, neghalf = sb("mean", [P, 12]), sb("rstd", [P, 12]), sb("neghalf", [P, 12])
    lam = sb("lam", [P, 8])
    m8, s8 = sb("m8", [P, 2, 8]), sb("s8", [P, 2, 8])
    ropc, rops = sb("ropc", [P, T, ROT]), sb("rops", [P, T, ROT])
    gate_b = sb("gate_b", [P, T, B_GATES])
    cmpk = sb("cmpk", [HD, KVG * NC])
    pos2 = sb("pos2", [P, T], I32)

    modrow1 = v3(big[:, 0:1024], NW)
    mtmp = v3(big[:, 1024:2048], NW)
    vec1, vec2 = big[:, 2048:2176], big[:, 2176:2304]
    lamv = v3(big[:, 2304:2560], HD)
    qkw = v3(big[:, 2560:2688], HD)
    qkws = v3(big[:, 2688:2816], HD)
    rcos, rsin = v3(big[:, 2816:3200], HD), v3(big[:, 3200:3584], HD)
    posf, ang, angk, invf = (v3(big[:, 3584 + 16 * n:3600 + 16 * n], ROT) for n in range(4))
    scale_ctx, shift_ctx = big[:, 3648:3664], big[:, 3664:3680]
    junk = big[:, 4096:6144]
    qk6 = v3(qkv[:, 0:6144], W1)
    kv_out = qkv[:, 2048:10240].rearrange("p (w t n) -> p w t n", w=2, t=4)
    v1 = v3(qkv[:, 6144:10240], W1)
    gates = v3(big, 2 * D)
    u_rows = v3(res[:, 0:2048], W1)
    dT = v3(res[:, 2048:4096], L)
    cflat = sb("cflat", [P, 4 * KT + P - 4], F32R)
    cvec = cflat[:, 0:4 * KT].rearrange("p (k c) -> p k c", c=4)
    band = rows[:, 2048:4096].rearrange("p (s g n) -> p s g n", s=2, g=4)
    poolw = rows[:, 2048:4096].rearrange("p (g c n) -> p g c n", g=4, c=2)
    cosw, sinw = v3(tab[:, 0:384], HD), v3(tab[:, 384:768], HD)
    heads = v3(res[:, 0:2048], W1)
    prob = v3(rows[:, 0:1024], NW)
    probT = rows[:, 1792:2304]
    slab2 = v3(rows[:, 0:768], P)
    slab = v3(rows[:, 1024:1792], P)
    slabT = rows[:, 2304:3072]
    orow, osq = v3(rows[:, 3840:4096], VD), rows[:, 3200:3328]
    modrow2 = rows[:, 3328:3840]
    upa, upb = v3(res[:, 0:1024], NW), v3(res[:, 1024:2048], NW)
    yacc = v3(big[:, 0:4096], D)
    ga_b, gm_b = qkv[:, 4096:6144], qkv[:, 6144:8192]
    modrow3 = v3(qkv[:, 8192:9216], NW)
    hid = v3(rows[:, 0:2048], W1)
    q2, z2 = v3(big[:, 0:4096], D), v3(big[:, 4096:8192], D)
    kv_a = v3(qkv[:, 0:1024], NW)
    kv6 = v3(qkv[:, 0:3072], 1536)
    qs = v3(qkv[:, 3072:4096], NW)
    qT = qkv[0:HD, 4096:6144].rearrange("p (h t n) -> p h t n", h=HG, t=T)
    sm = v3(qkv[:, 6144:8192], L)
    pT = v3(qkv[:, 8192:9216], NW)
    kTs = qkv[0:HD, 9216:10240]
    kTw = z2[0:HD, 0, 0:1024]
    kdup = z2[:, 0, 1024:2048].rearrange("p (t g n) -> p t g n", t=T, g=KVG)
    kcT = z2[:, 1, 0:1024]
    cmpv = z2[0:NC, 1, 0:256]
    cmpk_g, cmpv_g = cols1[0:HD, 0:NC], modcol[0:NC, :]
    v_g = z2[:, 1, 256:512].rearrange("p (w t n) -> p w t n", w=2, t=T)
    blkT = z2[:, 1, 1024:1984].rearrange("p (l g c) -> p l g c", l=16, g=KVG)
    w1c = v3(rows, 256)
    w2c = qkv[:, 8192:8448].rearrange("p (w k n) -> p w k n", w=2, k=2)
    hx, hy, hz = sm[0:60, 0, :], sm[0:60, 1, :], sm[0:60, 2, :]
    hT = v3(qkv[:, 6144 + 768:6144 + 888], 60)
    rope_t = [qkv[:, 8448 + 128 * n:8448 + 128 * (n + 1)] for n in range(4)]
    causal, windowed = tab[:, 0:384], tab[:, 384:640]
    cmp_mask, cmp_any = tab[:, 640:670], tab[:, 670:672]
    sk = silu_c[:, :, 0:8]
    norm, norm_q, norm_half = (silu_c[:, 0, 8 + T * n:8 + T * n + T] for n in range(3))
    sm2 = v3(qkv[:, 1024:3072], L)
    sm_a = [[x[:, h, :] for h in range(HG)] for x in (sm, sm2)]
    sm3 = v3(z2[:, 0, 1024:2048], L), v3(z2[:, 1, 1024:2048], L)
    sm_b = [sm_a[0], [sm3[h // 4][:, h % 4, :] for h in range(HG)]]
    otmp = z2[:, 1, 512:1024]
    fin_w = big[:, 0:2048]

    acc = ctx.enter_context(nc.psum_tensor("acc", [P, 4, NW], F32))
    turn = ctx.enter_context(nc.psum_tensor("turn", [P, 2, NW], F32))
    aux = ctx.enter_context(nc.psum_tensor("aux", [P, 2, NW], F32))
    aux_flat = aux[:, :, :].rearrange("p b n -> p (b n)")
    turn_flat = turn[:, :, :].rearrange("p b n -> p (b n)")

    raw_in = [sem(f"raw_in{i}") for i in range(4)]
    hi_ready, lo_ready = sem("hi_ready"), sem("lo_ready")
    units_used = sem("units_used")
    acc_freed = sem("acc_freed")
    turned = sem("turned")
    hi_rounded, xt_ready = sem("hi_rounded"), sem("xt_ready")
    act_chain, dve_chain = sem("act_chain"), sem("dve_chain")
    params_in, setup_turned, cols_ready = sem("params_in"), sem("setup_turned"), sem("cols_ready")
    silu_exp, modw_ready = sem("silu_exp"), sem("modw_ready")
    sumsq_ready, mean_ready, rstd_ready = sem("sumsq_ready"), sem("mean_ready"), sem("rstd_ready")
    normed = sem("normed")
    modcol_ready, modcol_taken = sem("modcol_ready"), sem("modcol_taken")
    modrow_ready, bias_in, c_in, rows_in = sem("modrow_ready"), sem("bias_in"), sem("c_in"), sem("rows_in")
    cond_ready, lam_done, sin_arg, sin_done = sem("cond_ready"), sem("lam_done"), sem("sin_arg"), sem("sin_done")
    pe_passed, act_passed, dve_passed, pool_passed = (sem(n) for n in ("pe_passed", "act_passed", "dve_passed", "pool_passed"))
    lam_sum, half_set = sem("lam_sum"), sem("half_set")
    pool_in, pooled, pooled_copied = sem("pool_in"), sem("pooled"), sem("pooled_copied")
    slab_ready, slab_turned, slabT_ready = sem("slab_ready"), sem("slab_turned"), sem("slabT_ready")
    scores1, max1, exp1, attn1 = sem("scores1"), sem("max1"), sem("exp1"), sem("attn1")
    attn_turned, attnT_ready, head_out, head_done = sem("attn_turned"), sem("attnT_ready"), sem("head_out"), sem("head_done")
    head_sq = sem("head_sq")
    x_in, squared, res_done, norm_ready, norm_done = (sem(n) for n in ("x_in", "squared", "res_done", "norm_ready", "norm_done"))
    masks_in, roped, kT_turned, kT_ready = sem("masks_in"), sem("roped"), sem("kT_turned"), sem("kT_ready")
    qs_ready, q_turned, qT_ready = sem("qs_ready"), sem("q_turned"), sem("qT_ready")
    scores2, masked2, max2, exp2, sink_arg, sink_exp = (sem(n) for n in ("scores2", "masked2", "max2", "exp2", "sink_arg", "sink_exp"))
    probs_turned, out2, out2_taken = (sem(n) for n in ("probs_turned", "out2", "out2_taken"))
    probsT_ready = sem("probsT_act"), sem("probsT_dve")
    cmp_w_in, dup_ready, cmp_turned, cmp_copied, blk_ready, hid_ready = (sem(n) for n in (
        "cmp_w_in", "dup_ready", "cmp_turned", "cmp_copied", "blk_ready", "hid_ready"))
    gelu_x, gelu_arg, gelu_tanh, gelu_done, hT_turned, hT_ready, cmp_out, cmp_stored = (sem(n) for n in (
        "gelu_x", "gelu_arg", "gelu_tanh", "gelu_done", "hT_turned", "hT_ready", "cmp_out", "cmp_stored"))
    gate_ready, values_ready, gated, fin_in, out_sent = sem("gate_ready"), sem("values_ready"), sem("gated"), sem("fin_in"), sem("out_sent")

    def apart(eng, signal, value, passed):
        eng.wait_ge(signal, value)
        eng.sem_inc(passed, 1)

    def chained(eng, signal):
        count = [0, 0]

        def link(ins, i=None):
            count[0] += 1
            ins.then_inc(signal, 1)
            eng.wait_ge(signal, plus(count[0], count[1], i))

        def looped(per, turns):
            count[1] = per
            start = count[0]

            def end():
                assert count[0] - start == per, (count[0] - start, per)
                count[0], count[1] = start + per * turns, 0
            return end
        return link, looped

    block = ctx.enter_context(nc.Block())

    @block.sync
    def _(sp):
        def load(u, src, i=None, per=0):
            if not (u < 4 and i is None):
                sp.wait_ge(lo_ready, plus(2 * (u - 3), 2 * per, i))
            sp.dma_start(raw[:, u % 4], src.rearrange("(k p) n -> p k n", p=P)).then_inc(raw_in[u % 4], 16)

        def column_blocks(name, w, first, blocks, c0=0, k_units=4, skip=0):
            with sp.Fori(0, blocks) as j:
                for k in range(k_units):
                    load(UNIT[name] + first + k, w[k * 512:(k + 1) * 512, bass.ds(c0 + j * NW, NW)], j, k_units)

        for k in range(4):
            load(k, a["w_mod"][k * 512:(k + 1) * 512, 0:NW])
        with sp.Fori(1, 8) as j:
            for k in range(4):
                sp.wait_ge(lo_ready, 8 * j + 2 * (k - 3))
                sp.dma_start(raw[:, k], a["w_mod"][k * 512:(k + 1) * 512, bass.ds(j * NW, NW)]
                             .rearrange("(k p) n -> p k n", p=P)).then_inc(raw_in[k], 16)
        column_blocks("ctx", a["w_in"], 0, 4, c0=W1)
        column_blocks("in", a["w_in"], 0, 8)
        with sp.Fori(0, HEADS1) as h:
            for k in range(4):
                load(UNIT["att"] + 2 * k, a["w_in"][k * 512:(k + 1) * 512, bass.ds(2 * D + h * NW, NW)], h, 8)
                load(UNIT["att"] + 2 * k + 1, a["w_mod"][k * 512:(k + 1) * 512, bass.ds(3 * D + h * NW, NW)], h, 8)
        for half, c0 in ((0, 2 * D), (1, 5 * D)):
            with sp.Fori(0, 2) as j:
                for k in range(4):
                    up = (a["w_a_up"], a["w_b_up"])[k // 2]
                    u = UNIT["up"] + 24 * half + 3 * k
                    load(u, up[(k % 2) * 512:(k % 2 + 1) * 512, bass.ds(half * W1 + j * NW, NW)], j, 12)
                    for n in range(2):
                        m = 2 * k + n
                        load(u + 1 + n, a["w_mod"][(m % 4) * 512:(m % 4 + 1) * 512,
                                                   bass.ds(c0 + j * W1 + (m // 4) * NW, NW)], j, 12)
        column_blocks("wo", a["w_o"], 0, 4)
        with sp.Fori(0, 8) as e:
            for n in range(2):
                for k in range(4):
                    load(UNIT["mlp"] + 4 * n + k,
                         a["w_ff1"][k * 512:(k + 1) * 512, bass.ds(e * W1 + n * NW, NW)], e, 16)
            for n in range(4):
                for k in range(2):
                    load(UNIT["mlp"] + 8 + 2 * n + k,
                         a["w_ff2"][bass.ds(e * W1 + k * 512, 512), n * NW:(n + 1) * NW], e, 16)
        column_blocks("a_in", a["a_w_in"], 0, 5)
        column_blocks("a_z", a["a_w_in"], 0, 4, c0=D + 2 * KVG * HD)
        column_blocks("a_out", a["a_w_out"], 0, 4)
        column_blocks("b_att", a["b_w_in"], 0, 4, c0=D)
        column_blocks("b_att", a["b_w_in"], 16, 4)
        column_blocks("b_z", a["b_w_in"], 0, 4, c0=D + 6 * KVG * HD + B_GATES)
        column_blocks("b_out", a["b_w_out"], 0, 4)
        sp.wait_ge(norm_done, 1)
        sp.dma_start(out.rearrange("(t p) n -> p t n", p=P), rows3).then_inc(out_sent, 16)
        sp.wait_ge(out_sent, 16)

    @block.gpsimd
    def _(pool):
        pool.memset(neghalf[:, :], -0.5).then_inc(half_set, 1)
        pool.dma_start(rows3, a["ctx"].rearrange("(t p) n -> p t n", p=P)).then_inc(rows_in, 16)
        pool.dma_start(res3, a["x"].rearrange("(t p) n -> p t n", p=P)).then_inc(rows_in, 16)
        small = [
            (sel[:, :], a["c_sel"]),
            (vec2[V_NORM1:V_NORM2, :], a["norm_attn_w"].rearrange("(r n) -> r n", n=P)),
            (vec2[V_NORM2:V_NORM_A, :], a["norm_mlp_w"].rearrange("(r n) -> r n", n=P)),
            (vec2[V_NORM_A:V_POOL, :], a["norm_w"].rearrange("l (r n) -> (l r) n", n=P)),
            (vec2[V_POOL:V_SUBLN, :], a["pool_scale"].rearrange("(r n) -> r n", n=P)),
            (vec2[V_SUBLN:V_KPOS, :], a["subln_w"].rearrange("(r n) -> r n", n=P)),
            (vec2[V_KPOS:V_VPOS, :], a["kpos"].rearrange("(l two) d -> l (two d)", two=2)),
            (vec2[V_VPOS:V_END, :], a["vpos"].rearrange("(l two) d -> l (two d)", two=2)),
            (qkw[:, 0, :], a["q_norm_w"].partition_broadcast(P)), (qkw[:, 1, :], a["k_norm_w"].partition_broadcast(P)),
            (rcos, a["c_cos"]), (rsin, a["c_sin"]), (invf[:, 0, :], a["c_invf"]),
            (pos2[:, :], a["positions"].rearrange("(t p) -> p t", p=P)),
            (sinks[:, :], a["sinks"].partition_broadcast(P)),
        ] + [(lamv[:, n, :], a[f"lam{n}"].partition_broadcast(P)) for n in range(4)]
        assert len(small) == SMALL
        for dst, src in small:
            slow = {"allow_slow_non_contiguous": True} if dst.dtype == I32 else {}
            pool.dma_start(dst, src, **slow).then_inc(params_in, 16)
        pool.wait_ge(half_set, 1)

        def root(n, width, i=None, per=0):
            pool.wait_ge(mean_ready, plus(n + 1, per, i))
            pool.tensor_tensor(rstd[:, 0:width], mean[:, 0:width], neghalf[:, 0:width], ALU.pow).then_inc(rstd_ready, 1)

        with pool.Fori(0, 4) as i:
            root(RMS["rows"], 1, i, 1)
        pool.wait_ge(turned, BUILD["x"])
        pool.dma_start(band, a["c_band"]).then_inc(pool_in, 16)
        root(RMS["att1"], 12)
        with pool.Fori(0, HEADS1 - 1) as h:
            root(RMS["att1"] + 1, 1, h, 3)
            root(RMS["att1"] + 2, 12, h, 3)
            root(RMS["att1"] + 3, 1, h, 3)
        root(RMS["att1"] + 22, 1)
        root(RMS["att1"] + 23, 1)
        pool.wait_ge(modcol_taken, 1 + 12)
        pool.dma_start(poolw, a["pool_w"].rearrange("g (c p) n -> p g c n", p=P)).then_inc(pool_in, 16)
        pool.dma_start(ga_b, a["b_mod"][2 * D:3 * D].partition_broadcast(P)).then_inc(bias_in, 16)
        pool.dma_start(gm_b, a["b_mod"][5 * D:6 * D].partition_broadcast(P)).then_inc(bias_in, 16)
        pool.dma_start(tab[:, 0:672], a["c_masks"]).then_inc(masks_in, 16)
        pool.wait_ge(acc_freed, GROUP["wo"])
        pool.dma_start(res3, a["x"].rearrange("(t p) n -> p t n", p=P)).then_inc(x_in, 16)
        root(RMS["mlp"], 2)
        root(RMS["a"], 2)

        def queries(n, g):
            apart(pool, q_turned, 1 + plus(4 * n, 4, g), pool_passed)
            pool.tensor_copy(qs, q2[:, :, bass.ds(g * NW, NW)]).then_inc(qs_ready, 1)

        pool.wait_ge(roped, 1)
        with pool.Fori(0, KVG) as g:
            queries(0, g)
            apart(pool, out2, 2 + plus(4 * ROUND_A, 8, g), pool_passed)
            pool.tensor_copy(v_g[:, 0], kv_a[:, :, bass.ds(256 + g * HD, HD)]).then_inc(values_ready, 1)
        root(RMS["b"], 2)
        pool.wait_ge(turned, BUILD["b"] + 8)
        for n, (w1, w2) in enumerate((("kw1", "kw2"), ("vw1", "vw2"))):
            if n:
                pool.wait_ge(hid_ready, n)
            else:
                pool.wait_ge(out2, 2 + 4 * ROUND_B)
            pool.dma_start(w1c, a[w1].rearrange("(k p) n -> p k n", p=P)).then_inc(cmp_w_in, 16)
            pool.dma_start(w2c[:, n], a[w2].rearrange("(k p) n -> p k n", p=P)).then_inc(cmp_w_in, 16)
        pool.wait_ge(roped, 3)
        pool.wait_ge(cmp_stored, 2)
        with pool.Fori(0, KVG) as g:
            queries(4, g)
            apart(pool, out2, 2 + plus(4 * ROUND_B, 24, g), pool_passed)
            pool.tensor_copy(cmpk_g, cmpk[:, bass.ds(g * NC, NC)])
            pool.tensor_copy(cmpv_g, cmpv[:, bass.ds(g * HD, HD)])
            for n, v0 in enumerate((768, 1280)):
                ins = pool.tensor_copy(v_g[:, n], kv6[:, :, bass.ds(v0 + g * HD, HD)])
            ins.then_inc(values_ready, 1)
        pool.wait_ge(gated, 2 * KVG)
        pool.dma_start(fin_w, a["final_norm_w"].partition_broadcast(P)).then_inc(fin_in, 16)
        root(RMS["final"], 2)

    @block.scalar
    def _(act):
        for signal in (head_sq, exp1):
            act.sem_inc(signal, 1)
        link, looped = chained(act, act_chain)

        def split_halves(first, n, i=None, per=0):
            for k, half in ((h // 2, h % 2) for h in range(first, first + n)):
                if k < UNITS:
                    if half == 0:
                        act.wait_ge(raw_in[k % 4], plus(16 * (k // 4 + 1), 4 * per, i))
                    if k >= 2:
                        act.wait_ge(units_used, plus(2 * k - 3 + half, 2 * per, i))
                    on = slice(half * UK // 2, (half + 1) * UK // 2)
                    act.activation(whi[:, k % 2, on], raw[:, k % 4, on], ACT.Copy).then_inc(hi_ready, 1)

        def split(u, n, i=None, per=0):
            split_halves(2 * u, 2 * n, i, per)

        def split_filled(name, n, g):
            before, used = halves_filled(name, n)
            split_halves(2 * UNIT[name] + 4 + before, used, g, 4)

        def group_done(last, i=None, per=0):
            act.wait_ge(units_used, plus(2 * last + 2, 2 * per, i))

        def banks(g):
            return acc[:, 2 * (g % 2):2 * (g % 2) + 2, :]

        def build(g, k, dst, scale=None, shift=None, i=None, per=0):
            bank = turn[:, g % 2, :]
            act.wait_ge(turned, plus(g + 1, per, i))
            out2 = dst[:, k:k + 2, :].rearrange("p k n -> p (k n)")
            if scale is None:
                act.activation(out2, bank, ACT.Copy).then_inc(hi_rounded, 1)
            elif shift is None:
                for n in range(2):
                    ins = act.activation(dst[:, k + n, :], bank[:, n * L:(n + 1) * L], ACT.Copy, scale=scale(k + n))
                ins.then_inc(hi_rounded, 1)
            else:
                if g % 8 >= 2:
                    act.wait_ge(xt_ready, g - 1)
                for n in range(2):
                    ins = act.activation(mtmp[:, g % 2, n * L:(n + 1) * L], bank[:, n * L:(n + 1) * L],
                                         ACT.Identity, scale=scale(k + n), bias=shift(k + n))
                link(ins)
                act.activation(out2, mtmp[:, g % 2, :], ACT.Copy).then_inc(hi_rounded, 1)

        act.dma_start(ident[:, :], a["c_ident"]).then_inc(c_in, 16)
        act.dma_start(vec1[96:112, :], a["c"].rearrange("(r n) -> r n", n=P)).then_inc(c_in, 16)
        act.dma_start(vec1[112:128, :], a["c_ctx"].rearrange("(r n) -> r n", n=P)).then_inc(c_in, 16)
        act.dma_start(vec1[0:96, :], a["b_mod"].rearrange("(r n) -> r n", n=P)).then_inc(c_in, 16)
        act.wait_ge(setup_turned, 1)
        act.activation(cols1[:, :], aux[:, 0, 0:P], ACT.Copy).then_inc(cols_ready, 1)
        act.wait_ge(cols_ready, 1)
        act.activation(silu_c[:, :, :].rearrange("p c k -> p (c k)"), cols1[:, 96:128], ACT.Silu).then_inc(silu_exp, 1)

        split(0, 2)
        u0 = UNIT["mod1"]
        act.wait_ge(rows_in, 32)
        with act.Fori(0, 4) as i:
            act.activation(junk, arena[:, bass.ds(i * D, D)], ACT.Square, accum_out=lam[:, 6:7]).then_inc(sumsq_ready, 1)
            for n in range(2):
                split(u0 + 4 * n + 2, 4, i, 8)
                if n == 0:
                    act.wait_ge(modcol_ready, 1 + i)
                group_done(u0 + 4 * n + 3, i, 8)
                act.activation(modrow1[0:4, n, :], acc[0:4, 2 * n, :], ACT.Copy).then_inc(acc_freed, 1)
        act.wait_ge(setup_turned, 2)
        act.activation(cols2[:, :], aux[:, 0, 0:V_END], ACT.Copy).then_inc(cols_ready, 1)
        act.wait_ge(cond_ready, 1)
        for g in range(8):
            build(BUILD["ctx"] + g, 2 * g, xhi, lambda k: scale_ctx[:, k:k + 1], lambda k: shift_ctx[:, k:k + 1])
        act.wait_ge(lam_sum, 1)
        act.activation(lam[:, 2:4], lam[:, 0:2], ACT.Exp).then_inc(lam_done, 1)
        act.wait_ge(sin_arg, 1)
        act.activation(rops[:, :, :], ang, ACT.Sin)
        act.activation(ropc[:, :, :], angk, ACT.Sin).then_inc(sin_done, 1)
        u0 = UNIT["ctx"]
        with act.Fori(0, 2) as i:
            for n in range(2):
                split(u0 + 4 * n + 2, 4, i, 8)
                group_done(u0 + 4 * n + 3, i, 8)
                act.activation(kv_out[:, i, 2:4, n * NW:(n + 1) * NW], banks(n), ACT.Copy).then_inc(acc_freed, 1)
        for g in range(8):
            build(BUILD["x"] + g, 2 * g, xhi, lambda k: scale_x[:, k:k + 1], lambda k: shift_x[:, k:k + 1])
        u0 = UNIT["in"]
        dst = [qk6[:, 0:2, :], qk6[:, 2:4, :], v1[:, 0:2, :], u_rows]
        for g in range(8):
            split(u0 + 4 * g + 2, 4)
            group_done(u0 + 4 * g + 3)
            if g == 6:
                act.wait_ge(turned, BUILD["heads"])
            act.activation(dst[g // 2][:, :, (g % 2) * NW:(g % 2 + 1) * NW], banks(g), ACT.Copy).then_inc(acc_freed, 1)
        for b in range(4):
            act.wait_ge(pooled, b + 1)
            act.activation(dT[:, 2 * b:2 * b + 2, :].rearrange("p k n -> p (k n)"), turn[:, b % 2, :], ACT.Copy)\
               .then_inc(pooled_copied, 1)
        u0, g0 = UNIT["att"], GROUP["att"]
        with act.Fori(0, HEADS1) as h:
            act.wait_ge(slab_turned, 1 + (h + 1))
            act.activation(slabT, aux_flat[:, 0:768], ACT.Copy).then_inc(slabT_ready, 1)

            def exponentials(t):
                act.wait_ge(max1, plus(t + 1, T, h))
                for c in range(2):
                    ins = act.activation(prob[:, c, :], turn[:, c, :], ACT.Exp, scale=HD ** -0.5,
                                         bias=lam[:, c:c + 1], accum_out=lam[:, 2 + c:3 + c])
                ins.then_inc(exp1, 1)

            def copy_probs(t):
                act.wait_ge(attn_turned, plus(t + 1, T, h))
                act.activation(probT, aux[:, 0, :], ACT.Copy).then_inc(attnT_ready, 1)

            def copy_output(t):
                act.wait_ge(head_out, plus(t + 1, T, h))
                act.activation(orow[:, t, :], aux[:, 1, 0:VD], ACT.Copy).then_inc(head_sq, 1)

            split(u0 + 2, 2, h, 8)
            exponentials(0)
            split(u0 + 4, 2, h, 8)
            copy_probs(0)
            exponentials(1)
            split(u0 + 6, 2, h, 8)
            copy_output(0)
            copy_probs(1)
            split(u0 + 8, 1, h, 8)
            group_done(u0 + 6, h, 8)
            act.activation(gates[:, :, bass.ds(h * NW, NW)], banks(0), ACT.Tanh, scale=0.5).then_inc(acc_freed, 1)
            act.wait_ge(modcol_ready, 1 + plus(4, 1, h))
            group_done(u0 + 7, h, 8)
            act.activation(modrow2[0:4, :], acc[0:4, 2, :], ACT.Copy).then_inc(modrow_ready, 1)
            split(u0 + 9, 1, h, 8)
            copy_output(1)
        for g in range(4):
            build(BUILD["heads"] + g, 2 * g, xhi, lambda k: cols2[:, V_SUBLN:V_SUBLN + 1])
        for g in range(4):
            build(BUILD["pool"] + g, 8 + 2 * g, xhi, lambda k: cols2[:, V_POOL + k - 8:V_POOL + k - 7])
        u0 = UNIT["up"]
        with act.Fori(0, 4) as i:
            split(u0 + 2, 6, i, 12)
            for n in range(2):
                if n == 0:
                    act.wait_ge(modcol_ready, 1 + plus(12, 1, i))
                group_done(u0 + 5 + 6 * n, i, 12)
                act.activation(modrow3[0:4, n, :], turn[0:4, n, :], ACT.Copy).then_inc(modrow_ready, 1)
                split(u0 + 8 + 4 * n, 4 - 2 * n, i, 12)
        for g in range(8):
            build(BUILD["mix"] + g, 2 * g, xhi, lambda k: 0.5)
        with act.Fori(0, 4) as i:
            split(UNIT["wo"] + 2, 4, i, 4)
        for g in range(8):
            build(BUILD["mlp"] + g, 2 * g, xhi, lambda k: scale_x[:, k:k + 1], lambda k: shift_x[:, k:k + 1])
        def quarter(e, u0, b0, last=False):
            def relu(n):
                group_done(u0 + 4 * n + 3, e, 16)
                act.activation(hid[:, :, n * NW:(n + 1) * NW], banks(n), ACT.Relu).then_inc(acc_freed, 1)

            def hidden(g):
                build(b0 + g, 2 * g, hhi, i=e, per=4)

            split(u0 + 2, 4, e, 16)
            relu(0)
            split(u0 + 6, 2, e, 16)
            hidden(0)
            split(u0 + 8, 1, e, 16)
            hidden(1)
            split(u0 + 9, 1, e, 16)
            relu(1)
            hidden(2)
            hidden(3)
            for n in range(4):
                split(u0 + 10 + 2 * n, 1, e, 16)
                if last and n:
                    for g in (2 * n - 2, 2 * n - 1):
                        build(BUILD["a"] + g, 2 * g, xhi, norm_a)
                split(u0 + 11 + 2 * n, 1, e, 16)

        def mean_squares():
            for t in range(T):
                act.activation(rows3[:, t], res3[:, t], ACT.Square, accum_out=lam[:, 6 + t:7 + t]).then_inc(sumsq_ready, 1)

        def scaled(dst, src, func, scale):
            for t in range(T):
                ins = act.activation(dst[:, t], src[:, t], func, scale=scale[:, t:t + 1])
            return ins

        norm_a = lambda k: cols2[:, V_NORM_A + k:V_NORM_A + k + 1]
        norm_b = lambda k: cols2[:, V_NORM_B + k:V_NORM_B + k + 1]
        with act.Fori(0, 7) as e:
            quarter(e, UNIT["mlp"], BUILD["hidden"])
        quarter(None, UNIT["mlp"] + 7 * 16, BUILD["hidden"] + 7 * 4, last=True)
        u0 = UNIT["a_in"]
        for g in range(4):
            if g == 0:
                split(u0 + 2, 1)
                for n in (6, 7):
                    build(BUILD["a"] + n, 2 * n, xhi, norm_a)
                mean_squares()
                split(u0 + 3, 3)
            else:
                split(u0 + 4 * g + 2, 4)
            group_done(u0 + 4 * g + 3)
            if g == 0:
                act.wait_ge(norm_ready, 1)
            scaled(q2[:, :, g * NW:(g + 1) * NW], banks(g), ACT.Copy, norm_q).then_inc(acc_freed, 1)
        split_halves(2 * (u0 + 18), 8)
        group_done(u0 + 16 + 3)
        scaled(kv_a, banks(0), ACT.Copy, norm).then_inc(acc_freed, 1)

        def turn_keys(n, dst):
            act.wait_ge(kT_turned, n + 1)
            act.activation(dst, turn_flat[0:HD, :], ACT.Copy).then_inc(kT_ready, 1)

        def queries(n, g, name):
            for b in range(4):
                act.wait_ge(q_turned, 1 + (plus(4 * n + b + 1, 4, g)))
                act.activation(qT[:, 2 * b:2 * b + 2].rearrange("p h t n -> p (h t n)"), turn[0:HD, b % 2, :], ACT.Copy)\
                   .then_inc(qT_ready, 1)
            split_filled(name, 0, g)

        def exponentials(r, g, per, sm, keys, sink, pairs):
            act.wait_ge(max2, plus(r + 1, per, g))
            for p in pairs:
                for h in (2 * p, 2 * p + 1):
                    x = sm[r % 2][h][:, 0:keys]
                    ins = act.activation(x, x, ACT.Exp, bias=m8[:, r % 2, h:h + 1], accum_out=s8[:, r % 2, h:h + 1])
                ins.then_inc(exp2, 1)
            if sink and 3 in pairs:
                act.wait_ge(sink_arg, plus(r + 1, per, g))
                act.activation(sk[:, r % 2, :], sk[:, r % 2, :], ACT.Exp).then_inc(sink_exp, 1)

        def copy_probs(r, g, per, p, keys):
            act.wait_ge(probs_turned, plus(4 * r + p + 1, 4 * per, g))
            act.wait_ge(out2, 2 + (plus(4 * r + p - 1, 4 * per, g)))
            n, w = min(keys, P), 2 * -(-keys // P) * P
            act.activation(pT[0:n, p % 2, 0:w], turn[0:n, p % 2, 0:w], ACT.Copy).then_inc(probsT_ready[0], 1)

        def rounds(r0, keys, g, sm, name, sink=False):
            per = len(keys)
            for j in range(-1, per):
                if j >= 0:
                    exponentials(r0 + j, g, per, sm, keys[j], sink, (0, 1))
                    copy_probs(r0 + j, g, per, 0, keys[j])
                    exponentials(r0 + j, g, per, sm, keys[j], sink, (2, 3))
                    copy_probs(r0 + j, g, per, 2, keys[j])
                split_filled(name, j + 2, g)

        def gate(u0, g):
            apart(act, units_used, plus(2 * u0 + 8, 8, g), act_passed)
            scaled(q2[:, :, bass.ds(g * NW, NW)], banks(1), ACT.Tanh, norm_half).then_inc(gate_ready, 1)

        turn_keys(0, kTs)
        with act.Fori(0, KVG) as g:
            queries(0, g, "a_z")
            rounds(ROUND_A, KEYS_A, g, sm_a, "a_z", sink=True)
            gate(UNIT["a_z"], g)
        for g in range(8):
            build(BUILD["a_o"] + g, 2 * g, ghi, lambda k: 0.5)
        for u in range(16):
            split(UNIT["a_out"] + u + 2, 1)
            if u >= 4 and u % 4 == 1:
                for g in (u // 4 * 2 - 2, u // 4 * 2 - 1):
                    build(BUILD["b"] + g, 2 * g, xhi, norm_b)
        u0, g0 = UNIT["b_att"], GROUP["b_att"]
        for n in range(4):
            if n == 0:
                split(u0 + 2, 1)
                for g in (6, 7):
                    build(BUILD["b"] + g, 2 * g, xhi, norm_b)
                mean_squares()
                split(u0 + 3, 3)
            else:
                split(u0 + 4 * n + 2, 4)
            group_done(u0 + 4 * n + 3)
            if n == 0:
                act.wait_ge(norm_ready, 2)
            if n < 3:
                scaled(kv6[:, :, n * NW:(n + 1) * NW], banks(g0 + n), ACT.Copy, norm).then_inc(acc_freed, 1)
            else:
                scaled(gate_b, banks(g0 + 3)[:, :, 0:B_GATES], ACT.Sigmoid, norm).then_inc(acc_freed, 1)

        def step(kind, n):
            if kind == "turn":
                act.wait_ge(cmp_turned, n + 1)
                act.activation(kcT, turn_flat, ACT.Copy).then_inc(cmp_copied, 1)
            elif kind == "hidden":
                act.wait_ge(hid_ready, n + 1)
                act.activation(hx, aux[0:60, 0, 0:256], ACT.Copy).then_inc(gelu_x, 1)
                act.wait_ge(gelu_arg, n + 1)
                act.activation(hy, hy, ACT.Tanh, scale=0.7978845608028654).then_inc(gelu_tanh, 1)
            elif kind == "turn_hidden":
                act.wait_ge(hT_turned, n + 1)
                act.activation(hT, v3(aux[:, 1, 0:120], 60), ACT.Copy).then_inc(hT_ready, 1)
            elif kind == "out":
                act.wait_ge(cmp_out, n + 1)
                if n == 0:
                    act.activation(cmpk[:, :], aux[0:HD, 0, 0:60], ACT.Copy).then_inc(cmp_stored, 1)
                else:
                    act.activation(cmpv, aux[0:NC, 0, 0:256], ACT.Copy).then_inc(cmp_stored, 1)
            else:
                turn_keys(n, (kTs, kTw)[n - 1])

        for u in range(16):
            split(u0 + 16 + u + 2, 1)
            if u in STEPS:
                step(*STEPS[u])
            if u % 4 == 3:
                group_done(u0 + 16 + u)
                scaled(q2[:, :, u // 4 * NW:(u // 4 + 1) * NW], banks(g0 + u // 4), ACT.Copy, norm_q).then_inc(acc_freed, 1)
        with act.Fori(0, KVG) as g:
            queries(4, g, "b_z")
            rounds(ROUND_B, KEYS_B, g, sm_b, "b_z")
            gate(UNIT["b_z"], g)
        for g in range(8):
            build(BUILD["b_o"] + g, 2 * g, xhi, lambda k: 0.5)
        with act.Fori(0, 3) as i:
            split(UNIT["b_out"] + 2, 4, i, 4)
        split(UNIT["b_out"] + 14, 2)

    @block.vector
    def _(dve):
        for signal, n in ((modcol_taken, 1), (masked2, 4), (out2_taken, 2)):
            dve.sem_inc(signal, n)
        link, looped = chained(dve, dve_chain)
        bc = lambda ap, shape: ap.to_broadcast(shape)

        def split_halves(first, n, i=None, per=0):
            for k, half in ((h // 2, h % 2) for h in range(first, first + n)):
                if k < UNITS:
                    on = slice(half * UK // 2, (half + 1) * UK // 2)
                    dve.wait_ge(hi_ready, plus(2 * k + 1 + half, 2 * per, i))
                    dve.tensor_tensor(wlo[:, k % 2, on], raw[:, k % 4, on], whi[:, k % 2, on].bitcast(F32), ALU.subtract)\
                       .then_inc(lo_ready, 1)

        def split(u, n, i=None, per=0):
            split_halves(2 * u, 2 * n, i, per)

        def split_filled(name, n, g):
            before, used = halves_filled(name, n)
            split_halves(2 * UNIT[name] + 4 + before, used, g, 4)

        def group_done(last, i=None, per=0):
            dve.wait_ge(units_used, plus(2 * last + 2, 2 * per, i))

        def banks(g):
            return acc[:, 2 * (g % 2):2 * (g % 2) + 2, :]

        def build(g, k, hi, lo, scale=None, shift=False, i=None, per=0):
            dve.wait_ge(hi_rounded, plus(g + 1, per, i))
            bank = turn[:, g % 2, :]
            flat = lambda x: x[:, k:k + 2, :].rearrange("p k n -> p (k n)")
            if shift:
                dve.tensor_tensor(flat(lo), mtmp[:, g % 2, :], flat(hi).bitcast(F32), ALU.subtract).then_inc(xt_ready, 1)
            elif scale is None:
                dve.tensor_tensor(flat(lo), bank, flat(hi).bitcast(F32), ALU.subtract).then_inc(xt_ready, 1)
            else:
                for n in range(2):
                    ins = dve.scalar_tensor_tensor(lo[:, k + n, :], bank[:, n * L:(n + 1) * L], scale(k + n),
                                                   hi[:, k + n, :].bitcast(F32), ALU.mult, ALU.subtract)
                ins.then_inc(xt_ready, 1)

        def left_operand_of_conditions():
            sc = silu_c[:, :, :].rearrange("p c k -> p k c")
            dve.memset(cflat[:, 4 * KT:].bitcast(F32), 0.0)
            link(dve.tensor_copy(cvec[:, :, 0:2], sc))
            dve.tensor_tensor(cvec[:, :, 2:4], sc, cvec[:, :, 0:2].bitcast(F32), ALU.subtract).then_inc(modw_ready, 1)

        def rms_rows(n, eps, dst, src, width):
            for t in range(T):
                ins = dve.tensor_tensor_reduce(out=dst[:, t], in0=src[:, t], in1=src[:, t], scale=1.0, scalar=0.0,
                                               op0=ALU.mult, op1=ALU.add, accum_out=mean[:, t:t + 1])
            link(ins)
            dve.tensor_scalar(mean[:, 0:T], mean[:, 0:T], 1.0 / width, eps, ALU.mult, ALU.add).then_inc(mean_ready, 1)
            dve.wait_ge(rstd_ready, n + 1)
            for t in range(T):
                ins = dve.tensor_scalar(dst[:, t], src[:, t], rstd[:, t:t + 1], None, ALU.mult)
            return ins

        dve.wait_ge(silu_exp, 1)
        left_operand_of_conditions()
        split(0, 2)
        u0 = UNIT["mod1"]
        with dve.Fori(0, 4) as i:
            end = looped(0, 4)
            split(u0 + 2, 4, i, 8)
            dve.wait_ge(sumsq_ready, i + 1)
            dve.tensor_scalar(mean[:, 0:1], lam[:, 6:7], 1.0 / D, EPS1, ALU.mult, ALU.add).then_inc(mean_ready, 1)
            split(u0 + 6, 2, i, 8)
            dve.wait_ge(rstd_ready, i + 1)
            part = arena[:, bass.ds(i * D, D)]
            dve.tensor_scalar(part, part, rstd[:, 0:1], None, ALU.mult).then_inc(normed, 1)
            split(u0 + 8, 2, i, 8)
            dve.wait_ge(modcol_ready, 1 + (i + 1))
            dve.tensor_copy(modcol[:, bass.ds(i * 16, 16)], aux[:, 1, 0:16]).then_inc(modcol_taken, 1)
            end()
        mc = modcol[:, :].rearrange("p (s c) -> p c s", c=2)
        dve.wait_ge(modcol_taken, 1 + 4)
        dve.wait_ge(cols_ready, 2)
        for c, (sc, sh) in enumerate(((scale_x, shift_x), (scale_ctx, shift_ctx))):
            link(dve.tensor_tensor(sc[:, :], mc[:, c, 16:32], cols1[:, 16:32], ALU.add))
            ins = dve.scalar_tensor_tensor(sc[:, :], sc[:, :], 1.0, cols2[:, V_NORM1:V_NORM1 + KT], ALU.add, ALU.mult)
            link(ins)
            ins = dve.tensor_tensor(sh[:, :], mc[:, c, 0:16], cols1[:, 0:16], ALU.add)
        ins.then_inc(cond_ready, 1)
        for g in range(8):
            build(BUILD["ctx"] + g, 2 * g, xhi, xlo, shift=True)
        dve.wait_ge(params_in, 16 * SMALL)
        for n in range(2):
            ins = dve.tensor_tensor_reduce(out=junk[:, 0:HD], in0=lamv[:, 2 * n, :], in1=lamv[:, 2 * n + 1, :], scale=1.0,
                                           scalar=0.0, op0=ALU.mult, op1=ALU.add, accum_out=lam[:, n:n + 1])
            link(ins) if n == 0 else ins.then_inc(lam_sum, 1)
        for n in range(2):
            w = qkw[:, n, :].rearrange("p (f two d) -> p f two d", f=2, two=2)
            ws = qkws[:, n, :].rearrange("p (f two d) -> p f two d", f=2, two=2)
            dve.tensor_copy(ws[:, :, 0, :], w[:, :, 1, :])
            link(dve.tensor_copy(ws[:, :, 1, :], w[:, :, 0, :]))
        for n, s0, s1 in ((0, 0, 2), (1, 2, 6)):
            dve.tensor_tensor(cosw[:, s0:s1, :], rcos[:, s0:s1, :], bc(qkw[:, n:n + 1, :], [P, s1 - s0, HD]), ALU.mult)
            dve.tensor_tensor(sinw[:, s0:s1, :], rsin[:, s0:s1, :], bc(qkws[:, n:n + 1, :], [P, s1 - s0, HD]), ALU.mult)
        link(dve.tensor_copy(posf[:, 0, 0:T], pos2[:, :]))
        for t in range(T):
            ins = dve.tensor_scalar(ang[:, t, :], invf[:, 0, :], posf[:, 0, t:t + 1], None, ALU.mult)
        link(ins)
        link(dve.tensor_scalar(angk, ang, 1.0 / (2 * np.pi), None, ALU.mult))
        link(dve.tensor_scalar(angk, angk, 12582912.0, None, ALU.add))
        link(dve.tensor_scalar(angk, angk, -12582912.0, None, ALU.add))
        for part in (6.28125, 0.0019350051879882812, 3.0199159819567e-07):
            link(dve.scalar_tensor_tensor(ang, angk, -part, ang, ALU.mult, ALU.add))
        link(dve.tensor_scalar(ang, ang, 3.1415925, -3.1415925, ALU.min, ALU.max))
        link(dve.tensor_scalar(angk, ang, -1.0, None, ALU.mult))
        link(dve.tensor_tensor(angk, ang, angk, ALU.max))
        dve.tensor_scalar(angk, angk, -1.0, float(np.float32(np.pi / 2)), ALU.mult, ALU.add).then_inc(sin_arg, 1)

        dve.wait_ge(lam_done, 1)
        link(dve.tensor_tensor(lam[:, 4:5], lam[:, 2:3], lam[:, 3:4], ALU.subtract))
        link(dve.tensor_scalar(lam[:, 5:6], lam[:, 4:5], LAM_INIT, None, ALU.add))
        with dve.Fori(0, 4) as i:
            split(UNIT["ctx"] + 2, 4, i, 4)
        for g in range(8):
            build(BUILD["x"] + g, 2 * g, xhi, xlo, shift=True)
        with dve.Fori(0, 8) as i:
            split(UNIT["in"] + 2, 4, i, 4)

        halves = lambda x: x.rearrange("p s (c f two d) -> p s c f two d", c=2, f=2, two=2)
        pairs_of = lambda x: x.rearrange("p s (c d) -> p s c d", c=2)

        def prepare(h, i, root):
            src = qk6[:, :, bass.ds(h * P, P)]
            link(dve.tensor_tensor(slab2, src, src, ALU.mult), i)
            link(dve.tensor_reduce(mean[:, 0:12], slab2.rearrange("p s (c d) -> p (s c) d", c=2), AX.X, ALU.add), i)
            dve.tensor_scalar(mean[:, 0:12], mean[:, 0:12], 1.0 / HD, EPS1, ALU.mult, ALU.add).then_inc(mean_ready, 1)
            dve.wait_ge(rstd_ready, root)
            link(dve.tensor_tensor(pairs_of(slab), pairs_of(src),
                                   bc(rstd[:, 0:12].rearrange("p (s c) -> p s c", c=2).unsqueeze(3), [P, 6, 2, HD]), ALU.mult), i)
            sw = sinw.rearrange("p s (f two d) -> p s f two d", f=2, two=2)
            for c in range(2):
                for two in range(2):
                    ins = dve.tensor_tensor(halves(slab2)[:, :, c, :, two, :], halves(slab)[:, :, c, :, 1 - two, :],
                                            sw[:, :, :, two, :], ALU.mult)
            link(ins, i)
            link(dve.tensor_tensor(pairs_of(slab), pairs_of(slab), bc(cosw.unsqueeze(2), [P, 6, 2, HD]), ALU.mult), i)
            dve.tensor_tensor(slab, slab, slab2, ALU.add).then_inc(slab_ready, 1)

        prepare(0, None, RMS["att1"] + 1)
        u0 = UNIT["att"]

        def head(h, i, last=False):
            def probabilities(t):
                dve.wait_ge(scores1, plus(t + 1, T, h))
                link(dve.tensor_reduce(lam[:, 0:2], turn[:, :, :], AX.X, ALU.max), i)
                dve.tensor_scalar(lam[:, 0:2], lam[:, 0:2], -(HD ** -0.5), None, ALU.mult).then_inc(max1, 1)
                dve.wait_ge(exp1, 1 + (plus(t + 1, T, h)))
                link(dve.reciprocal(s8[:, 0, 0:2], lam[:, 2:4]), i)
                link(dve.tensor_scalar(prob[:, 1, :], prob[:, 1, :], s8[:, 0, 1:2], lam[:, 5:6], ALU.mult, ALU.mult), i)
                dve.scalar_tensor_tensor(prob[:, 0, :], prob[:, 0, :], s8[:, 0, 0:1], prob[:, 1, :], ALU.mult, ALU.subtract)\
                   .then_inc(attn1, 1)

            def output(t):
                root = RMS["att1"] + (2 if t == 0 else 3 if last else 4)
                dve.wait_ge(head_sq, 1 + (plus(t + 1, T, h)))
                link(dve.tensor_tensor_reduce(out=osq, in0=orow[:, t, :], in1=orow[:, t, :], scale=1.0, scalar=0.0, op0=ALU.mult,
                                              op1=ALU.add, accum_out=mean[:, 0:1]), i)
                dve.tensor_scalar(mean[:, 0:1], mean[:, 0:1], 1.0 / VD, EPS1, ALU.mult, ALU.add).then_inc(mean_ready, 1)
                dve.wait_ge(rstd_ready, plus(root, 3, h))
                ins = dve.tensor_scalar(heads[:, t, bass.ds(h * VD, VD)], orow[:, t, :], rstd[:, 0:1], 1.0 - LAM_INIT,
                                        ALU.mult, ALU.mult)
                if t == 0:
                    link(ins, i)
                else:
                    ins.then_inc(head_done, 1)

            split(u0 + 2, 2, h, 8)
            probabilities(0)
            split(u0 + 4, 2, h, 8)
            probabilities(1)
            split(u0 + 6, 2, h, 8)
            output(0)
            dve.wait_ge(attn_turned, plus(2, T, h))
            if not last:
                prepare(h + 1, i, plus(RMS["att1"] + 3, 3, h))
            split(u0 + 8, 2, h, 8)
            output(1)
            dve.wait_ge(modcol_ready, 1 + plus(5, 1, h))
            dve.tensor_copy(modcol[:, bass.ds(h * 8, 8)], acc[:, 3, 0:8]).then_inc(modcol_taken, 1)

        with dve.Fori(0, HEADS1 - 1) as h:
            end = looped(14, HEADS1 - 1)
            head(h, h)
            end()
        head(HEADS1 - 1, None, last=True)
        for g in range(4):
            build(BUILD["heads"] + g, 2 * g, xhi, xlo, lambda k: cols2[:, V_SUBLN:V_SUBLN + 1])
        for g in range(4):
            build(BUILD["pool"] + g, 8 + 2 * g, xhi, xlo, lambda k: cols2[:, V_POOL + k - 8:V_POOL + k - 7])
        dve.wait_ge(modcol_taken, 1 + 12)
        link(dve.tensor_tensor(scale_x[:, :], mc[:, 0, 16:32], cols1[:, 64:80], ALU.add))
        link(dve.scalar_tensor_tensor(scale_x[:, :], scale_x[:, :], 1.0, cols2[:, V_NORM2:V_NORM2 + KT], ALU.add, ALU.mult))
        dve.tensor_tensor(shift_x[:, :], mc[:, 0, 0:16], cols1[:, 48:64], ALU.add).then_inc(cond_ready, 1)

        dve.wait_ge(bias_in, 32)
        for half, gate in enumerate((ga_b, gm_b)):
            u0 = UNIT["up"] + 24 * half
            with dve.Fori(0, 2) as i:
                end = looped(1, 2)
                split(u0 + 2, 10, i, 12)
                group_done(u0 + 9, i, 12)
                cols = bass.ds(half * W1 + i * NW, NW)
                for n, (dst, g) in enumerate(((upa, cols), (upb, bass.ds(D + half * W1 + i * NW, NW)))):
                    for t in range(T):
                        ins = dve.scalar_tensor_tensor(dst[:, t, :], gates[:, t, g], 1.0, acc[:, 2 * n + t, :], ALU.add, ALU.mult)
                    ins.then_inc(acc_freed, 1) if n == 0 else link(ins, i)
                dve.tensor_tensor(rows3[:, :, cols], upa, upb, ALU.add).then_inc(acc_freed, 1)
                split(u0 + 12, 2, i, 12)
                dve.wait_ge(modcol_ready, 1 + plus(13 + 2 * half, 1, i))
                part = gate[:, bass.ds(i * W1, W1)]
                dve.tensor_tensor(part, aux_flat, part, ALU.add).then_inc(modcol_taken, 1)
                end()
        for g in range(8):
            build(BUILD["mix"] + g, 2 * g, xhi, xlo, lambda k: 0.5)
        dve.wait_ge(x_in, 16)
        u0, g0 = UNIT["wo"], GROUP["wo"]
        with dve.Fori(0, 2) as i:
            end = looped(2, 2)
            for n in range(2):
                split(u0 + 4 * n + 2, 4, i, 8)
                group_done(u0 + 4 * n + 3, i, 8)
                cols = bass.ds(i * W1 + n * NW, NW)
                link(dve.tensor_tensor(mtmp, banks(n), bc(ga_b[:, cols].unsqueeze(1), [P, T, NW]), ALU.mult), i)
                dve.tensor_tensor(res3[:, :, cols], res3[:, :, cols], mtmp, ALU.add).then_inc(acc_freed, 1)
            end()
        dve.wait_ge(acc_freed, GROUP["mlp"])
        rms_rows(RMS["mlp"], EPS1, rows3, res3, D).then_inc(normed, 1)
        for g in range(8):
            build(BUILD["mlp"] + g, 2 * g, xhi, xlo, shift=True)
        dve.wait_ge(xt_ready, BUILD["hidden"])
        link(dve.memset(yacc, 0.0))
        norm_a = lambda k: cols2[:, V_NORM_A + k:V_NORM_A + k + 1]
        norm_b = lambda k: cols2[:, V_NORM_B + k:V_NORM_B + k + 1]

        def quarter(e, u0, g0, b0, s0, last=False):
            def square(n):
                dve.wait_ge(acc_freed, plus(g0 + n + 1, 6, e))
                part = hid[:, :, n * NW:(n + 1) * NW]
                dve.tensor_tensor(part, part, part, ALU.mult).then_inc(squared, 1)

            def hidden(g):
                build(b0 + g, 2 * g, hhi, hlo, i=e, per=4)

            split(u0 + 2, 4, e, 16)
            square(0)
            split(u0 + 6, 2, e, 16)
            hidden(0)
            split(u0 + 8, 1, e, 16)
            hidden(1)
            split(u0 + 9, 1, e, 16)
            square(1)
            hidden(2)
            hidden(3)
            for n in range(4):
                split(u0 + 10 + 2 * n, 1, e, 16)
                if last and n:
                    for g in (2 * n - 2, 2 * n - 1):
                        build(BUILD["a"] + g, 2 * g, xhi, xlo, norm_a)
                split(u0 + 11 + 2 * n, 1, e, 16)
                group_done(u0 + 9 + 2 * n, e, 16)
                cols = slice(n * NW, (n + 1) * NW)
                part = yacc[:, :, cols]
                dve.tensor_tensor(part, banks(n), part, ALU.add).then_inc(acc_freed, 1)
                if last:
                    dve.wait_ge(acc_freed, g0 + 2 + n + 1)
                    link(dve.tensor_tensor(part, part, bc(gm_b[:, cols].unsqueeze(1), [P, T, NW]), ALU.mult))
                    dve.tensor_tensor(res3[:, :, cols], res3[:, :, cols], part, ALU.add).then_inc(res_done, 1)

        def norms(n, root):
            dve.wait_ge(sumsq_ready, 4 + T * n)
            dve.tensor_scalar(mean[:, 0:T], lam[:, 6:8], 1.0 / D, EPS2, ALU.mult, ALU.add).then_inc(mean_ready, 1)
            dve.wait_ge(rstd_ready, root + 1)
            dve.tensor_copy(norm[:, :], rstd[:, 0:T])
            dve.tensor_scalar(norm_q[:, :], rstd[:, 0:T], HD ** -0.5, None, ALU.mult)
            dve.tensor_scalar(norm_half[:, :], rstd[:, 0:T], 0.5, None, ALU.mult).then_inc(norm_ready, 1)

        with dve.Fori(0, 7) as e:
            quarter(e, UNIT["mlp"], GROUP["mlp"], BUILD["hidden"], 0)
        quarter(None, UNIT["mlp"] + 7 * 16, GROUP["mlp"] + 7 * 6, BUILD["hidden"] + 7 * 4, 14, last=True)
        split(UNIT["a_in"] + 2, 1)
        for g in (6, 7):
            build(BUILD["a"] + g, 2 * g, xhi, xlo, norm_a)
        norms(1, RMS["a"])
        split(UNIT["a_in"] + 3, 3)

        def rotate(x, n_heads, i=None):
            x1, x2 = x[:, :, :, 0:ROT], x[:, :, :, ROT:2 * ROT]
            shape = [P, T, n_heads, ROT]
            cos, sin = (bc(w[:, :, :].unsqueeze(2), shape) for w in (ropc, rops))
            tmp = [r[:, 0:T * n_heads * ROT].rearrange("p (t h d) -> p t h d", t=T, d=ROT) for r in rope_t]
            for dst, src, w in ((tmp[0], x1, cos), (tmp[1], x2, sin), (tmp[2], x2, cos), (tmp[3], x1, sin)):
                ins = dve.tensor_tensor(dst, src, w, ALU.mult)
            link(ins, i)
            dve.tensor_tensor(x1, tmp[0], tmp[1], ALU.subtract)
            ins = dve.tensor_tensor(x2, tmp[2], tmp[3], ALU.add)
            return ins

        heads_of = lambda x, n: x.rearrange("p t (h d) -> p t h d", h=n)
        with dve.Fori(0, 4) as i:
            end = looped(2, 4)
            dve.wait_ge(acc_freed, GROUP["a_in"] + 1 + i)
            link(rotate(heads_of(q2[:, :, bass.ds(i * NW, NW)], HG), HG, i), i)
            split(UNIT["a_in"] + 6, 4, i, 4)
            end()
        dve.wait_ge(acc_freed, GROUP["a_z"])
        rotate(heads_of(kv_a[:, :, 0:256], KVG), KVG).then_inc(roped, 1)

        def maxima(r, g, per, sm, keys, mask, pairs):
            for p in pairs:
                apart(dve, scores2, plus(4 * r + p + 1, 4 * per, g), dve_passed)
                for h in (2 * p, 2 * p + 1):
                    ins = dve.tensor_tensor_reduce(out=sm[r % 2][h][:, 0:keys], in0=acc[:, p % 2, (h % 2) * L:(h % 2) * L + keys],
                                                   in1=mask, scale=1.0, scalar=3 * NEG, op0=ALU.add, op1=ALU.max,
                                                   accum_out=m8[:, r % 2, h:h + 1])
                ins.then_inc(masked2, 1)

        def less_maxima(r, g, per, sink, any_key):
            top = m8[:, r % 2, :]
            dve.wait_ge(masked2, 4 + plus(4 * r + 4, 4 * per, g))
            if sink:
                link(dve.tensor_tensor(top, top, sinks[:, bass.ds(g * HG, HG)], ALU.max), g)
            if any_key is not None:
                link(dve.tensor_scalar(top, top, any_key, None, ALU.mult), g)
            dve.tensor_scalar(top, top, -1.0, None, ALU.mult).then_inc(max2, 1)
            if sink:
                dve.wait_ge(max2, plus(r + 1, per, g))
                dve.tensor_tensor(sk[:, r % 2, :], top, sinks[:, bass.ds(g * HG, HG)], ALU.add).then_inc(sink_arg, 1)

        def copy_probs(r, g, per, p, keys):
            dve.wait_ge(probs_turned, plus(4 * r + p + 1, 4 * per, g))
            dve.wait_ge(out2, 2 + (plus(4 * r + p - 1, 4 * per, g)))
            n, w = min(keys, P), 2 * -(-keys // P) * P
            dve.tensor_copy(pT[0:n, p % 2, 0:w], turn[0:n, p % 2, 0:w]).then_inc(probsT_ready[1], 1)

        def outputs(r, g, per, t, sink, any_key, gate):
            total = s8[:, r % 2, :]
            dve.wait_ge(exp2, plus(4 * r + 4, 4 * per, g))
            if sink:
                dve.wait_ge(sink_exp, plus(r + 1, per, g))
                link(dve.tensor_tensor(total, total, sk[:, r % 2, :], ALU.add), g)
            if any_key is not None:
                link(dve.tensor_scalar(total, total, 1.0e-30, None, ALU.max), g)
            link(dve.reciprocal(total, total), g)
            if gate is not None:
                link(dve.tensor_tensor(total, total, gate_b[:, t, bass.ds(gate * 32 + g * HG, HG)], ALU.mult), g)
            dve.wait_ge(out2, 2 + (plus(4 * r + 4, 4 * per, g)))
            o = aux[:, r % 2, :].rearrange("p (h d) -> p h d", h=HG)
            dst = rows3[:, t, bass.ds(g * NW, NW)]
            w = bc(total.unsqueeze(2), [P, HG, HD])
            if not gate:
                dve.tensor_tensor(dst.rearrange("p (h d) -> p h d", h=HG), o, w, ALU.mult).then_inc(out2_taken, 1)
            else:
                dve.tensor_tensor(otmp.rearrange("p (h d) -> p h d", h=HG), o, w, ALU.mult).then_inc(out2_taken, 1)
                dve.wait_ge(out2_taken, 2 + plus(r + 1, per, g))
                link(dve.tensor_tensor(dst, dst, otmp, ALU.add), g)

        def rounds(r0, kinds, g, sm, name, sink=False):
            per = len(kinds)
            split_filled(name, 0, g)
            for j in range(-1, per):
                if j < 0:
                    maxima(r0, g, per, sm, kinds[0][0], kinds[0][1], (0, 1))
                else:
                    copy_probs(r0 + j, g, per, 1, kinds[j][0])
                if j + 1 < per:
                    keys, mask, _, any_key, _ = kinds[j + 1]
                    maxima(r0 + j + 1, g, per, sm, keys, mask, (2, 3))
                    less_maxima(r0 + j + 1, g, per, sink, any_key)
                if j >= 0:
                    copy_probs(r0 + j, g, per, 3, kinds[j][0])
                if j + 2 < per:
                    maxima(r0 + j + 2, g, per, sm, kinds[j + 2][0], kinds[j + 2][1], (0, 1))
                if j >= 0:
                    _, _, t, any_key, gate = kinds[j]
                    outputs(r0 + j, g, per, t, sink, any_key, gate)
                split_filled(name, j + 2, g)
            cols = bass.ds(g * NW, NW)
            dve.wait_ge(gate_ready, plus(GATES_BEFORE[name] + 1, 1, g))
            dve.scalar_tensor_tensor(q2[:, :, cols], q2[:, :, cols], 1.0, banks(1), ALU.add, ALU.mult).then_inc(acc_freed, 1)
            dve.wait_ge(acc_freed, plus(GROUP[name] + 1, 1, g))
            dve.wait_ge(out2_taken, 2 + plus(r0 + per, per, g))
            for t in range(T):
                ins = dve.scalar_tensor_tensor(rows3[:, t, cols], rows3[:, t, cols], norm[:, t:t + 1], q2[:, t, cols],
                                               ALU.mult, ALU.mult)
            ins.then_inc(gated, 1)

        dve.wait_ge(masks_in, 16)
        with dve.Fori(0, KVG) as g:
            end = looped(6, KVG)
            rounds(ROUND_A, [(P, causal[:, 0:P], 0, None, None), (L, windowed, 1, None, None)], g, sm_a, "a_z",
                   sink=True)
            end()
        for g in range(8):
            build(BUILD["a_o"] + g, 2 * g, ghi, glo, lambda k: 0.5)

        def residual(name, turns):
            u0, g0 = UNIT[name], GROUP[name]
            with dve.Fori(0, turns) as i:
                for n in range(2):
                    split(u0 + 4 * n + 2, 4, i, 8)
                    group_done(u0 + 4 * n + 3, i, 8)
                    part = res3[:, :, bass.ds(i * W1 + n * NW, NW)]
                    dve.tensor_tensor(part, banks(g0 + n), part, ALU.add).then_inc(acc_freed, 1)

        for u in range(16):
            split(UNIT["a_out"] + u + 2, 1)
            if u >= 4 and u % 4 == 1:
                for g in (u // 4 * 2 - 2, u // 4 * 2 - 1):
                    build(BUILD["b"] + g, 2 * g, xhi, xlo, norm_b)
            if u % 4 == 3:
                n = u // 4
                group_done(UNIT["a_out"] + u)
                part = res3[:, :, n * NW:(n + 1) * NW]
                dve.tensor_tensor(part, banks(GROUP["a_out"] + n), part, ALU.add).then_inc(acc_freed, 1)
        split(UNIT["b_att"] + 2, 1)
        for g in (6, 7):
            build(BUILD["b"] + g, 2 * g, xhi, xlo, norm_b)
        norms(2, RMS["b"])
        split(UNIT["b_att"] + 3, 3)
        with dve.Fori(0, 3) as i:
            split(UNIT["b_att"] + 6, 4, i, 4)

        def twice(n):
            src = kv6[:, :, n * 256:(n + 1) * 256].rearrange("p t (g d) -> p t g d", g=KVG)
            dve.tensor_copy(kdup[:, :, :, 0:HD], src)
            dve.tensor_copy(kdup[:, :, :, HD:P], src).then_inc(dup_ready, 1)

        def step(kind, n):
            if kind == "turn":
                dve.wait_ge(cmp_copied, n + 1)
                pos = cols2[:, V_KPOS + 16 * n:V_KPOS + 16 * n + 16]
                for half in range(2):
                    on = slice(half * HD, (half + 1) * HD)
                    kc = kcT[on, :].rearrange("p (g c m two) -> p two m g c", g=KVG, c=16, two=2)[:, half]
                    for l in range(2):
                        ins = dve.tensor_tensor(blkT[on, 8 * l:8 * l + 8], kc[:, :, :, l:l + NC],
                                                bc(pos[on, 8 * l:8 * l + 8].unsqueeze(2).unsqueeze(3), [HD, 8, KVG, NC]), ALU.add)
                ins.then_inc(blk_ready, 1)
                if n == 0:
                    twice(1)
            elif kind == "hidden":
                dve.wait_ge(gelu_x, n + 1)
                link(dve.tensor_tensor(hy, hx, hx, ALU.mult))
                link(dve.tensor_scalar(hy, hy, 0.044715, 1.0, ALU.mult, ALU.add))
                dve.tensor_tensor(hy, hy, hx, ALU.mult).then_inc(gelu_arg, 1)
                dve.wait_ge(gelu_tanh, n + 1)
                link(dve.tensor_scalar(hy, hy, 0.5, 0.5, ALU.mult, ALU.add))
                dve.tensor_tensor(hz, hx, hy, ALU.mult).then_inc(gelu_done, 1)

        dve.wait_ge(acc_freed, GROUP["b_att"] + 3)
        twice(0)
        link(rotate(heads_of(kv6[:, :, 512:768], KVG), KVG))
        rotate(heads_of(kv6[:, :, 1024:1280], KVG), KVG).then_inc(roped, 1)
        dve.wait_ge(roped, 2)
        for u in range(16):
            split(UNIT["b_att"] + 16 + u + 2, 1)
            if u in STEPS:
                step(*STEPS[u])
            if u % 4 == 3:
                dve.wait_ge(acc_freed, GROUP["b_att"] + 5 + u // 4)
                ins = rotate(heads_of(q2[:, :, u // 4 * NW:(u // 4 + 1) * NW], HG), HG)
                link(ins) if u < 15 else ins.then_inc(roped, 1)
        with dve.Fori(0, KVG) as g:
            end = looped(20, KVG)
            kinds = []
            for t in range(T):
                mask = causal[:, 0:P] if t == 0 else causal[:, P:3 * P]
                kinds += [(NC, cmp_mask[:, NC * t:NC * t + NC], t, cmp_any[:, t:t + 1], 0),
                          ((t + 1) * P, mask, t, None, 1), ((t + 1) * P, mask, t, None, 2)]
            rounds(ROUND_B, kinds, g, sm_b, "b_z")
            end()
        for g in range(8):
            build(BUILD["b_o"] + g, 2 * g, xhi, xlo, lambda k: 0.5)
        residual("b_out", 1)
        u0, g0 = UNIT["b_out"], GROUP["b_out"]
        for n in (2, 3):
            split(u0 + 4 * n + 2, 4)
            group_done(u0 + 4 * n + 3)
            part = res3[:, :, n * NW:(n + 1) * NW]
            dve.tensor_tensor(part, banks(g0 + n), part, ALU.add).then_inc(acc_freed, 1)
        dve.wait_ge(acc_freed, g0 + 4)
        link(rms_rows(RMS["final"], EPS2, rows3, res3, D))
        dve.wait_ge(fin_in, 16)
        dve.tensor_tensor(rows3, rows3, bc(fin_w.unsqueeze(1), [P, T, D]), ALU.mult).then_inc(norm_done, 1)

    @block.tensor
    def _(pe):
        for signal, n in ((modcol_ready, 1), (slab_turned, 1), (out2, 2), (q_turned, 1)):
            pe.sem_inc(signal, n)
        def multiply(u, k, k_units, bank0, k_first=0, hi=xhi, lo=xlo, i=None, per=0, width=NW, tiles=range(UK)):
            for kk in tiles:
                if kk % 2 == 0:
                    pe.wait_ge(lo_ready, plus(2 * u + 1 + kk // 2, 2 * per, i))
                kt = k_first + UK * k + kk
                w_hi, w_lo = whi[:, u % 2, kk, 0:width], wlo[:, u % 2, kk, 0:width]
                for t in range(T):
                    bank = acc[:, bank0 + t, 0:width]
                    tok = slice(t * P, (t + 1) * P)
                    pe.matmul(bank, hi[:, kt, tok], w_hi, start=kt == k_first, stop=False, skip_group_check=True)
                    pe.matmul(bank, hi[:, kt, tok], w_lo, start=False, stop=False, skip_group_check=True)
                    mm = pe.matmul(bank, lo[:, kt, tok], w_hi, start=False, stop=kt == k_first + UK * k_units - 1,
                                   skip_group_check=True)
                if kk % 2 == 1:
                    mm.then_inc(units_used, 1)

        def product(u0, g, k_units, k_first=0, hi=xhi, lo=xlo, built=None, i=None, per=0, g_count=0, g_per=0, width=NW):
            if g_count >= 2:
                pe.wait_ge(acc_freed, plus(g_count - 1, g_per, i))
            for k in range(k_units):
                if built is not None:
                    built(k)
                multiply(u0 + k, k, k_units, 2 * (g % 2), k_first, hi, lo, i, per, width)

        def condition(u, k, bank, i, per):
            for kk in range(UK):
                if kk % 2 == 0:
                    pe.wait_ge(lo_ready, plus(2 * u + 1 + kk // 2, 2 * per, i))
                kt = UK * k + kk
                left = cflat[:, 4 * kt:4 * kt + P]
                pe.matmul(bank, left, whi[:, u % 2, kk], start=kt == 0, stop=False, skip_group_check=True)
                mm = pe.matmul(bank, left, wlo[:, u % 2, kk], start=False, stop=kt == KT - 1, skip_group_check=True)
                if kk % 2 == 1:
                    mm.then_inc(units_used, 1)

        def condition_columns():
            for n in range(2):
                for s in range(4):
                    o = 2 * (4 * n + s)
                    mm = pe.matmul(aux[:, 1, o:o + 2], modrow1[0:4, n, s * P:(s + 1) * P], sel[0:4, P:P + 2],
                                   start=True, stop=True)
            mm.then_inc(modcol_ready, 1)

        def turn_rows(name, src, pairs=range(8), i=None, per=0, ready=None):
            for g in pairs:
                n = (BUILD[name] if name in BUILD else name) + g
                if ready is not None:
                    ready(g)
                if n >= 2:
                    pe.wait_ge(xt_ready, plus(n - 1, per, i))
                for k in range(2):
                    for t in range(T):
                        mm = pe.transpose(turn[:, n % 2, k * L + t * P:k * L + (t + 1) * P],
                                          src[:, t, (2 * g + k) * P:(2 * g + k + 1) * P], ident[:, :])
                mm.then_inc(turned, 1)

        def built(name, i=None, per=0):
            return lambda k: pe.wait_ge(xt_ready, plus(BUILD[name] + 2 * k + 2, per, i))

        def groups(name, turns, first=0, build=None, i_width=2):
            with pe.Fori(0, turns) as i:
                for n in range(2):
                    product(UNIT[name] + 4 * (first + n), GROUP[name] + first + n, 4, built=built(build), i=i, per=8,
                            g_count=GROUP[name] + first + n, g_per=2)

        pe.wait_ge(c_in, 64)
        pe.transpose(aux[:, 0, 0:P], vec1, ident[:, :]).then_inc(setup_turned, 1)
        pe.wait_ge(modw_ready, 1)
        with pe.Fori(0, 4) as i:
            for n in range(2):
                for k in range(4):
                    condition(UNIT["mod1"] + 4 * n + k, k, acc[:, 2 * n, :], i, 8)
            pe.wait_ge(acc_freed, plus(2, 2, i))
            pe.wait_ge(modcol_taken, 1 + i)
            pe.wait_ge(params_in, 16 * SMALL)
            condition_columns()
        pe.transpose(aux[:, 0, 0:V_END], vec2[0:V_END, :], ident[0:V_END, 0:V_END]).then_inc(setup_turned, 1)
        pe.wait_ge(normed, 4)
        turn_rows("ctx", rows3)
        groups("ctx", 2, build="ctx")
        turn_rows("x", res3)
        groups("in", 4, build="x")
        pe.wait_ge(pool_in, 16)
        pe.wait_ge(acc_freed, GROUP["att"])
        for b in range(4):
            if b >= 2:
                pe.wait_ge(pooled_copied, b - 1)
            for n in range(2):
                s = 2 * b + n
                for t in range(T):
                    mm = pe.matmul(turn[:, b % 2, n * L:(n + 1) * L], u_rows[:, t, s * P:(s + 1) * P], band[:, t, s // 2, :],
                                   start=t == 0, stop=t == T - 1)
            mm.then_inc(pooled, 1)
        pe.wait_ge(pooled_copied, 4)
        u0, g0 = UNIT["att"], GROUP["att"]
        with pe.Fori(0, HEADS1) as h:
            def fill(k):
                if k == 0:
                    pe.wait_ge(acc_freed, plus(g0, 1, h))
                multiply(u0 + 2 * k, k, 4, 0, i=h, per=8)
                condition(u0 + 2 * k + 1, k, acc[:, 2, :], h, 8)

            def scores(t):
                pe.wait_ge(exp1, 1 + (plus(t, T, h)))
                for c in range(2):
                    on = slice(c * HD, (c + 1) * HD)
                    mm = pe.matmul(turn[:, c, :], slabT[on, t * P:(t + 1) * P], slabT[on, 256:768], start=True, stop=True)
                mm.then_inc(scores1, 1)

            def turn_probs(t):
                pe.wait_ge(attn1, plus(t + 1, T, h))
                for k in range(4):
                    mm = pe.transpose(aux[:, 0, k * P:(k + 1) * P], prob[:, 0, k * P:(k + 1) * P], ident[:, :])
                mm.then_inc(attn_turned, 1)

            def output(t):
                pe.wait_ge(attnT_ready, plus(t + 1, T, h))
                pe.wait_ge(head_sq, 1 + plus(t, T, h))
                for k in range(4):
                    mm = pe.matmul(aux[:, 1, 0:VD], probT[:, k * P:(k + 1) * P], v1[:, k, bass.ds(h * VD, VD)],
                                   start=k == 0, stop=k == 3)
                mm.then_inc(head_out, 1)

            pe.wait_ge(slab_ready, h + 1)
            pe.wait_ge(head_sq, 1 + (2 * h))
            for s in range(6):
                mm = pe.transpose(aux_flat[:, s * P:(s + 1) * P], slab[:, s, :], ident[:, :])
            mm.then_inc(slab_turned, 1)
            fill(0)
            pe.wait_ge(slabT_ready, h + 1)
            scores(0)
            fill(1)
            turn_probs(0)
            scores(1)
            fill(2)
            output(0)
            turn_probs(1)
            fill(3)
            output(1)
            pe.wait_ge(modrow_ready, h + 1)
            pe.wait_ge(modcol_taken, 1 + plus(4, 1, h))
            for s in range(4):
                mm = pe.matmul(acc[:, 3, 2 * s:2 * s + 2], modrow2[0:4, s * P:(s + 1) * P], sel[0:4, P:P + 2],
                               start=True, stop=True)
            mm.then_inc(modcol_ready, 1)
        pe.wait_ge(head_done, HEADS1)
        turn_rows("heads", heads, range(4))
        pe.wait_ge(pool_in, 32)
        for g in range(4):
            n = BUILD["pool"] + g
            pe.wait_ge(xt_ready, n - 1)
            for d in range(2):
                for c in range(2):
                    mm = pe.matmul(turn[:, n % 2, d * L:(d + 1) * L], poolw[:, g, c, d * P:(d + 1) * P],
                                   dT[:, 2 * g + c, :], start=c == 0, stop=c == 1)
            mm.then_inc(turned, 1)
        pe.wait_ge(xt_ready, BUILD["mix"])
        pe.wait_ge(acc_freed, GROUP["up"])
        u0, g0 = UNIT["up"], GROUP["up"]
        with pe.Fori(0, 4) as i:
            for k in range(4):
                if k % 2 == 0:
                    pe.wait_ge(acc_freed, plus(g0 + k // 2 - 1, 2, i))
                multiply(u0 + 3 * k, k % 2, 2, 2 * (k // 2), 8 * (k // 2), i=i, per=12)
                for n in range(2):
                    m = 2 * k + n
                    if m % 4 == 0:
                        pe.wait_ge(modrow_ready, plus(8 + m // 4 - 1, 2, i))
                    condition(u0 + 3 * k + 1 + n, m % 4, turn[:, m // 4, :], i, 12)
            pe.wait_ge(modrow_ready, plus(8 + 2, 2, i))
            pe.wait_ge(modcol_taken, 1 + plus(12, 1, i))
            for n in range(2):
                mm = pe.matmul(aux[:, n, :], sel[0:4, 0:P], modrow3[0:4, n, :], start=True, stop=True)
            mm.then_inc(modcol_ready, 1)
        pe.wait_ge(acc_freed, GROUP["wo"])
        turn_rows("mix", rows3)
        groups("wo", 2, build="mix")
        pe.wait_ge(cond_ready, 2)
        pe.wait_ge(normed, 5)
        turn_rows("mlp", rows3)
        u0, g0 = UNIT["mlp"], GROUP["mlp"]

        def quarter(e, u0, g0, b0, s0, last=False):
            def hidden(pairs):
                turn_rows(b0, hid, pairs, i=e, per=4,
                          ready=lambda g: pe.wait_ge(squared, plus(s0 + g // 2 + 1, 2, e)))

            product(u0, 0, 4, built=built("mlp"), i=e, per=16, g_count=g0, g_per=6)
            pe.wait_ge(acc_freed, plus(g0, 6, e))
            for k in range(4):
                multiply(u0 + 4 + k, k, 4, 2, i=e, per=16)
                if k in (1, 2):
                    hidden((k - 1,))
            pe.wait_ge(acc_freed, plus(g0 + 1, 6, e))
            pe.wait_ge(xt_ready, plus(b0 + 2, 4, e))
            for tiles in ((0, 1, 2), (3,)):
                multiply(u0 + 8, 0, 2, 0, 0, hhi, hlo, e, 16, tiles=tiles)
                if tiles[0] == 0:
                    hidden((2, 3))
            pe.wait_ge(xt_ready, plus(b0 + 4, 4, e))
            multiply(u0 + 9, 1, 2, 0, 0, hhi, hlo, e, 16)
            for n in range(1, 4):
                pe.wait_ge(acc_freed, plus(g0 + 1 + n, 6, e))
                for k in range(2):
                    multiply(u0 + 8 + 2 * n + k, k, 2, 2 * (n % 2), 0, hhi, hlo, e, 16)
                    if last and k == 0:
                        turn_rows("a", res3, (2 * n - 2, 2 * n - 1), ready=lambda g: pe.wait_ge(res_done, g // 2 + 1))

        with pe.Fori(0, 7) as e:
            quarter(e, u0, g0, BUILD["hidden"], 0)
        quarter(None, u0 + 7 * 16, g0 + 7 * 6, BUILD["hidden"] + 7 * 4, 14, last=True)
        u0, g0 = UNIT["a_in"], GROUP["a_in"]
        for g in range(2):
            pe.wait_ge(acc_freed, g0 + g - 1)
            for k in range(4):
                if g == 0:
                    built("a")(k)
                multiply(u0 + 4 * g + k, k, 4, 2 * g)
                if g == 0 and k == 0:
                    turn_rows("a", res3, (6, 7), ready=lambda g: pe.wait_ge(res_done, 4))
        groups("a_in", 1, first=2, build="a")
        product(u0 + 16, 0, 4, built=built("a"), g_count=g0 + 4)

        def turn_keys(keys, n):
            for g in range(KVG):
                for t in range(T):
                    mm = pe.transpose(turn_flat[0:HD, g * L + t * P:g * L + (t + 1) * P], keys[:, t, g * HD:(g + 1) * HD],
                                      ident[:, :])
            mm.then_inc(kT_turned, 1)

        def queries(n, g, fill):
            apart(pe, qs_ready, plus(n + 1, 1, g), pe_passed)
            for b in range(4):
                if b >= 2:
                    fill(0, b - 2)
                    apart(pe, qT_ready, plus(4 * n + b - 1, 4, g), pe_passed)
                for h in range(2):
                    for t in range(T):
                        o = (2 * h + t) * P
                        hh = 2 * b + h
                        mm = pe.transpose(turn[0:HD, b % 2, o:o + P], qs[:, t, hh * HD:(hh + 1) * HD], ident[:, :])
                mm.then_inc(q_turned, 1)
            fill(0, 2)
            pe.wait_ge(qT_ready, plus(4 * n + 4, 4, g))

        def scores(r, g, per, p, kind):
            keys, t, kT, _ = kind
            apart(pe, masked2, 4 + plus(4 * r + p - 1, 4 * per, g), pe_passed)
            for h in range(2):
                mm = pe.matmul(acc[:, p % 2, h * L:h * L + keys], qT[:, 2 * p + h, t, :], kT, start=True, stop=True)
            mm.then_inc(scores2, 1)

        def turn_probs(r, g, per, p, kind, sm):
            kt, n = -(-kind[0] // P), min(kind[0], P)
            pe.wait_ge(exp2, plus(4 * r + p + 1, 4 * per, g))
            for h in range(2):
                for k in range(kt):
                    o = (h * kt + k) * P
                    mm = pe.transpose(turn[0:n, p % 2, o:o + P], sm[r % 2][2 * p + h][:, k * P:k * P + n], ident[:, :])
            mm.then_inc(probs_turned, 1)

        def outputs(r, g, per, p, kind):
            keys, _, _, v_of = kind
            kt, n = -(-keys // P), min(keys, P)
            apart(pe, probsT_ready[p % 2], plus(2 * r + p // 2 + 1, 2 * per, g), pe_passed)
            for h in range(2):
                for k in range(kt):
                    o = (h * kt + k) * P
                    hh = 2 * p + h
                    mm = pe.matmul(aux[:, r % 2, hh * HD:(hh + 1) * HD], pT[0:n, p % 2, o:o + P], v_of(k),
                                   start=k == 0, stop=k == kt - 1)
            mm.then_inc(out2, 1)

        def rounds(r0, kinds, g, sm, fill):
            per = len(kinds)
            for j in range(-1, per):
                def ahead(n, p):
                    if 0 <= j + n < per:
                        scores(r0 + j + n, g, per, p, kinds[j + n])

                turn_pair = lambda p: turn_probs(r0 + j, g, per, p, kinds[j], sm) if j >= 0 else None
                output = lambda p: outputs(r0 + j, g, per, p, kinds[j]) if j >= 0 else None
                if j < 0:
                    ahead(1, 0)
                    ahead(1, 1)
                fill(j + 2, 0)
                if j >= 0:
                    pe.wait_ge(out2_taken, 2 + plus(r0 + j - 1, per, g))
                turn_pair(0)
                turn_pair(1)
                fill(j + 2, 1)
                output(0)
                ahead(1, 2)
                turn_pair(2)
                fill(j + 2, 2)
                output(1)
                ahead(1, 3)
                turn_pair(3)
                output(2)
                ahead(2, 0)
                ahead(2, 1)
                fill(j + 2, 3)
                output(3)

        def filler(name, g):
            done = [0]

            def fill(part, n):
                for _ in range(FILLS[name][part][n]):
                    k, kk = divmod(done[0], UK)
                    done[0] += 1
                    if k == 0 and kk == 0:
                        pe.wait_ge(acc_freed, plus(GROUP[name], 1, g))
                    multiply(UNIT[name] + k, k, 4, 2, i=g, per=4, tiles=(kk,))
            return fill

        pe.wait_ge(roped, 1)
        turn_keys(kv_a, 0)
        pe.wait_ge(kT_ready, 1)
        with pe.Fori(0, KVG) as g:
            fill = filler("a_z", g)
            queries(0, g, fill)
            pe.wait_ge(values_ready, g + 1)
            v_of = lambda k: v_g[:, 0, k]
            rounds(ROUND_A, [(n * P, n - 1, kTs[:, bass.ds(g * L, n * P)], v_of) for n in (1, 2)], g, sm_a,
                   fill)
        pe.wait_ge(gated, KVG)
        turn_rows("a_o", rows3)
        u0, g0 = UNIT["a_out"], GROUP["a_out"]
        through = lambda g: pe.wait_ge(acc_freed, g0 + g // 2 + 1)
        for n in range(4):
            pe.wait_ge(acc_freed, g0 + n - 1)
            for k in range(4):
                if n == 0:
                    built("a_o")(k)
                multiply(u0 + 4 * n + k, k, 4, 2 * ((g0 + n) % 2), 0, ghi, glo)
                if n and k == 1:
                    turn_rows("b", res3, (2 * n - 2, 2 * n - 1), ready=through)
        u0, g1 = UNIT["b_att"], GROUP["b_att"]
        for n in range(4):
            pe.wait_ge(acc_freed, g1 + n - 1)
            for k in range(4):
                if n == 0:
                    built("b")(k)
                multiply(u0 + 4 * n + k, k, 4, 2 * ((g1 + n) % 2), width=NW if n < 3 else B_GATES)
                if n == 0 and k == 0:
                    turn_rows("b", res3, (6, 7), ready=through)
        g0 = g1

        def step(kind, n):
            if kind == "turn":
                pe.wait_ge(dup_ready, n + 1)
                for g in range(KVG):
                    for t in range(T):
                        mm = pe.transpose(turn_flat[:, g * L + t * P:g * L + (t + 1) * P], kdup[:, t, g, :], ident[:, :])
                mm.then_inc(cmp_turned, 1)
            elif kind == "hidden":
                pe.wait_ge(blk_ready, n + 1)
                pe.wait_ge(cmp_w_in, 32 * (n + 1))
                for l in range(16):
                    mm = pe.matmul(aux[0:60, 0, 0:256], blkT[:, l].rearrange("p g c -> p (g c)"), w1c[:, l, :],
                                   start=l == 0, stop=l == 15)
                mm.then_inc(hid_ready, 1)
            elif kind == "turn_hidden":
                pe.wait_ge(gelu_done, n + 1)
                for k in range(2):
                    mm = pe.transpose(aux[:, 1, k * 60:(k + 1) * 60], hz[:, k * P:(k + 1) * P], ident[0:60, 0:60])
                mm.then_inc(hT_turned, 1)
            elif kind == "out":
                pe.wait_ge(hT_ready, n + 1)
                if n == 0:
                    for k in range(2):
                        mm = pe.matmul(aux[0:HD, 0, 0:60], w2c[:, 0, k, :], hT[:, k, :], start=k == 0, stop=k == 1)
                else:
                    for g in range(KVG):
                        for k in range(2):
                            mm = pe.matmul(aux[0:NC, 0, g * HD:(g + 1) * HD], hT[:, k, g * NC:(g + 1) * NC], w2c[:, 1, k, :],
                                           start=k == 0, stop=k == 1)
                mm.then_inc(cmp_out, 1)
            else:
                pe.wait_ge(roped, 2)
                pe.wait_ge(kT_ready, n)
                turn_keys(kv6[:, :, 512 * n:512 * n + 256], n)

        pe.wait_ge(xt_ready, BUILD["b_o"])
        for u in range(16):
            if u % 4 == 0:
                pe.wait_ge(acc_freed, g0 + 4 + u // 4 - 1)
            multiply(u0 + 16 + u, u % 4, 4, 2 * ((g0 + u // 4) % 2))
            if u in STEPS:
                step(*STEPS[u])
        pe.wait_ge(kT_ready, 3)
        with pe.Fori(0, KVG) as g:
            fill = filler("b_z", g)
            queries(4, g, fill)
            pe.wait_ge(values_ready, g + (KVG + 1))
            v_of = [lambda k, n=n: v_g[:, n, k] for n in range(2)]
            kinds = []
            for t in range(T):
                kinds.append((NC, t, cmpk_g, lambda k: cmpv_g))
                kinds += [((t + 1) * P, t, kT[:, bass.ds(g * L, (t + 1) * P)], v) for kT, v in zip((kTs, kTw), v_of)]
            rounds(ROUND_B, kinds, g, sm_b, fill)
        pe.wait_ge(gated, 2 * KVG)
        turn_rows("b_o", rows3)
        groups("b_out", 2, build="b_o")

    ctx.close()


def shape_constants():
    f = np.float32
    sel = np.zeros((4, P + 2), f)
    sel[0, 0:P] = sel[2, 0:P] = 1
    for c in range(2):
        sel[c, P + c] = sel[2 + c, P + c] = 1
    band = np.zeros((L, 4, L), f)
    for g, w in enumerate((2, 4, 8, 16)):
        for t in range(L):
            lo, hi = max(t - w // 2, 0), min(t + w - w // 2, L)
            band[lo:hi, g, t] = 1.0 / (hi - lo)
            band[t, g, t] -= 1
    band = band.reshape(T, P, 4, L).transpose(1, 0, 2, 3)
    half = HD // 2
    inv = (f(10000.0) ** (-np.arange(0, half, 2, dtype=f) / f(half))).astype(f)
    tok = np.arange(L)
    cos, sin = np.ones((6, P, HD), f), np.zeros((6, P, HD), f)
    for n, pos in enumerate((tok // 64, tok % 64)):
        ang = pos.astype(f)[:, None] * inv[None, :]
        c, s = np.cos(ang).reshape(T, P, 16), np.sin(ang).reshape(T, P, 16)
        for tiles in (slice(0, 2), slice(2, 4)):
            cos[tiles, :, n * 32:n * 32 + 16] = cos[tiles, :, n * 32 + 16:n * 32 + 32] = c
            sin[tiles, :, n * 32:n * 32 + 16], sin[tiles, :, n * 32 + 16:n * 32 + 32] = -s, s
    invf = (500000.0 ** (-np.arange(0, 16, 2) / 16.0)).astype(f)
    p = np.arange(P)
    masks = np.zeros((P, 672), f)
    k1, k2 = np.arange(P), np.arange(L)
    masks[:, 0:128] = np.where(k1[None] <= p[:, None], 0, NEG)
    q = P + p[:, None]
    masks[:, 128:384] = np.where(k2[None] <= q, 0, NEG)
    masks[:, 384:640] = np.where((k2[None] <= q) & (q - k2[None] < 128), 0, NEG)
    for t in range(T):
        valid = 16 * np.arange(NC)[None] + 31 <= (t * P + p)[:, None]
        masks[:, 640 + NC * t:640 + NC * t + NC] = np.where(valid, 0, NEG)
        masks[:, 670 + t] = valid.any(1)
    return {"c_ident": np.eye(P, dtype=f), "c_sel": sel, "c_band": np.ascontiguousarray(band),
            "c_cos": np.ascontiguousarray(cos.transpose(1, 0, 2)), "c_sin": np.ascontiguousarray(sin.transpose(1, 0, 2)),
            "c_invf": np.ascontiguousarray(np.broadcast_to(invf, (P, ROT))), "c_masks": masks}


NAMES = {
    "x": "x", "c": "c", "ctx": "ctx", "c_ctx": "c_ctx", "w_mod": "w_mod", "b_mod": "b_mod", "norm_attn_w": "norm_attn_w",
    "w_in": "w_in", "q_norm_w": "q_norm_w", "k_norm_w": "k_norm_w", "lam0": "lambda_q1", "lam1": "lambda_k1",
    "lam2": "lambda_q2", "lam3": "lambda_k2", "subln_w": "subln_w", "pool_w": "pool_w", "pool_scale": "pool_scale",
    "w_a_up": "w_a_up", "w_b_up": "w_b_up", "w_o": "w_o", "norm_mlp_w": "norm_mlp_w", "w_ff1": "w_ff1", "w_ff2": "w_ff2",
    "positions": "positions_2", "norm_w": "norm_w_2", "final_norm_w": "final_norm_w_2", "a_w_in": "a_w_in_2",
    "sinks": "a_sinks_2", "a_w_out": "a_w_out_2", "b_w_in": "b_w_in_2", "kpos": "b_cmp_k_pos_2", "kw1": "b_cmp_k_w1_2",
    "kw2": "b_cmp_k_w2_2", "vpos": "b_cmp_v_pos_2", "vw1": "b_cmp_v_w1_2", "vw2": "b_cmp_v_w2_2", "b_w_out": "b_w_out_2",
}


def kernel(**inputs):
    import concourse.bacc as bacc
    from concourse.bass_utils import run_bass_kernel_spmd

    nc = bacc.Bacc("TRN2", target_bir_lowering=False, num_devices=1)
    arrays = {}
    for name, given in NAMES.items():
        x = np.ascontiguousarray(inputs[given])
        if name not in ("norm_w", "c_ctx", "final_norm_w") and x.ndim > 1 and x.shape[0] == 1:
            x = x[0]
        arrays[name] = x
    arrays.update(shape_constants())
    aps = {n: nc.dram_tensor(f"in_{n}", x.shape, mybir.dt.from_np(x.dtype), kind="ExternalInput").ap()
           for n, x in arrays.items()}
    out = nc.dram_tensor("out_y", (L, D), F32, kind="ExternalOutput").ap()
    dit_kernel(nc, aps, out)
    r = run_bass_kernel_spmd(nc, [{f"in_{n}": x for n, x in arrays.items()}], core_ids=[0])
    return r.results[0]["out_y"].reshape(1, L, D)
```
